# Optimizing a Trainium2 kernel written in Bass

```python
import jax, jax.numpy as jnp
from jax import lax
import numpy as np
import math
import jax
import jax.numpy as jnp

D_MODEL = 1024
BATCH = 1
SEQ = 256
DEPTH = 2

HEAD_DIM = 64
ATTN_HEADS = 8
ATTN_WIDTH = ATTN_HEADS * HEAD_DIM
GLA_HEADS = 4
GLA_DK = 64
GLA_DV = 128
GLA_K_WIDTH = GLA_HEADS * GLA_DK
GLA_V_WIDTH = GLA_HEADS * GLA_DV
GLA_GATE_RANK = 16
GLA_TAU = 16.0
GLA_CHUNK = 64
MIX_WIDTH = ATTN_WIDTH + GLA_V_WIDTH
IN_WIDTH = 3 * ATTN_WIDTH + 2 * GLA_K_WIDTH + 2 * GLA_V_WIDTH + GLA_GATE_RANK
D_FF = -(-8 * D_MODEL // (3 * 256)) * 256
ROPE_THETA = 500000.0
ROPE_DIM = HEAD_DIM // 4
DILATED_PATTERNS = ((128, 1), (512, 4), (2048, 16))
N_PATTERNS = len(DILATED_PATTERNS)
N_KEYS = DILATED_PATTERNS[0][0] // DILATED_PATTERNS[0][1] + 1
Q_BLOCK = 128
RMS_EPS = 1e-6


F32 = jnp.float32

def rmsnorm(x, g):
    xf = x.astype(F32)
    y = xf * lax.rsqrt(jnp.mean(xf * xf, axis=-1, keepdims=True) + RMS_EPS)
    return (y * g.astype(F32)).astype(x.dtype)

def rope_partial(x, pos):
    half = ROPE_DIM // 2
    inv = ROPE_THETA ** (-(jnp.arange(half, dtype=F32) * 2.0) / ROPE_DIM)
    ang = pos.astype(F32)[:, None] * inv[None, :]
    cos = jnp.cos(ang)[None, :, None, :]
    sin = jnp.sin(ang)[None, :, None, :]
    xr = x[..., :ROPE_DIM].astype(F32)
    x1, x2 = xr[..., :half], xr[..., half:]
    rot = jnp.concatenate([x1 * cos - x2 * sin, x2 * cos + x1 * sin], axis=-1).astype(x.dtype)
    return jnp.concatenate([rot, x[..., ROPE_DIM:]], axis=-1)

def dilated_attention(q, k, v):
    B, S, H, hd = q.shape
    nblk = S // Q_BLOCK
    dists = jnp.concatenate([d * jnp.arange(w // d + 1) for (w, d) in DILATED_PATTERNS])
    q_blocks = q.reshape(B, nblk, Q_BLOCK, H, hd).transpose(1, 0, 2, 3, 4)
    starts = jnp.arange(nblk) * Q_BLOCK
    scale = hd ** -0.5

    def block(args):
        q_blk, start = args
        pos = start + jnp.arange(Q_BLOCK)
        idx = pos[:, None] - dists[None, :]
        valid = idx >= 0
        idx_c = jnp.maximum(idx, 0)
        kg = jnp.take(k, idx_c, axis=1).astype(F32)
        vg = jnp.take(v, idx_c, axis=1).astype(F32)
        s = jnp.einsum('bqhd,bqnhd->bhqn', q_blk.astype(F32), kg) * scale
        s = jnp.where(valid[None, None], s, -jnp.inf)
        s = s.reshape(B, H, Q_BLOCK, N_PATTERNS, N_KEYS)
        lse = jax.nn.logsumexp(s, axis=-1, keepdims=True)
        p = jnp.exp(s - lse)
        o_pat = jnp.einsum('bhqpn,bqpnhd->bhqpd', p,
                           vg.reshape(B, Q_BLOCK, N_PATTERNS, N_KEYS, H, hd))
        w = jax.nn.softmax(lse, axis=-2)
        o = jnp.sum(w * o_pat, axis=-2)
        return o.transpose(0, 2, 1, 3).astype(q.dtype)

    out = lax.map(block, (q_blocks, starts))
    return out.transpose(1, 0, 2, 3, 4).reshape(B, S, H, hd)

def gla_chunked(q, k, v, g):
    B, S, H, dk = q.shape
    dv = v.shape[-1]
    C = GLA_CHUNK
    nc = S // C

    def chunks(t):
        return t.astype(F32).reshape(B, nc, C, H, t.shape[-1]).transpose(1, 0, 3, 2, 4)

    causal = jnp.tril(jnp.ones((C, C), dtype=bool))

    def step(state, inp):
        qc, kc, vc, gc = inp
        b = jnp.cumsum(gc, axis=-2)
        o_inter = jnp.einsum('bhtk,bhkv->bhtv', qc * jnp.exp(b), state)
        diff = b[:, :, :, None, :] - b[:, :, None, :, :]
        decay = jnp.exp(jnp.where(causal[None, None, :, :, None], diff, -jnp.inf))
        attn = jnp.einsum('bhtk,bhsk,bhtsk->bhts', qc, kc, decay)
        o_intra = jnp.einsum('bhts,bhsv->bhtv', attn, vc)
        b_last = b[:, :, -1:, :]
        state = jnp.exp(b_last[:, :, 0, :])[..., None] * state + \
            jnp.einsum('bhsk,bhsv->bhkv', kc * jnp.exp(b_last - b), vc)
        return state, o_intra + o_inter

    s0 = jnp.zeros((B, H, dk, dv), F32)
    _, o = lax.scan(step, s0, (chunks(q) * (dk ** -0.5), chunks(k), chunks(v), chunks(g)))
    return o.transpose(1, 0, 3, 2, 4).reshape(B, S, H, dv).astype(v.dtype)

def hybrid_mixer(h, w_in, gla_w_gate_up, gla_b_gate, gla_out_norm, attn_out_norm, w_out):
    B, S, _ = h.shape
    proj = h @ w_in
    cuts = [ATTN_WIDTH, 2 * ATTN_WIDTH, 3 * ATTN_WIDTH,
            3 * ATTN_WIDTH + GLA_K_WIDTH, 3 * ATTN_WIDTH + 2 * GLA_K_WIDTH,
            3 * ATTN_WIDTH + 2 * GLA_K_WIDTH + GLA_V_WIDTH,
            3 * ATTN_WIDTH + 2 * GLA_K_WIDTH + 2 * GLA_V_WIDTH]
    aq, ak, av, gq, gk, gv, gr, g_low = jnp.split(proj, cuts, axis=-1)

    pos = jnp.arange(S)
    aq = rope_partial(aq.reshape(B, S, ATTN_HEADS, HEAD_DIM), pos)
    ak = rope_partial(ak.reshape(B, S, ATTN_HEADS, HEAD_DIM), pos)
    av = av.reshape(B, S, ATTN_HEADS, HEAD_DIM)
    a_out = dilated_attention(aq, ak, av).reshape(B, S, ATTN_WIDTH)
    a_out = rmsnorm(a_out, attn_out_norm)

    z = g_low @ gla_w_gate_up + gla_b_gate
    log_alpha = jax.nn.log_sigmoid(z.astype(F32)) / GLA_TAU
    o = gla_chunked(gq.reshape(B, S, GLA_HEADS, GLA_DK),
                    gk.reshape(B, S, GLA_HEADS, GLA_DK),
                    gv.reshape(B, S, GLA_HEADS, GLA_DV),
                    log_alpha.reshape(B, S, GLA_HEADS, GLA_DK))
    o = rmsnorm(o, gla_out_norm.reshape(GLA_HEADS, GLA_DV)).reshape(B, S, GLA_V_WIDTH)
    g_out = o * jax.nn.silu(gr)

    mixed = jnp.concatenate([a_out, g_out], axis=-1)
    return mixed @ w_out

def swiglu(h, w_gate, w_up, w_down):
    return (jax.nn.silu(h @ w_gate) * (h @ w_up)) @ w_down

def first_inputs(seed: int = 0) -> dict:
    key = jax.random.key(seed)
    ks = jax.random.split(key, 16)
    L, D = DEPTH, D_MODEL

    def nrm(k, shape, fan_in):
        return jax.random.normal(k, shape, F32) * (fan_in ** -0.5)

    def gain(k, shape):
        return 1.0 + 0.05 * jax.random.normal(k, shape, F32)

    return {
        "x": jax.random.normal(ks[0], (BATCH, SEQ, D), F32),
        "mix_pre_norm": gain(ks[1], (L, D)),
        "mix_post_norm": gain(ks[2], (L, D)),
        "ffn_pre_norm": gain(ks[3], (L, D)),
        "ffn_post_norm": gain(ks[4], (L, D)),
        "w_in": nrm(ks[5], (L, D, IN_WIDTH), D),
        "gla_w_gate_up": nrm(ks[6], (L, GLA_GATE_RANK, GLA_K_WIDTH), GLA_GATE_RANK),
        "gla_b_gate": 0.1 * jax.random.normal(ks[7], (L, GLA_K_WIDTH), F32),
        "gla_out_norm": gain(ks[8], (L, GLA_V_WIDTH)),
        "attn_out_norm": gain(ks[9], (L, ATTN_WIDTH)),
        "w_out": nrm(ks[10], (L, MIX_WIDTH, D), MIX_WIDTH),
        "w_gate": nrm(ks[11], (L, D, D_FF), D),
        "w_up": nrm(ks[12], (L, D, D_FF), D),
        "w_down": nrm(ks[13], (L, D_FF, D), D_FF),
    }

def first_block(x, mix_pre_norm, mix_post_norm, ffn_pre_norm, ffn_post_norm, w_in,
              gla_w_gate_up, gla_b_gate, gla_out_norm, attn_out_norm, w_out,
              w_gate, w_up, w_down):
    h = x
    for l in range(DEPTH):
        m = hybrid_mixer(rmsnorm(h, mix_pre_norm[l]), w_in[l], gla_w_gate_up[l], gla_b_gate[l],
                         gla_out_norm[l], attn_out_norm[l], w_out[l])
        h = h + rmsnorm(m, mix_post_norm[l])
        f = swiglu(rmsnorm(h, ffn_pre_norm[l]), w_gate[l], w_up[l], w_down[l])
        h = h + rmsnorm(f, ffn_post_norm[l])
    return h


DEPTH_2 = 1

N_HEADS_FOX = 8
N_HEADS_MOBA = 8
FOX_WIDTH = N_HEADS_FOX * HEAD_DIM
MOBA_WIDTH = N_HEADS_MOBA * HEAD_DIM
MIX_WIDTH_2 = FOX_WIDTH + MOBA_WIDTH
IN_WIDTH_2 = 3 * FOX_WIDTH + 3 * MOBA_WIDTH + N_HEADS_FOX
MOBA_BLOCK = 256
MOBA_TOPK = 3
MOBA_Q_CHUNK = 64
NUM_BUCKETS = 32
MAX_DISTANCE = 128
N_EXPERTS = 32
TOP_K = 4
D_EXPERT = D_MODEL
SWIGLU_LIMIT = 7.0
SWIGLU_ALPHA = 1.702
EXPERT_ROW_BLOCK = 128


def rms_norm(x, g):
    x32 = x.astype(jnp.float32)
    y = x32 * lax.rsqrt(jnp.mean(x32 * x32, axis=-1, keepdims=True) + RMS_EPS)
    return (y * g.astype(jnp.float32)).astype(x.dtype)

def t5_bucket(dist):
    dist = jnp.maximum(dist, 0)
    max_exact = NUM_BUCKETS // 2
    d = jnp.maximum(dist, 1).astype(jnp.float32)
    large = max_exact + (jnp.log(d / max_exact) / math.log(MAX_DISTANCE / max_exact)
                         * (NUM_BUCKETS - max_exact)).astype(jnp.int32)
    large = jnp.minimum(large, NUM_BUCKETS - 1)
    return jnp.where(dist < max_exact, dist, large)

def fox_attention(q, k, v, log_f):
    B, S, H, Dh = q.shape
    scale = Dh ** -0.5
    cum = jnp.cumsum(log_f, axis=1)
    cum_h = cum.transpose(0, 2, 1)
    kh = k.transpose(0, 2, 1, 3)
    vh = v.transpose(0, 2, 1, 3)
    nq = S // Q_BLOCK
    qb = q.reshape(B, nq, Q_BLOCK, H, Dh).transpose(1, 0, 3, 2, 4)
    cb = cum.reshape(B, nq, Q_BLOCK, H).transpose(1, 0, 3, 2)
    key_pos = jnp.arange(S)

    def block(args):
        i, qi, ci = args
        s = jnp.einsum('bhqd,bhkd->bhqk', qi, kh).astype(jnp.float32) * scale
        s = s + ci[..., None] - cum_h[:, :, None, :]
        qpos = i * Q_BLOCK + jnp.arange(Q_BLOCK)
        s = jnp.where(key_pos[None, :] <= qpos[:, None], s, -jnp.inf)
        p = jax.nn.softmax(s, axis=-1)
        return jnp.einsum('bhqk,bhkd->bhqd', p.astype(vh.dtype), vh)

    out = lax.map(block, (jnp.arange(nq), qb, cb))
    return out.transpose(1, 0, 3, 2, 4).reshape(B, S, H, Dh)

def moba_attention(q, k, v, rel_bias):
    B, S, H, Dh = q.shape
    scale = Dh ** -0.5
    s_pad = -(-S // MOBA_BLOCK) * MOBA_BLOCK
    pad = ((0, 0), (0, s_pad - S), (0, 0), (0, 0))
    q, k, v = jnp.pad(q, pad), jnp.pad(k, pad), jnp.pad(v, pad)
    nb = s_pad // MOBA_BLOCK
    k_sel_n = min(MOBA_TOPK, nb)
    kb = k.reshape(B, nb, MOBA_BLOCK, H, Dh).transpose(0, 3, 1, 2, 4)
    vb = v.reshape(B, nb, MOBA_BLOCK, H, Dh).transpose(0, 3, 1, 2, 4)
    kmean = jnp.mean(kb.astype(jnp.float32), axis=3)
    nq = s_pad // MOBA_Q_CHUNK
    qc = q.reshape(B, nq, MOBA_Q_CHUNK, H, Dh).transpose(1, 0, 2, 3, 4)
    bi = jnp.arange(B)[:, None, None, None]
    hi = jnp.arange(H)[None, None, :, None]
    hi5 = jnp.arange(H)[None, None, :, None, None]
    blk_pos = jnp.arange(MOBA_BLOCK)

    def chunk(args):
        i, qi = args
        qpos = i * MOBA_Q_CHUNK + jnp.arange(MOBA_Q_CHUNK)
        own = (i * MOBA_Q_CHUNK) // MOBA_BLOCK
        gate = jnp.einsum('bqhd,bhnd->bqhn', qi.astype(jnp.float32), kmean)
        gate = jnp.where(jnp.arange(nb) < own, gate, -jnp.inf)
        _, idx = lax.top_k(gate, k_sel_n)
        valid = jnp.arange(k_sel_n) < own
        ksel = kb[bi, hi, idx]
        vsel = vb[bi, hi, idx]
        s_sel = jnp.einsum('bqhd,bqhjpd->bqhjp', qi, ksel).astype(jnp.float32) * scale
        kpos_sel = idx[..., None] * MOBA_BLOCK + blk_pos
        dist_sel = qpos[None, :, None, None, None] - kpos_sel
        s_sel = s_sel + rel_bias[t5_bucket(dist_sel), hi5].astype(jnp.float32)
        s_sel = jnp.where(valid[None, None, None, :, None], s_sel, -jnp.inf)
        k_own = lax.dynamic_index_in_dim(kb, own, axis=2, keepdims=False)
        v_own = lax.dynamic_index_in_dim(vb, own, axis=2, keepdims=False)
        s_own = jnp.einsum('bqhd,bhpd->bqhp', qi, k_own).astype(jnp.float32) * scale
        dist_own = qpos[:, None] - (own * MOBA_BLOCK + blk_pos)[None, :]
        bias_own = rel_bias[t5_bucket(dist_own)].transpose(0, 2, 1)
        s_own = s_own + bias_own[None].astype(jnp.float32)
        s_own = jnp.where((dist_own >= 0)[None, :, None, :], s_own, -jnp.inf)
        logits = jnp.concatenate(
            [s_sel.reshape(B, MOBA_Q_CHUNK, H, k_sel_n * MOBA_BLOCK), s_own], axis=-1)
        p = jax.nn.softmax(logits, axis=-1).astype(vb.dtype)
        p_sel = p[..., :k_sel_n * MOBA_BLOCK].reshape(B, MOBA_Q_CHUNK, H, k_sel_n, MOBA_BLOCK)
        p_own = p[..., k_sel_n * MOBA_BLOCK:]
        return (jnp.einsum('bqhjp,bqhjpd->bqhd', p_sel, vsel)
                + jnp.einsum('bqhp,bhpd->bqhd', p_own, v_own))

    out = lax.map(chunk, (jnp.arange(nq), qc))
    return out.transpose(1, 0, 2, 3, 4).reshape(B, s_pad, H, Dh)[:, :S]

def clamped_swiglu(hdn):
    x_glu = jnp.minimum(hdn[..., :D_EXPERT], SWIGLU_LIMIT)
    x_lin = jnp.clip(hdn[..., D_EXPERT:], -SWIGLU_LIMIT, SWIGLU_LIMIT)
    return x_glu * jax.nn.sigmoid(SWIGLU_ALPHA * x_glu) * (x_lin + 1)

def moe_ffn(h, w_router, b_router, w_gate_up, b_gate_up, w_down, b_down):
    B, S, D = h.shape
    T = B * S
    xt = h.reshape(T, D)
    logits = (xt @ w_router).astype(jnp.float32) + b_router.astype(jnp.float32)
    top_v, top_i = lax.top_k(logits, TOP_K)
    gates = jax.nn.softmax(top_v, axis=-1)
    A = T * TOP_K
    e_flat = top_i.reshape(A)
    tok_flat = jnp.arange(A) // TOP_K
    g_flat = gates.reshape(A)
    order = jnp.argsort(e_flat)
    e_sorted, tok_sorted, g_sorted = e_flat[order], tok_flat[order], g_flat[order]
    counts = jnp.bincount(e_flat, length=N_EXPERTS)
    padded = ((counts + EXPERT_ROW_BLOCK - 1) // EXPERT_ROW_BLOCK) * EXPERT_ROW_BLOCK
    starts = jnp.cumsum(counts) - counts
    pends = jnp.cumsum(padded)
    pstarts = pends - padded
    dest = pstarts[e_sorted] + jnp.arange(A) - starts[e_sorted]
    n_rows = A + N_EXPERTS * EXPERT_ROW_BLOCK
    n_blk = n_rows // EXPERT_ROW_BLOCK
    rows = jnp.zeros((n_rows, D), xt.dtype).at[dest].set(xt[tok_sorted])
    block_e = jnp.minimum(
        jnp.searchsorted(pends, jnp.arange(n_blk) * EXPERT_ROW_BLOCK, side='right'), N_EXPERTS - 1)

    def expert_block(args):
        xb, e = args
        hdn = xb @ w_gate_up[e] + b_gate_up[e]
        return clamped_swiglu(hdn) @ w_down[e] + b_down[e]

    y = lax.map(expert_block, (rows.reshape(n_blk, EXPERT_ROW_BLOCK, D), block_e)).reshape(n_rows, D)
    out = jnp.zeros((T, D), y.dtype).at[tok_sorted].add(y[dest] * g_sorted[:, None].astype(y.dtype))
    return out.reshape(B, S, D)

def second_inputs(seed: int = 0) -> dict:
    key = jax.random.key(seed)
    ks = jax.random.split(key, 20)
    nrm = jax.random.normal
    f32 = jnp.float32
    return {
        "x": nrm(ks[0], (BATCH, SEQ, D_MODEL), f32),
        "c": nrm(ks[1], (BATCH, D_MODEL), f32),
        "w_ada": nrm(ks[2], (DEPTH_2, D_MODEL, 6 * D_MODEL), f32) * (0.5 * D_MODEL ** -0.5),
        "b_ada": nrm(ks[3], (DEPTH_2, 6 * D_MODEL), f32) * 0.01,
        "g_pre_mix": 1.0 + 0.05 * nrm(ks[4], (DEPTH_2, D_MODEL), f32),
        "g_post_mix": 1.0 + 0.05 * nrm(ks[5], (DEPTH_2, D_MODEL), f32),
        "w_in": nrm(ks[6], (DEPTH_2, D_MODEL, IN_WIDTH_2), f32) * D_MODEL ** -0.5,
        "b_forget": nrm(ks[7], (DEPTH_2, N_HEADS_FOX), f32) * 0.1,
        "rel_bias": nrm(ks[8], (NUM_BUCKETS, N_HEADS_MOBA), f32) * 0.5,
        "w_out": nrm(ks[9], (DEPTH_2, MIX_WIDTH_2, D_MODEL), f32) * MIX_WIDTH_2 ** -0.5,
        "g_pre_ffn": 1.0 + 0.05 * nrm(ks[10], (DEPTH_2, D_MODEL), f32),
        "g_post_ffn": 1.0 + 0.05 * nrm(ks[11], (DEPTH_2, D_MODEL), f32),
        "w_router": nrm(ks[12], (DEPTH_2, D_MODEL, N_EXPERTS), f32) * D_MODEL ** -0.5,
        "b_router": nrm(ks[13], (DEPTH_2, N_EXPERTS), f32) * 0.01,
        "w_gate_up": nrm(ks[14], (DEPTH_2, N_EXPERTS, D_MODEL, 2 * D_EXPERT), f32) * D_MODEL ** -0.5,
        "b_gate_up": nrm(ks[15], (DEPTH_2, N_EXPERTS, 2 * D_EXPERT), f32) * 0.01,
        "w_down": nrm(ks[16], (DEPTH_2, N_EXPERTS, D_EXPERT, D_MODEL), f32) * D_EXPERT ** -0.5,
        "b_down": nrm(ks[17], (DEPTH_2, N_EXPERTS, D_MODEL), f32) * 0.01,
    }

def second_block(x, c, w_ada, b_ada, g_pre_mix, g_post_mix, w_in, b_forget, rel_bias, w_out,
              g_pre_ffn, g_post_ffn, w_router, b_router, w_gate_up, b_gate_up, w_down, b_down):
    B, S, D = x.shape
    cond = jax.nn.silu(c)
    for l in range(DEPTH_2):
        mod = cond @ w_ada[l] + b_ada[l]
        sh_m, sc_m, gt_m, sh_f, sc_f, gt_f = jnp.split(mod, 6, axis=-1)
        h = rms_norm(x, g_pre_mix[l]) * (1 + sc_m[:, None, :]) + sh_m[:, None, :]
        proj = h @ w_in[l]
        o = np.cumsum([FOX_WIDTH] * 3 + [MOBA_WIDTH] * 3)
        q_a, k_a, v_a = proj[..., :o[0]], proj[..., o[0]:o[1]], proj[..., o[1]:o[2]]
        q_b, k_b, v_b = proj[..., o[2]:o[3]], proj[..., o[3]:o[4]], proj[..., o[4]:o[5]]
        f_logit = proj[..., o[5]:]
        log_f = jax.nn.log_sigmoid(f_logit.astype(jnp.float32) + b_forget[l].astype(jnp.float32))
        hs_a = (B, S, N_HEADS_FOX, HEAD_DIM)
        hs_b = (B, S, N_HEADS_MOBA, HEAD_DIM)
        y_a = fox_attention(q_a.reshape(hs_a), k_a.reshape(hs_a), v_a.reshape(hs_a), log_f)
        y_b = moba_attention(q_b.reshape(hs_b), k_b.reshape(hs_b), v_b.reshape(hs_b), rel_bias)
        mix = jnp.concatenate([y_a.reshape(B, S, FOX_WIDTH), y_b.reshape(B, S, MOBA_WIDTH)], axis=-1)
        x = x + gt_m[:, None, :] * rms_norm(mix @ w_out[l], g_post_mix[l])
        h = rms_norm(x, g_pre_ffn[l]) * (1 + sc_f[:, None, :]) + sh_f[:, None, :]
        y = moe_ffn(h, w_router[l], b_router[l], w_gate_up[l], b_gate_up[l], w_down[l], b_down[l])
        x = x + gt_f[:, None, :] * rms_norm(y, g_post_ffn[l])
    return x


def setup_inputs(seed=0):
    out = dict(first_inputs(seed))
    for name, value in second_inputs(seed + 1).items():
        if name != "x":
            out[name + "_2"] = value
    return out


def reference(
    x, mix_pre_norm, mix_post_norm, ffn_pre_norm, ffn_post_norm, w_in, gla_w_gate_up,
    gla_b_gate, gla_out_norm, attn_out_norm, w_out, w_gate, w_up, w_down, c_2, w_ada_2, b_ada_2,
    g_pre_mix_2, g_post_mix_2, w_in_2, b_forget_2, rel_bias_2, w_out_2, g_pre_ffn_2,
    g_post_ffn_2, w_router_2, b_router_2, w_gate_up_2, b_gate_up_2, w_down_2, b_down_2,
):
    x = first_block(
        x, mix_pre_norm, mix_post_norm, ffn_pre_norm, ffn_post_norm, w_in, gla_w_gate_up,
        gla_b_gate, gla_out_norm, attn_out_norm, w_out, w_gate, w_up, w_down,
    )
    return second_block(
        x, c_2, w_ada_2, b_ada_2, g_pre_mix_2, g_post_mix_2, w_in_2, b_forget_2, rel_bias_2,
        w_out_2, g_pre_ffn_2, g_post_ffn_2, w_router_2, b_router_2, w_gate_up_2, b_gate_up_2,
        w_down_2, b_down_2,
    )


_drawn_inputs = setup_inputs


def setup_inputs(seed=0):
    import zlib

    import numpy as np

    out = dict(_drawn_inputs(seed))
    spreads = {}
    factors = {'b_ada_2': 4.525,
     'g_pre_mix_2': 6.004,
     'g_post_mix_2': 5.861,
     'b_forget_2': 8.0,
     'rel_bias_2': 3.91,
     'g_pre_ffn_2': 2.726,
     'g_post_ffn_2': 8.0,
     'b_router_2': 6.478,
     'b_gate_up_2': 8.0,
     'b_down_2': 52.876}
    for name, (base, spread) in spreads.items():
        noise = np.random.default_rng([zlib.crc32(name.encode()), seed]).standard_normal(out[name].shape)
        drawn = base * np.exp(spread * noise) if base else spread * noise
        out[name] = jnp.asarray(drawn.astype(out[name].dtype))
    for name, factor in factors.items():
        out[name] = (out[name] * factor).astype(out[name].dtype)
    return out
```

```python
from contextlib import ExitStack

import concourse.bass as bass
import numpy as np
from concourse import mybir

P = 128
S = 256
T = S // P
D = 1024
KD = D // P
L = 2
HD = 64
AH = 8
AW = AH * HD
GH, GDV = 4, 128
GK = GH * HD
GR = 16
TAU = 16.0
F = 2816
FB = F // P
NE, TOPK = 32, 4
SLOTS = 64
PARTS = S // SLOTS
ITEMS = NE + S * TOPK // SLOTS
PAIRS = ITEMS // 2
LISTED = ITEMS + 2
LIMIT, ALPHA = 7.0, 1.702
EPS = 1e-6
SCALE = HD ** -0.5
OFF = 1e30
ROPE = 16
THETA = 500000.0
BUCKETS, MAXDIST = 32, 128

BANK = 512
SLOT = 4096
DENSE_SLOTS = 5
RING = 6
IN_CHUNKS, OUT_CHUNKS = 6, 2
GU_CHUNKS = FB // 2
DN_CHUNKS = -(-FB // 4)
CHUNKS = IN_CHUNKS + OUT_CHUNKS + GU_CHUNKS + DN_CHUNKS
USES = CHUNKS // DENSE_SLOTS
assert USES * DENSE_SLOTS == CHUNKS
ADA_W = 1536
ADA_STEPS = 3 * D // ADA_W * KD
LEVELS = 8

F32 = mybir.dt.float32
U32 = mybir.dt.uint32
I32 = mybir.dt.int32
ALU = mybir.AluOpType
ACT = mybir.ActivationFunctionType
X_AXIS = mybir.AxisListType.X

CONST = {}
_at = 0
for _name, _n in (("ident", P), ("rotate", P), ("upto", P), ("before", P), ("flip", P),
                  ("cos_q", S), ("sin_q", S), ("cos_k", S), ("sin_k", S),
                  ("dilated", 3 * P), ("causal", 3 * P), ("level", LEVELS * P),
                  ("bucket", 2 * S), ("iota", SLOTS + 1), ("full", 1), ("expert", 1), ("pairs", PAIRS)):
    CONST[_name] = (_at, _at + _n)
    _at += _n
NCONST = _at


def constants():
    c = {k: np.zeros((P, b - a), np.float32) for k, (a, b) in CONST.items()}
    i = np.arange(P)
    c["ident"][i, i] = 1
    half = ROPE // 2
    for h in range(0, P, HD):
        for d in range(half):
            c["rotate"][h + d + half, h + d] = -1
            c["rotate"][h + d, h + d + half] = 1
    c["upto"][:] = i[:, None] <= i[None, :]
    c["before"][:] = i[:, None] < i[None, :]
    c["flip"][i, P - 1 - i] = 1
    inv = np.float32(THETA) ** (-(np.arange(half, dtype=np.float32) * np.float32(2)) / np.float32(ROPE))
    angle = np.arange(S, dtype=np.float32)[None, :] * inv.astype(np.float32)[:, None]
    cos, sin = np.ones((HD, S)), np.zeros((HD, S))
    cos[:ROPE] = np.tile(np.cos(angle.astype(np.float64)), (2, 1))
    sin[:ROPE] = np.tile(np.sin(angle.astype(np.float64)), (2, 1))
    for name, sign in (("q", -SCALE), ("k", 1.0)):
        c["cos_" + name][:] = np.tile(cos, (2, 1)) * sign
        c["sin_" + name][:] = np.tile(sin, (2, 1)) * sign
    for t in range(T):
        to = slice(0, P) if t == 0 else slice(P, 3 * P)
        d = (t * P + i)[:, None] - np.arange((t + 1) * P)[None, :]
        seen = sum(((d >= 0) & (d <= w) & (d % r == 0)).astype(int) for w, r in ((128, 1), (512, 4), (2048, 16)))
        c["dilated"][:, to] = np.where(seen > 0, -np.log(np.maximum(seen, 1)), OFF)
        c["causal"][:, to] = np.where(d >= 0, 0, OFF)
    for n in range(LEVELS):
        b = 2 << n
        if b <= P:
            m = (i[:, None] // b == i[None, :] // b) & (i[:, None] % b < b // 2) & (i[None, :] % b >= b // 2)
        else:
            m = i[:, None] == i[None, :]
        c["level"][:, n * P:(n + 1) * P] = m
    d = S - 1 - np.arange(2 * S)
    exact = BUCKETS // 2
    far = exact + (np.log(np.maximum(d, 1).astype(np.float32) / np.float32(exact))
                   / np.float32(np.log(MAXDIST / exact)) * np.float32(BUCKETS - exact)).astype(np.int32)
    bucket = np.where(d < exact, np.maximum(d, 0), np.minimum(far, BUCKETS - 1))
    c["bucket"][np.where(d >= 0, bucket, BUCKETS), np.arange(2 * S)] = np.where(d >= 0, -1, OFF)
    c["iota"][:] = np.arange(SLOTS + 1)
    c["full"][:, 0] = np.where(i < NE, -1, i // NE * SLOTS)
    c["expert"][:, 0] = i % NE
    c["pairs"][:] = np.arange(PAIRS) * 2
    return np.concatenate([c[k] for k in CONST], axis=1).astype(np.float32)


PER = dict(
    x_ready=4, sumsq_act=5, sumsq_gla=1, rstd_ready=6, xn_ready=3, transposed_a=3, transposed_b=3,
    ht_act=3, ht_dve=3, gains_ready=1, post_gains=32, gate_weights=48,
    q_proj=1, q_raw=1, q_rot=1, q_ready=1, k_proj=1, k_raw=1, k_rot=1, k_ready=1,
    v_proj=1, v_ready=1, gqk_proj=1, gqk_ready=1, low_proj=1, low_ready=1, z_proj=1, z_abs=1, z_exp=1,
    z_log=1, decay_sum=1, gv_proj=1, gv_ready=1, gr_proj=1, gr_ready=1,
    scores=AH, logits=AH, probs=AH, probs_t=AH, probs_ready=AH, attended=AH, attn_out=1,
    gla_diff=LEVELS, gla_abs=LEVELS, gla_decay=LEVELS, gla_qe=LEVELS, gla_ke=LEVELS,
    gla_scores=LEVELS + 1, gla_merged=LEVELS + 1, gla_done=1, gla_square=1, zeros_set=1,
    mix_done=OUT_CHUNKS, dn_done=DN_CHUNKS, gu_done=GU_CHUNKS, silu_done=GU_CHUNKS, act_done=GU_CHUNKS,
    ada_used=ADA_STEPS, ada_sum=1, ada_mod=1, ada_rows=1, ada_cols=1,
    dve_step=12, pool_step=6,
)
PERG = dict(
    sel_ready=1, selected=1, gathered=2, xt_act=1, xt_dve=1, wt_t=1, wt_ready=1, gu_chunk=8, gu_drained=2, clipped=2,
    sig_ready=2, gated=2, actv_ready=2, act_t=2, att_ready=2, dn_chunk=2, yp_act=1, yp_dve=1, combined=1,
)
GU_CREDIT, DN_CREDIT = PERG["gu_chunk"], PERG["dn_chunk"]
PRE_MIX, ATTN, GLA, POST_MIX, PRE_FFN, POST_FFN = range(6)
USED_2 = [("q_proj", L, 1), ("k_proj", L, 1), ("v_proj", L, 1)]
USED = ([(n, 1) for n in ("q_proj", "k_proj", "v_proj", "gqk_proj", "gv_proj", "gr_proj")]
        + [("mix_done", n + 1) for n in range(OUT_CHUNKS)] + [("gu_done", n + 1) for n in range(GU_CHUNKS)]
        + [("dn_done", DN_CHUNKS + n + 1) for n in range(DN_CHUNKS)])

GAINS = (("mix_pre_norm", 0, KD), ("attn_out_norm", KD, 4), ("gla_out_norm", KD + 4, 4), ("ffn_pre_norm", 2 * KD, KD))


def times(ap, axis, n):
    return ap.unsqueeze(axis).broadcast_to(tuple(ap.shape[:axis]) + (n,) + tuple(ap.shape[axis:]))


def program(nc, A, const, out):
    ctx = ExitStack()
    with ctx:
        def sb(name, shape, dt=F32):
            return ctx.enter_context(nc.sbuf_tensor(name, shape, dt))

        def pb(name):
            return ctx.enter_context(nc.psum_tensor(name, [P, 2, BANK], F32))

        X = sb("X", [P, T, D])
        XN = sb("XN", [P, T, D])
        HT = sb("HT", [P, KD, S])
        ring = sb("ring", [P, RING, SLOT])
        K = sb("K", [P, NCONST])
        arena = sb("arena", [P, FB * S])
        gla = sb("gla", [P, 7 * 1024])
        prob = sb("prob", [P, 4, 3 * P])
        POSTG = sb("POSTG", [P, 2, D])
        gain_all = sb("gain_all", [P, L * 3 * KD])
        GC = sb("GC", [P, 3 * KD])
        WLOW = sb("WLOW", [P, KD, GR])
        WGU = sb("WGU", [GR, GK])
        BGATE = sb("BGATE", [P, 2])
        LOW = sb("LOW", [GR, S])
        ones = sb("ones", [P, P])
        stat = sb("stat", [P, 3, 8 * 6])
        eps, half = sb("eps", [P, 8]), sb("half", [P, 8])
        wait_col = sb("wait_col", [P, 3])
        soft = sb("soft", [P, 3, 2 * 2 * AH])
        cc = sb("cc", [P, 2, KD])
        modc = sb("modc", [P, L, 2 * KD])
        PA, PB, PC, PD = (pb(n) for n in ("PA", "PB", "PC", "PD"))

        def k_(name, rows=P):
            a, b = CONST[name]
            return K[0:rows, a:b]

        ident = k_("ident")
        ar = lambda a, n: arena[:, a:a + n]
        QRAW, KRAW = (ar(1024 * n, 1024).rearrange("p (b s) -> p b s", s=S) for n in (0, 1))
        QT = ar(2048, 1024).rearrange("p (b s) -> p b s", s=S)
        KT = ar(3072, 2048).rearrange("p (h s) -> p h s", s=S)
        ACTT = arena[:, :].rearrange("p (f s) -> p f s", s=S)
        gl = lambda a, n: gla[:, a:a + n]
        V = [ar(5120, AW), gl(6656, AW)]
        GKT = gl(0, 1024).rearrange("p (h s) -> p h s", s=S)
        GQ, GB, DIFF, EDEC = (gl(1024 + 512 * n, 512).rearrange("p (a s) -> p a s", a=2) for n in range(4))
        LA = EDEC
        QE = gl(3072, 1024).rearrange("p (u a s) -> p u a s", u=2, a=2)
        KE = ring[:, 5, 1024:3072].rearrange("p (u h s) -> p u h s", u=2, s=S)
        GV, GRS = (gl(4096 + 1024 * n, 1024).rearrange("p (t n) -> p t n", t=T) for n in (0, 1))
        MERGED = ring[:, 5, 0:T * GH * P].rearrange("p (t h n) -> p t h n", t=T, h=GH)
        ACROSS = gl(6144, 512).rearrange("p (h n) -> p h n", h=GH)
        SG = gl(1536, 1024).rearrange("p (u n) -> p u n", u=2)
        ADAB = gl(4096, 2 * ADA_W).rearrange("p (u n) -> p u n", u=2)
        ASUM = ring[:, 5, 0:3 * D]
        MINMAX, SUM, RSUM = (soft[:, n, :] for n in range(3))

        QF, KF, VF = (ar(0, 1024).rearrange("p (b s) -> p b s", s=S), ar(1024, 2048).rearrange("p (h s) -> p h s", s=S),
                      [ar(3072 + AW * t, AW) for t in range(T)])
        r5 = lambda a, n: ring[:, 5, a:a + n]
        GATES = [r5(3 * D, D), r5(2 * D, D)]
        QB, KB, VB = (r5(0, 1024).rearrange("p (b s) -> p b s", s=S), r5(1024, 2048).rearrange("p (h s) -> p h s", s=S),
                      [r5(3072 + AW * t, AW) for t in range(T)])
        BIAS_B = gl(0, AH * 3 * P).rearrange("p (h n) -> p h n", h=AH)
        BIAS_F = gl(AH * 3 * P, AH * 3 * P).rearrange("p (h n) -> p h n", h=AH)
        FLIPPED = BIAS_F
        ADAROWS = HT[:, :, :].rearrange("p c s -> p (c s)")
        WF = sb("WF", [P, KD, AH])
        WR = sb("WR", [P, KD, NE])
        REL = sb("REL", [BUCKETS + 1, AH])
        DIST = arena[0:AH, 0:2 * S]
        badac = sb("badac", [P, 6 * KD])
        gpre = sb("gpre", [P, 2, KD])
        cols = sb("cols", [P, 4, KD])
        brow = sb("brow", [P, NE + AH])
        LF = sb("LF", [P, 3, T, AH])
        XT = ar(0, 1024).rearrange("p (c n) -> p c n", c=KD)
        YP = ar(1024, D)
        WT = ar(2048, S)
        SELG = ar(2304, S).rearrange("p (t e n) -> p t e n", t=T, e=2)
        WG = ar(2560, S).rearrange("p (t e n) -> p t e n", t=T, e=2)
        ATT = [ar(2816 + 512 * n, 512).rearrange("p (h j n) -> p j h n", h=2, n=SLOTS) for n in (0, 1)]
        BZ = [gl(2 * D * n, 2 * D) for n in (0, 1)]
        XG, XL, SIG, ACTV = (gl(4 * D + BANK * n, BANK) for n in range(4))
        BD = prob[0:NE, 0:3, :].rearrange("p a n -> p (a n)")[:, 0:D]
        PARTED = ar(3840, 2 * S).rearrange("p (u s) -> p u s", u=2)
        SLOT_OF, GATE_OF = (gl(6144 + T * LISTED * n, T * LISTED).rearrange("p (t n) -> p t n", t=T) for n in (0, 1))
        RK = gl(6400, T * P).rearrange("p (t n) -> p t n", t=T)
        GATE = gl(6656, T * P).rearrange("p (t n) -> p t n", t=T)
        PERM = gl(6912, LISTED)
        FLAG, PLACE, PAIRF, NPAIRS = gl(6976, 1), gl(6977, 2), gl(6979, PAIRS), gl(6979 + PAIRS, 1)
        rt = gl(4 * D, T * (5 * NE + 32 + P)).rearrange("p (t n) -> p t n", t=T)
        LOG = lambda t: rt[:, t, 0:NE]
        HOT = lambda t: rt[:, t, NE:5 * NE].rearrange("p (j e) -> p j e", j=TOPK)
        TOP = lambda t: rt[:, t, 5 * NE:5 * NE + 8]
        TOPF = lambda t: rt[:, t, 5 * NE + 8:5 * NE + 8 + TOPK]
        PROBS = lambda t: rt[:, t, 5 * NE + 16:5 * NE + 16 + TOPK]
        TSUM = lambda t, n: rt[:, t, 5 * NE + 24 + n:5 * NE + 25 + n]
        MASK = lambda t: rt[:, t, 5 * NE + 32:5 * NE + 32 + P]
        topi = sb("topi", [P, T, 8], U32)
        items = sb("items", [P, LISTED + 1], I32)
        dist_dram = nc.dram_tensor("dist", (AH, 2 * S), F32, kind="Internal").ap()

        S_ = {}

        def sem(name):
            S_[name] = ctx.enter_context(nc.semaphore(name))
            return S_[name]

        for name in (*PER, *PERG):
            sem(name)
        efull = [sem(f"expert_loaded_{s}") for s in range(RING)]
        bfull = [sem(f"expert_bias_loaded_{s}") for s in range(2)]
        (rel_loaded, rel_one, small_loaded, dist_done, dist_copied, dist_stored, flipped_loaded, flipped_done, bias_b_act,
         bias_b_dve, ada_rows_loaded, gates_loaded, gates_biased, gates_ready, cols_ready, kf_zeros, kb_zeros, forget_logits,
         forget_in, forget_abs, forget_exp, forget_log, log_forget, forget_sums, forget_cum, forget_rows, bias_f,
         router_done, top_ready, top_exp, mask_ready, ranks_done, flags_ready, routed, places_done, parted_t, parted, perm_ready, items_done,
         items_ready, bz_zeroed, bd_loaded) = (sem(n) for n in (
             "rel_loaded rel_one small_loaded dist_done dist_copied dist_stored flipped_loaded flipped_done bias_b_act "
             "bias_b_dve ada_rows_loaded gates_loaded gates_biased gates_ready cols_ready kf_zeros kb_zeros "
             "forget_logits forget_in forget_abs forget_exp forget_log log_forget forget_sums forget_cum forget_rows "
             "bias_f router_done top_ready top_exp mask_ready ranks_done flags_ready routed places_done "
             "parted_t parted perm_ready items_done items_ready bz_zeroed bd_loaded").split())
        wfull = [sem(f"weights_loaded_{s}") for s in range(DENSE_SLOTS)]
        afull = [sem(f"ada_loaded_{s}") for s in range(2)]
        const_loaded, x_loaded, gains_loaded, c_loaded = (
            sem(n) for n in ("const_loaded", "x_loaded", "gains_loaded", "c_loaded"))
        ones_set, half_set, c_silu = (sem(n) for n in ("ones_set", "half_set", "c_silu"))
        stored = sem("stored")

        def upto(name, l, k):
            return S_[name], l * PER[name] + k

        def pair_(name, G, k):
            return S_[name], G * PERG[name] + k

        def banks(pair):
            return pair[:, :, :].rearrange("p a n -> p (a n)")

        def st(row, ev, a, b):
            return stat[:, row, 8 * ev + a:8 * ev + b]

        def of_head(blocks, r):
            return blocks[r * HD:(r + 1) * HD].rearrange("p (a r) s -> p a r s", r=2)[:, :, r, :]

        def attention(h):
            n = h % AH
            q, k, val, bias, pair = (QF, KF, VF, BIAS_F, PC) if h < AH else (QB, KB, VB, BIAS_B, PB)
            return q[:, n // 2, :], k[:, n, :], [x[:, n * HD:(n + 1) * HD] for x in val], bias[:, n, :], pair

        block = ctx.enter_context(nc.Block())

        def layer_chunk(l, i):
            w = lambda name: A[name][bass.ds(l, 1), :, :].rearrange("l (c p) n -> p (l c) n", p=P)
            if i < IN_CHUNKS + OUT_CHUNKS:
                name, n = ("w_in", i) if i < IN_CHUNKS else ("w_out", i - IN_CHUNKS)
                src, rows, width = w(name)[:, :, n * BANK:(n + 1) * BANK], KD, BANK
            elif i < IN_CHUNKS + OUT_CHUNKS + GU_CHUNKS:
                n = i - IN_CHUNKS - OUT_CHUNKS
                return [(w(name)[:, :, n * S:(n + 1) * S], h * KD * S, KD, S)
                        for h, name in enumerate(("w_gate", "w_up"))]
            else:
                n = 4 * (i - IN_CHUNKS - OUT_CHUNKS - GU_CHUNKS)
                rows, width = min(4, FB - n), D
                src = w("w_down")[:, n:n + rows, :]
            h = rows // 2
            return [(src[:, 0:h, :], 0, h, width), (src[:, h:rows, :], h * width, rows - h, width)]

        @block.sync
        def _(sp):
            sp.dma_start(X[:, :, :], A["x"][0].rearrange("(t p) d -> p t d", p=P)).then_inc(x_loaded, 16)
            with sp.Fori(0, L) as l:
                for i in range(CHUNKS):
                    s = i % DENSE_SLOTS
                    if i >= DENSE_SLOTS:
                        sp.wait_ge(*upto(USED[i - DENSE_SLOTS][0], l, USED[i - DENSE_SLOTS][1]))
                    else:
                        sp.wait_ge(*upto("dn_done", l, DN_CHUNKS - DENSE_SLOTS + i + 1))
                    for src, at, rows, width in layer_chunk(l, i):
                        sp.dma_start(ring[:, s, at:at + rows * width].rearrange("p (c n) -> p c n", n=width),
                                     src).then_inc(wfull[s], 16)
            for i in range(IN_CHUNKS + OUT_CHUNKS):
                s = i % DENSE_SLOTS
                if i >= DENSE_SLOTS:
                    sp.wait_ge(*upto(*USED_2[i - DENSE_SLOTS]))
                else:
                    sp.wait_ge(*upto("dn_done", L, DN_CHUNKS - DENSE_SLOTS + i + 1))
                name, n = ("w_in_2", i) if i < IN_CHUNKS else ("w_out_2", i - IN_CHUNKS)
                src = A[name][0].rearrange("(c p) n -> p c n", p=P)[:, :, n * BANK:(n + 1) * BANK]
                for h in range(2):
                    rows = slice(h * KD // 2, (h + 1) * KD // 2)
                    sp.dma_start(ring[:, s, :].rearrange("p (c n) -> p c n", n=BANK)[:, rows, :], src[:, rows, :]) \
                        .then_inc(wfull[s], 16)

            def load_pair(G, experts):
                n = 0
                for x, e in enumerate(experts):
                    w = A["w_gate_up_2"][0, bass.ds(e, 1), :, :].rearrange("e (c p) n -> p (e c) n", p=P)
                    sp.wait_ge(*pair_("gu_chunk", G, 4 * x + 1))
                    sp.dma_start(BZ[x][0:1, :], A["b_gate_up_2"][0, bass.ds(e, 1), :]).then_inc(bfull[x], 16)
                    for c in range(4):
                        load_slot(G, n, w[:, 2 * c:2 * c + 2, :])
                        n += 1
                for q in range(2):
                    for e in experts:
                        w = A["w_down_2"][0, bass.ds(e, 1), :, :].rearrange("e (c p) n -> p (e c) n", p=P)
                        load_slot(G, n, w[:, 4 * q:4 * q + 4, :])
                        n += 1

            def load_slot(G, n, src):
                if n < 2:
                    sp.wait_ge(*pair_("gu_chunk", G, 7 + n))
                elif n < RING:
                    sp.wait_ge(*pair_("dn_chunk", G, n // 4 + 1))
                else:
                    sp.wait_ge(*pair_("gu_chunk", G, GU_CREDIT + n - RING + 1))
                s, rows = n % RING, src.shape[1]
                dst = ring[:, s, :].rearrange("p (c n) -> p c n", c=rows)
                for h in range(2):
                    part = slice(h * rows // 2, (h + 1) * rows // 2)
                    sp.dma_start(dst[:, part, :], src[:, part, :]).then_inc(efull[s], 16)

            sp.wait_ge(*upto("mix_done", L, OUT_CHUNKS))
            sp.wait_ge(bz_zeroed, 1)
            load_pair(0, (0, 1))
            sp.wait_ge(items_ready, 1)
            pairs = sp.value_load(items[0:1, LISTED:LISTED + 1], min_val=1, max_val=PAIRS)
            with sp.Fori(1, pairs) as G:
                load_pair(G, [sp.value_load(items[0:1, bass.ds(2 * G + x, 1)], min_val=0, max_val=NE - 1) for x in range(2)])
            for t in range(T):
                sp.wait_ge(*upto("x_ready", L, 4 + t))
                sp.dma_start(out[0, t * P:(t + 1) * P, :], X[:, t, :]).then_inc(stored, 16)
            sp.wait_ge(stored, 16 * T)

        @block.gpsimd
        def _(pool):
            steps = [0]

            def inverse_rms(l, ev, n, ready):
                pool.wait_ge(*ready)
                nc.gpsimd.tensor_tensor(st(1, ev, 0, n), st(0, ev, 0, n), eps[:, 0:n], ALU.add) \
                    .then_inc(S_["pool_step"], 1)
                steps[0] += 1
                pool.wait_ge(*upto("pool_step", l, steps[0]))
                nc.gpsimd.tensor_tensor(st(2, ev, 0, n), st(1, ev, 0, n), half[:, 0:n], ALU.pow) \
                    .then_inc(S_["rstd_ready"], 1)

            nc.gpsimd.memset(eps[:, :], EPS)
            nc.gpsimd.memset(half[:, :], -0.5).then_inc(half_set, 1)
            nc.gpsimd.memset(ones[:, :], 1.0).then_inc(ones_set, 1)
            nc.gpsimd.memset(gl(0, 1024), 0.0)
            pool.dma_start(REL[0:BUCKETS, :], A["rel_bias_2"]).then_inc(rel_loaded, 16)
            pool.dma_start(WF[:, :, :], A["w_in_2"][0, :, IN_CHUNKS * BANK:].rearrange("(c p) n -> p c n", p=P)) \
                .then_inc(small_loaded, 16)
            pool.dma_start(WR[:, :, :], A["w_router_2"][0].rearrange("(c p) n -> p c n", p=P)).then_inc(small_loaded, 16)
            pool.dma_start(badac[:, :], A["b_ada_2"][0].rearrange("(c p) -> p c", p=P), allow_slow_non_contiguous=True) \
                .then_inc(small_loaded, 16)
            for n, name in enumerate(("g_pre_mix_2", "g_pre_ffn_2")):
                pool.dma_start(gpre[:, n, :], A[name][0].rearrange("(c p) -> p c", p=P), allow_slow_non_contiguous=True) \
                    .then_inc(small_loaded, 16)
            pool.dma_start(brow[:, 0:NE], A["b_router_2"].broadcast_to((P, NE))).then_inc(small_loaded, 16)
            pool.dma_start(brow[:, NE:NE + AH], A["b_forget_2"].broadcast_to((P, AH))).then_inc(small_loaded, 16)
            pool.wait_ge(half_set, 1)
            pool.wait_ge(gains_loaded, 64)
            with pool.Fori(0, L) as l:
                steps[0] = 0
                pool.wait_ge(*upto("x_ready", l, 1))
                for _, at, n in GAINS:
                    last = nc.gpsimd.tensor_copy(GC[:, at:at + n], gain_all[:, bass.ds(l * n + L * at, n)])
                last.then_inc(S_["gains_ready"], 1)
                nc.gpsimd.memset(ar(3072, 2048), 0.0)
                nc.gpsimd.memset(ring[:, 5, 0:3072], 0.0).then_inc(S_["zeros_set"], 1)
                row = lambda name: A[name][bass.ds(l, 1), :]
                pool.dma_start(WLOW[:, :, :], A["w_in"][bass.ds(l, 1), :, IN_CHUNKS * BANK:]
                               .rearrange("l (c p) n -> p (l c) n", p=P)).then_inc(S_["gate_weights"], 16)
                pool.dma_start(WGU[:, :], A["gla_w_gate_up"][bass.ds(l, 1), :, :].rearrange("l r n -> (l r) n")) \
                    .then_inc(S_["gate_weights"], 16)
                pool.dma_start(BGATE[:, :], row("gla_b_gate").rearrange("l (a p) -> p (l a)", p=P),
                               allow_slow_non_contiguous=True) \
                    .then_inc(S_["gate_weights"], 16)
                pool.dma_start(POSTG[:, 0, :], row("mix_post_norm").broadcast_to((P, D))).then_inc(S_["post_gains"], 16)
                pool.dma_start(POSTG[:, 1, :], row("ffn_post_norm").broadcast_to((P, D))).then_inc(S_["post_gains"], 16)
                inverse_rms(l, PRE_MIX, T, upto("sumsq_act", l, 1))
                for n in range(LEVELS):
                    pool.wait_ge(*upto("gla_decay", l, n + 1))
                    if n >= 2:
                        pool.wait_ge(*upto("gla_scores", l, n))
                    for r in range(2):
                        last = nc.gpsimd.tensor_tensor(of_head(KE[:, n % 2], r), of_head(GKT, r),
                                                       EDEC[r * HD:(r + 1) * HD], ALU.mult)
                    last.then_inc(S_["gla_ke"], 1)
                inverse_rms(l, ATTN, T, upto("sumsq_act", l, 2))
                inverse_rms(l, GLA, T * GH, upto("sumsq_gla", l, 1))
                inverse_rms(l, POST_MIX, T, upto("sumsq_act", l, 3))
                inverse_rms(l, PRE_FFN, T, upto("sumsq_act", l, 4))
                for s in range(ADA_STEPS):
                    j, kc = divmod(s, KD)
                    if s >= 2:
                        pool.wait_ge(*upto("ada_used", l, s - 1))
                    pool.dma_start(ADAB[:, s % 2, :], A["w_ada_2"][0, kc * P:(kc + 1) * P,
                                                                   bass.ds(l * (3 * D) + j * ADA_W, ADA_W)]) \
                        .then_inc(afull[s % 2], 16)
                inverse_rms(l, POST_FFN, T, upto("sumsq_act", l, 5))
                assert steps[0] == PER["pool_step"]
            steps[0] = 0
            pool.wait_ge(*upto("dn_done", L, 2 * DN_CHUNKS - DN_CHUNKS))
            nc.gpsimd.memset(ar(1024, 2048), 0.0).then_inc(kf_zeros, 1)
            pool.wait_ge(*upto("x_ready", L, 1))
            pool.dma_start(POSTG[:, 0, :], A["g_post_mix_2"].broadcast_to((P, D))).then_inc(gates_loaded, 16)
            pool.dma_start(POSTG[:, 1, :], A["g_post_ffn_2"].broadcast_to((P, D))).then_inc(gates_loaded, 16)
            inverse_rms(L, PRE_MIX, T, upto("sumsq_act", L, 1))
            pool.wait_ge(gates_ready, 1)
            nc.gpsimd.memset(r5(1024, 2048), 0.0).then_inc(kb_zeros, 1)
            pool.wait_ge(*upto("logits", L, 2 * AH))
            for n in range(2):
                last = nc.gpsimd.memset(BZ[n], 0.0)
            last.then_inc(bz_zeroed, 1)
            inverse_rms(L, POST_MIX, T, upto("sumsq_act", L, 2))
            inverse_rms(L, PRE_FFN, T, upto("sumsq_act", L, 3))
            pool.wait_ge(*upto("attended", L, 2 * AH))
            pool.dma_start(BD, A["b_down_2"][0]).then_inc(bd_loaded, 16)
            inverse_rms(L, POST_FFN, T, upto("sumsq_act", L, 4))

        @block.scalar
        def _(act):
            A_ = nc.scalar.activation
            act.dma_start(K[:, :], const).then_inc(const_loaded, 16)
            for name, at, n in GAINS:
                act.dma_start(gain_all[:, L * at:L * (at + n)], A[name].rearrange("l (c p) -> p (l c)", p=P),
                              allow_slow_non_contiguous=True).then_inc(gains_loaded, 16)
            act.dma_start(cc[:, 0, :], A["c_2"][0].rearrange("(c p) -> p c", p=P), allow_slow_non_contiguous=True).then_inc(c_loaded, 16)
            act.wait_ge(dist_done, 1)
            A_(DIST, PA[0:AH, 0, :], ACT.Copy).then_inc(dist_copied, 1)
            act.wait_ge(dist_copied, 1)
            act.dma_start(dist_dram, DIST).then_inc(dist_stored, 16)
            act.wait_ge(dist_stored, 16)
            act.wait_ge(c_loaded, 16)
            A_(cc[:, 1, :], cc[:, 0, :], ACT.Silu).then_inc(c_silu, 1)

            def sum_squares(ev, src, junk, n):
                for t in range(T):
                    last = A_(junk(t), src(t), ACT.Square, scale=n ** -0.5, accum_out=st(0, ev, t, t + 1))
                last.then_inc(S_["sumsq_act"], 1)

            def fill_ht(l, n):
                act.wait_ge(*upto("transposed_a", l, n + 1))
                act.wait_ge(*upto("gains_ready", l, 1))
                for c in range(KD // 2):
                    last = A_(HT[:, c, :], PA[:, c // 2, (c % 2) * S:(c % 2 + 1) * S], ACT.Copy,
                              scale=GC[:, n * KD + c:n * KD + c + 1])
                last.then_inc(S_["ht_act"], 1)

            def fill_ht_2(n, at):
                act.wait_ge(*upto("transposed_a", L, n + 1))
                act.wait_ge(cols_ready, 1)
                for c in range(KD // 2):
                    last = A_(HT[:, c, :], PA[:, c // 2, (c % 2) * S:(c % 2 + 1) * S], ACT.Identity,
                              scale=cols[:, at, c:c + 1], bias=cols[:, at + 1, c:c + 1])
                last.then_inc(S_["ht_act"], 1)

            def softmax_exp(h, e, at):
                for t in range(T):
                    part = e[:, 0:P] if t == 0 else e[:, P:3 * P]
                    last = A_(part, part, ACT.Exp, scale=-1.0, bias=MINMAX[:, at + t * AH:at + t * AH + 1],
                              accum_out=SUM[:, at + t * AH:at + t * AH + 1])
                last.then_inc(S_["probs"], 1)

            def decay(l, n):
                act.wait_ge(*upto("gla_diff", l, n + 1))
                A_(DIFF[:, :, :], DIFF[:, :, :], ACT.Abs).then_inc(S_["gla_abs"], 1)
                act.wait_ge(*upto("gla_abs", l, n + 1))
                if n:
                    act.wait_ge(*upto("gla_qe", l, n))
                    act.wait_ge(*upto("gla_ke", l, n))
                A_(EDEC[:, :, :], DIFF[:, :, :], ACT.Exp, scale=-1.0 / TAU).then_inc(S_["gla_decay"], 1)

            with act.Fori(0, L) as l:
                act.wait_ge(*upto("x_ready", l, 1))
                sum_squares(PRE_MIX, lambda t: X[:, t, :], lambda t: XN[:, t, :], D)
                fill_ht(l, 0)
                act.wait_ge(*upto("q_proj", l, 1))
                A_(QRAW.rearrange("p b s -> p (b s)"), banks(PC), ACT.Copy).then_inc(S_["q_raw"], 1)
                act.wait_ge(*upto("k_proj", l, 1))
                A_(KRAW.rearrange("p b s -> p (b s)"), banks(PA), ACT.Copy).then_inc(S_["k_raw"], 1)
                act.wait_ge(*upto("v_proj", l, 1))
                for t in range(T):
                    last = A_(V[t], PC[:, t, :], ACT.Copy)
                last.then_inc(S_["v_ready"], 1)
                act.wait_ge(*upto("gqk_proj", l, 1))
                A_(GQ.rearrange("p a s -> p (a s)"), PD[:, 0, :], ACT.Copy, scale=SCALE)
                act.wait_ge(*upto("zeros_set", l, 1))
                for r in range(2):
                    last = A_(of_head(GKT, r), PD[r * HD:(r + 1) * HD, 1, :].rearrange("p (a s) -> p a s", s=S), ACT.Copy)
                last.then_inc(S_["gqk_ready"], 1)
                act.wait_ge(*upto("z_proj", l, 1))
                act.wait_ge(*upto("gate_weights", l, 48))
                for a in range(2):
                    last = A_(DIFF[:, a, :], PA[:, 1, a * S:(a + 1) * S], ACT.Abs, bias=BGATE[:, a:a + 1])
                last.then_inc(S_["z_abs"], 1)
                act.wait_ge(*upto("z_abs", l, 1))
                A_(DIFF[:, :, :], DIFF[:, :, :], ACT.Exp, scale=-1.0).then_inc(S_["z_exp"], 1)
                act.wait_ge(*upto("z_exp", l, 1))
                A_(DIFF[:, :, :], DIFF[:, :, :], ACT.Ln, bias=1.0).then_inc(S_["z_log"], 1)
                act.wait_ge(*upto("gv_proj", l, 1))
                A_(GV, PB[:, :, :], ACT.Copy).then_inc(S_["gv_ready"], 1)
                act.wait_ge(*upto("gr_proj", l, 1))
                A_(GRS, PC[:, :, :], ACT.Silu).then_inc(S_["gr_ready"], 1)
                decay(l, 0)
                for h in range(AH):
                    act.wait_ge(*upto("logits", l, h + 1))
                    softmax_exp(h, prob[:, h % 2, :], h)
                    if h + 1 < LEVELS:
                        decay(l, h + 1)
                    act.wait_ge(*upto("probs_t", l, h + 1))
                    if h >= 2:
                        act.wait_ge(*upto("attended", l, h - 1))
                    A_(prob[:, 2 + h % 2, :], PA[:, h % 2, 0:3 * P], ACT.Copy).then_inc(S_["probs_ready"], 1)
                act.wait_ge(*upto("attn_out", l, 1))
                sum_squares(ATTN, lambda t: XN[:, t, 0:AW], lambda t: ar(AW * t, AW), AW)
                act.wait_ge(*upto("gla_done", l, 1))
                A_(ar(1024, 1024), banks(PD), ACT.Square, scale=GDV ** -0.5).then_inc(S_["gla_square"], 1)
                fill_ht(l, 1)
                act.wait_ge(*upto("mix_done", l, OUT_CHUNKS))
                sum_squares(POST_MIX, lambda t: banks(PC if t == 0 else PD), lambda t: XN[:, t, :], D)
                act.wait_ge(*upto("x_ready", l, 3))
                sum_squares(PRE_FFN, lambda t: X[:, t, :], lambda t: XN[:, t, :], D)
                fill_ht(l, 2)
                for i in range(GU_CHUNKS):
                    act.wait_ge(*upto("gu_done", l, i + 1))
                    if i >= 2:
                        act.wait_ge(*upto("act_done", l, i - 1))
                    A_(SG[:, i % 2, :], PA[:, i % 2, :], ACT.Silu).then_inc(S_["silu_done"], 1)
                act.wait_ge(*upto("ada_mod", l, 1))
                A_(modc[:, bass.ds(l, 1), :], PA[:, 0:1, 0:2 * KD], ACT.Copy).then_inc(S_["ada_cols"], 1)
                act.wait_ge(*upto("dn_done", l, 2 * DN_CHUNKS))
                sum_squares(POST_FFN, lambda t: banks(PC if t == 0 else PD), lambda t: XN[:, t, :], D)

            for n in range(2):
                if n == 0:
                    act.wait_ge(*upto("act_done", L, 0))
                    act.wait_ge(*upto("ada_used", L, 0))
                act.dma_start(ADAROWS[:, n * D:(n + 1) * D], A["b_ada_2"][0:1, (3 * n + 2) * D:(3 * n + 3) * D]
                              .broadcast_to((P, D))).then_inc(ada_rows_loaded, 16)
            for t in range(T):
                act.dma_start(FLIPPED[:, :, t * P:P + 2 * t * P],
                              bass.AP(tensor=dist_dram.tensor, offset=P - P * t, ap=[[1, P], [2 * S, AH], [1, (t + 1) * P]])) \
                    .then_inc(flipped_loaded, 16)
            act.wait_ge(*upto("x_ready", L, 1))
            sum_squares(PRE_MIX, lambda t: X[:, t, :], lambda t: XN[:, t, :], D)
            act.wait_ge(flipped_done, 3)
            A_(BIAS_B.rearrange("p h n -> p (h n)")[:, 0:D], banks(PC), ACT.Copy).then_inc(bias_b_act, 1)
            fill_ht_2(0, 0)
            act.wait_ge(forget_in, 1)
            A_(LF[:, 1], LF[:, 0], ACT.Abs).then_inc(forget_abs, 1)
            act.wait_ge(forget_abs, 1)
            A_(LF[:, 1], LF[:, 1], ACT.Exp, scale=-1.0).then_inc(forget_exp, 1)
            act.wait_ge(forget_exp, 1)
            A_(LF[:, 1], LF[:, 1], ACT.Ln, bias=1.0).then_inc(forget_log, 1)

            def take(pair, done, n, q, k, val, zeros):
                if q is not None:
                    act.wait_ge(*upto("q_proj", L, n))
                    A_(q.rearrange("p b s -> p (b s)"), banks(pair), ACT.Copy, scale=-SCALE).then_inc(S_["q_ready"], 1)
                elif k is not None:
                    act.wait_ge(*upto("k_proj", L, n))
                    act.wait_ge(zeros, 1)
                    for r in range(2):
                        last = A_(of_head(k, r), banks(pair)[r * HD:(r + 1) * HD].rearrange("p (b s) -> p b s", s=S), ACT.Copy)
                    last.then_inc(S_["k_ready"], 1)
                else:
                    act.wait_ge(*upto("v_proj", L, n))
                    for t in range(T):
                        last = A_(val[t], pair[:, t, :], ACT.Copy)
                    last.then_inc(S_["v_ready"], 1)

            take(PC, "q_proj", 1, QF, None, None, None)
            take(PA, "k_proj", 1, None, KF, None, kf_zeros)
            take(PC, "v_proj", 1, None, None, VF, None)
            act.wait_ge(gates_ready, 1)
            take(PD, "q_proj", 2, QB, None, None, None)
            take(PB, "k_proj", 2, None, KB, None, kb_zeros)
            take(PA, "v_proj", 2, None, None, VB, None)
            for h in range(2 * AH):
                act.wait_ge(*upto("logits", L, h + 1))
                softmax_exp(h, prob[:, h % 2, :], (h // AH) * T * AH + h % AH)
                act.wait_ge(*upto("probs_t", L, h + 1))
                if h >= 2:
                    act.wait_ge(*upto("attended", L, h - 1))
                A_(prob[:, 2 + h % 2, :], PA[:, h % 2, 0:3 * P], ACT.Copy).then_inc(S_["probs_ready"], 1)
            act.wait_ge(*upto("transposed_a", L, 2))
            for c in range(KD // 2):
                last = A_(HT[:, c, :], PA[:, c // 2, (c % 2) * S:(c % 2 + 1) * S], ACT.Copy)
            last.then_inc(S_["ht_act"], 1)
            act.wait_ge(*upto("mix_done", L, OUT_CHUNKS))
            sum_squares(POST_MIX, lambda t: banks(PC if t == 0 else PD), lambda t: XN[:, t, :], D)
            act.wait_ge(*upto("x_ready", L, 3))
            sum_squares(PRE_FFN, lambda t: X[:, t, :], lambda t: XN[:, t, :], D)
            fill_ht_2(2, 2)
            act.wait_ge(top_ready, 1)
            for t in range(T):
                last = A_(PROBS(t), TOP(t)[:, 0:TOPK], ACT.Exp, bias=TSUM(t, 0), accum_out=TSUM(t, 1))
            last.then_inc(top_exp, 1)
            act.wait_ge(parted_t, 1)
            A_(PARTED.rearrange("p u s -> p (u s)"), PA[:, 1, :], ACT.Copy).then_inc(parted, 1)

            def take_rows(G):
                act.wait_ge(*pair_("gathered", G, 1))
                for c in range(KD // 2):
                    last = A_(XT[:, c, :], PA[:, 0, c * P:(c + 1) * P], ACT.Identity, scale=cols[:, 2, c:c + 1],
                              bias=cols[:, 3, c:c + 1])
                last.then_inc(S_["xt_act"], 1)

            act.wait_ge(items_ready, 1)
            pairs = act.value_load(items[0:1, LISTED:LISTED + 1], min_val=1, max_val=PAIRS)
            take_rows(0)
            with act.Fori(0, pairs) as G:
                act.wait_ge(*pair_("wt_t", G, 1))
                A_(WT, PA[:, 0, 0:S], ACT.Copy).then_inc(S_["wt_ready"], 1)
                for x in range(2):
                    act.wait_ge(*pair_("clipped", G, x + 1))
                    A_(SIG, XG, ACT.Sigmoid, scale=ALPHA).then_inc(S_["sig_ready"], 1)
                for x in range(2):
                    act.wait_ge(*pair_("act_t", G, x + 1))
                    A_(ATT[x], PB[:, x, :].rearrange("p (j h n) -> p j h n", j=4, n=SLOTS), ACT.Copy) \
                        .then_inc(S_["att_ready"], 1)
                take_rows(G + 1)
                act.wait_ge(*pair_("dn_chunk", G, 2 + DN_CREDIT))
                A_(YP[:, 0:BANK], PB[:, 0, :], ACT.Copy).then_inc(S_["yp_act"], 1)
            act.wait_ge(S_["combined"], pairs * PERG["combined"])
            sum_squares(POST_FFN, lambda t: banks(PC if t == 0 else PD), lambda t: XN[:, t, :], D)

        @block.vector
        def _(dve):
            v = nc.vector
            steps = [0]

            def then(l, ins):
                ins.then_inc(S_["dve_step"], 1)
                steps[0] += 1
                dve.wait_ge(*upto("dve_step", l, steps[0]))

            def norm(l, ev, order):
                dve.wait_ge(*upto("rstd_ready", l, order))
                for t in range(T):
                    last = v.tensor_scalar(XN[:, t, :], X[:, t, :], st(2, ev, t, t + 1), None, ALU.mult)
                last.then_inc(S_["xn_ready"], 1)

            def fill_ht(l, n):
                dve.wait_ge(*upto("transposed_b", l, n + 1))
                dve.wait_ge(*upto("gains_ready", l, 1))
                for c in range(KD // 2, KD):
                    b = c - KD // 2
                    last = v.tensor_scalar(HT[:, c, :], PB[:, b // 2, (b % 2) * S:(b % 2 + 1) * S],
                                           GC[:, n * KD + c:n * KD + c + 1], None, ALU.mult)
                last.then_inc(S_["ht_dve"], 1)

            def fill_ht_2(n, at):
                dve.wait_ge(*upto("transposed_b", L, n + 1))
                dve.wait_ge(cols_ready, 1)
                for c in range(KD // 2, KD):
                    b = c - KD // 2
                    last = v.tensor_scalar(HT[:, c, :], PB[:, b // 2, (b % 2) * S:(b % 2 + 1) * S],
                                           cols[:, at, c:c + 1], cols[:, at + 1, c:c + 1], ALU.mult, ALU.add)
                last.then_inc(S_["ht_dve"], 1)

            def residual(l, ev, order, g):
                dve.wait_ge(*upto("rstd_ready", l, order))
                if l is not L:
                    dve.wait_ge(*upto("post_gains", l, 32))
                for t in range(T):
                    then(l, v.scalar_tensor_tensor(XN[:, t, :], banks(PC if t == 0 else PD), st(2, ev, t, t + 1),
                                                   POSTG[:, g, :], ALU.mult, ALU.mult))
                    v.tensor_tensor(X[:, t, :], X[:, t, :], XN[:, t, :], ALU.add).then_inc(S_["x_ready"], 1)

            def rope(l, raw, rot, cos, sin, tmp, add, ready):
                dve.wait_ge(*upto(ready[0] + "_raw", l, 1))
                v.tensor_tensor(tmp, raw, times(k_(cos), 1, 4), ALU.mult).then_inc(S_["dve_step"], 1)
                steps[0] += 1
                dve.wait_ge(*upto(ready[0] + "_rot", l, 1))
                dve.wait_ge(*upto("dve_step", l, steps[0]))
                then(l, v.tensor_tensor(raw, banks(rot).rearrange("p (b s) -> p b s", s=S), times(k_(sin), 1, 4),
                                        ALU.mult))
                add().then_inc(S_[ready], 1)

            def add_q():
                return v.tensor_tensor(QT, QT, QRAW, ALU.add)

            def add_k():
                for r in range(2):
                    rows = slice(r * HD, (r + 1) * HD)
                    last = v.tensor_tensor(of_head(KT, r), QRAW[rows], KRAW[rows], ALU.add)
                return last

            def logits(l, h, bias, at):
                dve.wait_ge(*upto("scores", l, h + 1))
                if h >= 2:
                    dve.wait_ge(*upto("probs_t", l, h - 1))
                v.memset(wait_col[:, h % 2:h % 2 + 1], 0.0)
                e = prob[:, h % 2, :]
                for t in range(T):
                    part = slice(0, P) if t == 0 else slice(P, 3 * P)
                    last = v.tensor_tensor_reduce(out=e[:, part], in0=PD[:, h % 2, part], in1=bias[:, part], scale=1.0,
                                                  scalar=3.0e38, op0=ALU.add, op1=ALU.min,
                                                  accum_out=MINMAX[:, at + t * AH:at + t * AH + 1])
                last.then_inc(S_["logits"], 1)

            def attended(l, at, pair, to):
                then(l, v.reciprocal(RSUM[:, at:at + T * AH], SUM[:, at:at + T * AH]))
                for t in range(T):
                    last = v.tensor_tensor(XN[:, t, to:to + AW].rearrange("p (h d) -> p h d", d=HD),
                                           pair[:, t, :].rearrange("p (h d) -> p h d", d=HD),
                                           times(RSUM[:, at + t * AH:at + (t + 1) * AH], 2, HD), ALU.mult)
                return last

            def difference(l, n):
                b = 2 << n
                view = GB.rearrange("p a s -> p (a s)").rearrange("p (m b) -> p m b", b=b)
                if n:
                    dve.wait_ge(*upto("gla_decay", l, n))
                v.tensor_tensor(DIFF.rearrange("p a s -> p (a s)").rearrange("p (m b) -> p m b", b=b), view,
                                view[:, :, b // 2 - 1:b // 2].broadcast_to(tuple(view.shape)), ALU.subtract) \
                    .then_inc(S_["gla_diff"], 1)

            def merge(l, n):
                dve.wait_ge(*upto("gla_scores", l, n + 2))
                v.memset(wait_col[:, 2:3], 0.0)
                if n == LEVELS - 1:
                    last = v.tensor_copy(ACROSS, PB[:, 0, :].rearrange("p (h n) -> p h n", h=GH))
                else:
                    m = k_("level")[:, (n % LEVELS) * P:(n % LEVELS + 1) * P].bitcast(U32)
                    for t in range(T):
                        last = v.copy_predicated(MERGED[:, t], times(m, 1, GH),
                                                 PB[:, t, :].rearrange("p (h n) -> p h n", h=GH))
                last.then_inc(S_["gla_merged"], 1)

            v.memset(REL[BUCKETS:BUCKETS + 1, :], 1.0).then_inc(rel_one, 1)
            dve.wait_ge(x_loaded, 16)
            v.memset(soft[:, :, :], 0.0).then_inc(S_["x_ready"], 1)
            dve.wait_ge(const_loaded, 16)
            dve.wait_ge(c_silu, 1)
            dve.wait_ge(ones_set, 1)
            with dve.Fori(0, L) as l:
                steps[0] = 0
                norm(l, PRE_MIX, 1)
                fill_ht(l, 0)
                rope(l, QRAW, PD, "cos_q", "sin_q", QT, add_q, "q_ready")
                dve.wait_ge(*upto("q_ready", l, 1))
                dve.wait_ge(*upto("zeros_set", l, 1))
                rope(l, KRAW, PB, "cos_k", "sin_k", QRAW, add_k, "k_ready")
                dve.wait_ge(*upto("low_proj", l, 1))
                v.tensor_copy(LOW[:, :], PA[0:GR, 0, 0:S]).then_inc(S_["low_ready"], 1)
                dve.wait_ge(*upto("z_abs", l, 1))
                dve.wait_ge(*upto("gate_weights", l, 48))
                for a in range(2):
                    last = v.tensor_scalar(LA[:, a, :], PA[:, 1, a * S:(a + 1) * S], BGATE[:, a:a + 1], 0.0,
                                           ALU.add, ALU.min)
                then(l, last)
                dve.wait_ge(*upto("z_log", l, 1))
                then(l, v.tensor_tensor(LA, LA, DIFF, ALU.subtract))
                for a in range(2):
                    last = v.tensor_tensor_scan(GB[:, a, :], ones[:, 0:1].broadcast_to((P, S)),
                                                LA[:, a, :], 0.0, ALU.mult, ALU.add)
                last.then_inc(S_["decay_sum"], 1)
                dve.wait_ge(*upto("decay_sum", l, 1))
                difference(l, 0)
                merge(l, -1)
                for h in range(AH):
                    logits(l, h, k_("dilated"), h)
                    n = h
                    dve.wait_ge(*upto("gla_decay", l, n + 1))
                    if n >= 2:
                        dve.wait_ge(*upto("gla_scores", l, n))
                    v.tensor_tensor(QE[:, n % 2], GQ, EDEC, ALU.mult).then_inc(S_["gla_qe"], 1)
                    if n + 1 < LEVELS:
                        difference(l, n + 1)
                    if n:
                        merge(l, n - 1)
                merge(l, LEVELS - 1)
                dve.wait_ge(*upto("attended", l, AH))
                attended(l, 0, PC, 0).then_inc(S_["attn_out"], 1)
                dve.wait_ge(*upto("gla_square", l, 1))
                v.tensor_reduce(st(0, GLA, 0, T * GH), ar(1024, 1024).rearrange("p (g n) -> p g n", n=GDV), X_AXIS,
                                ALU.add).then_inc(S_["sumsq_gla"], 1)
                dve.wait_ge(*upto("gr_ready", l, 1))
                for t in range(T):
                    last = v.tensor_tensor(XN[:, t, AW:D], PD[:, t, :], GRS[:, t, :], ALU.mult)
                dve.wait_ge(*upto("rstd_ready", l, 2))
                dve.wait_ge(*upto("attn_out", l, 1))
                for t in range(T):
                    last = v.tensor_scalar(XN[:, t, 0:AW], XN[:, t, 0:AW], st(2, ATTN, t, t + 1), None, ALU.mult)
                then(l, last)
                dve.wait_ge(*upto("rstd_ready", l, 3))
                for t in range(T):
                    w = XN[:, t, AW:D].rearrange("p (h n) -> p h n", n=GDV)
                    last = v.tensor_tensor(w, w, times(st(2, GLA, t * GH, (t + 1) * GH), 2, GDV), ALU.mult)
                last.then_inc(S_["xn_ready"], 1)
                fill_ht(l, 1)
                residual(l, POST_MIX, 4, 0)
                norm(l, PRE_FFN, 5)
                fill_ht(l, 2)
                for i in range(GU_CHUNKS):
                    dve.wait_ge(*upto("silu_done", l, i + 1))
                    v.tensor_tensor(ACTT[:, 2 * i:2 * i + 2, :].rearrange("p f s -> p (f s)"), SG[:, i % 2, :],
                                    PB[:, i % 2, :], ALU.mult).then_inc(S_["act_done"], 1)
                    for s in range(2 * i, min(2 * i + 2, ADA_STEPS)):
                        j, kc = divmod(s, KD)
                        acc = ASUM[:, j * ADA_W:(j + 1) * ADA_W]
                        dve.wait_ge(afull[s % 2], l * (8 * ADA_STEPS) + 16 * (s // 2 + 1))
                        if kc == 0:
                            ins = v.tensor_scalar(acc, ADAB[:, s % 2, :], cc[:, 1, kc:kc + 1], None, ALU.mult)
                        else:
                            dve.wait_ge(*upto("ada_used", l, s))
                            ins = v.scalar_tensor_tensor(acc, ADAB[:, s % 2, :], cc[:, 1, kc:kc + 1], acc, ALU.mult,
                                                         ALU.add)
                        ins.then_inc(S_["ada_used"], 1)
                dve.wait_ge(*upto("ada_mod", l, 1))
                v.tensor_copy(ring[:, 5, bass.ds(3 * D - l * D, D)], banks(PB)).then_inc(S_["ada_rows"], 1)
                residual(l, POST_FFN, 6, 1)
                assert steps[0] == PER["dve_step"], steps
            steps[0] = 0
            dve.wait_ge(small_loaded, 16 * 7)
            dve.wait_ge(*upto("ada_cols", L, 0))
            dve.wait_ge(*upto("ada_rows", L, 0))
            for n in range(2):
                for m in range(2):
                    last = v.tensor_tensor(modc[:, n, m * KD:(m + 1) * KD], modc[:, n, m * KD:(m + 1) * KD],
                                           badac[:, (3 * n + m) * KD:(3 * n + m + 1) * KD], ALU.add)
            then(L, last)
            for n in range(2):
                v.scalar_tensor_tensor(cols[:, 2 * n, :], modc[:, n, KD:2 * KD], 1.0, gpre[:, n, :], ALU.add, ALU.mult)
                last = v.tensor_copy(cols[:, 2 * n + 1, :], modc[:, n, 0:KD])
            last.then_inc(cols_ready, 1)
            dve.wait_ge(cols_ready, 1)
            dve.wait_ge(ada_rows_loaded, 32)
            for n in range(2):
                last = v.tensor_tensor(GATES[n], GATES[n], ADAROWS[:, n * D:(n + 1) * D], ALU.add)
            last.then_inc(gates_biased, 1)
            dve.wait_ge(flipped_done, 3)
            bias_b = BIAS_B.rearrange("p h n -> p (h n)")
            v.tensor_copy(bias_b[:, D:2 * D], banks(PD))
            v.tensor_copy(bias_b[:, 2 * D:3 * D], banks(PA)).then_inc(bias_b_dve, 1)
            norm(L, PRE_MIX, 1)
            fill_ht_2(0, 0)
            dve.wait_ge(gates_biased, 1)
            dve.wait_ge(gates_loaded, 32)
            for n in range(2):
                last = v.tensor_tensor(POSTG[:, n, :], POSTG[:, n, :], GATES[n], ALU.mult)
            last.then_inc(gates_ready, 1)
            dve.wait_ge(forget_logits, 1)
            v.tensor_tensor(LF[:, 0], PB[:, 0, 0:T * AH].rearrange("p (t h) -> p t h", t=T),
                            times(brow[:, NE:NE + AH], 1, T), ALU.add).then_inc(forget_in, 1)
            dve.wait_ge(forget_log, 1)
            then(L, v.tensor_scalar(LF[:, 0], LF[:, 0], 0.0, None, ALU.min))
            v.tensor_tensor(LF[:, 0], LF[:, 0], LF[:, 1], ALU.subtract).then_inc(log_forget, 1)
            dve.wait_ge(forget_sums, 1)
            v.tensor_copy(LF[:, 2], PB[:, 0, 0:T * AH].rearrange("p (t h) -> p t h", t=T)).then_inc(forget_cum, 1)
            dve.wait_ge(forget_cum, 1)
            for h in range(AH):
                dve.wait_ge(forget_rows, h // 4 + 1)
                row = (PD, PB)[h // 4][:, h % 4 // 2, (h % 2) * S:(h % 2 + 1) * S]
                for t in range(T):
                    part = slice(0, P) if t == 0 else slice(P, 3 * P)
                    last = v.scalar_tensor_tensor(BIAS_F[:, h, part], row[:, 0:(t + 1) * P], LF[:, 2, t, h:h + 1],
                                                  k_("causal")[:, part], ALU.subtract, ALU.add)
                if h % 4 == 3:
                    last.then_inc(bias_f, 1)
            dve.wait_ge(bias_f, 2)
            for h in range(2 * AH):
                logits(L, h, attention(h)[3], (h // AH) * T * AH + h % AH)
                if h == AH + 1:
                    dve.wait_ge(*upto("attended", L, AH))
                    attended(L, 0, PC, 0)
            dve.wait_ge(*upto("attended", L, 2 * AH))
            attended(L, T * AH, PB, AW).then_inc(S_["xn_ready"], 1)
            dve.wait_ge(*upto("transposed_b", L, 2))
            for c in range(KD // 2, KD):
                b = c - KD // 2
                last = v.tensor_copy(HT[:, c, :], PB[:, b // 2, (b % 2) * S:(b % 2 + 1) * S])
            last.then_inc(S_["ht_dve"], 1)
            residual(L, POST_MIX, 2, 0)
            norm(L, PRE_FFN, 3)
            fill_ht_2(2, 2)
            dve.wait_ge(router_done, 1)
            for t in range(T):
                last = v.tensor_tensor(LOG(t), PA[:, 0, t * NE:(t + 1) * NE], brow[:, 0:NE], ALU.add)
            then(L, last)
            for t in range(T):
                last = v.max(TOP(t), LOG(t))
            then(L, last)
            for t in range(T):
                v.tensor_scalar(TSUM(t, 0), TOP(t)[:, 0:1], -1.0, None, ALU.mult)
                last = v.max_index(topi[:, t, :], TOP(t), LOG(t))
            last.then_inc(top_ready, 1)
            dve.wait_ge(top_ready, 1)
            for t in range(T):
                last = v.tensor_copy(TOPF(t), topi[:, t, 0:TOPK])
            then(L, last)
            for t in range(T):
                last = v.tensor_tensor(HOT(t), times(k_("iota")[:, 0:NE], 1, TOPK), times(TOPF(t), 2, NE), ALU.is_equal)
            then(L, last)
            for t in range(T):
                last = v.tensor_reduce(MASK(t).rearrange("p (r e) -> p r e", e=NE),
                                       times(HOT(t).rearrange("p j e -> p e j"), 1, PARTS), X_AXIS, ALU.add)
            last.then_inc(mask_ready, 1)
            dve.wait_ge(mask_ready, 1)
            dve.wait_ge(top_exp, 1)
            for t in range(T):
                last = v.reciprocal(TSUM(t, 2), TSUM(t, 1))
            then(L, last)
            for t in range(T):
                last = v.tensor_scalar(PROBS(t), PROBS(t), TSUM(t, 2), None, ALU.mult)
            then(L, last)
            for t in range(T):
                last = v.tensor_tensor(HOT(t), HOT(t), times(PROBS(t), 2, NE), ALU.mult)
            then(L, last)
            for t in range(T):
                last = v.tensor_reduce(GATE[:, t, :].rearrange("p (r e) -> p r e", e=NE),
                                       times(HOT(t).rearrange("p j e -> p e j"), 1, PARTS), X_AXIS, ALU.add)
            then(L, last)
            dve.wait_ge(ranks_done, 1)
            v.tensor_tensor(FLAG, PA[:, 0, 2 * NE:2 * NE + 1], k_("full"), ALU.is_gt).then_inc(flags_ready, 1)
            for t in range(T):
                last = v.scalar_tensor_tensor(RK[:, t, 0:NE], PA[:, 0, t * NE:(t + 1) * NE], 1.0, MASK(t)[:, 0:NE], ALU.add, ALU.mult)
            then(L, last)
            for t in range(T):
                for r in range(1, PARTS):
                    last = v.tensor_scalar(RK[:, t, r * NE:(r + 1) * NE], RK[:, t, 0:NE], float(-r * SLOTS), None, ALU.add)
            last.then_inc(routed, 1)
            dve.wait_ge(places_done, 1)
            then(L, v.tensor_copy(PLACE, PB[:, 0, 0:2]))
            v.tensor_scalar(PERM, k_("iota")[:, 0:LISTED], PLACE[:, 0:1], FLAG, ALU.is_equal, ALU.mult) \
                .then_inc(perm_ready, 1)
            then(L, v.tensor_scalar(PAIRF, k_("pairs"), PLACE[:, 1:2], None, ALU.is_lt))
            then(L, v.tensor_reduce(NPAIRS, PAIRF, X_AXIS, ALU.add))
            v.tensor_copy(items[:, LISTED:LISTED + 1], NPAIRS)
            dve.wait_ge(items_done, 1)
            v.tensor_copy(SLOT_OF, PA[:, 0, 0:T * LISTED].rearrange("p (t n) -> p t n", t=T))
            v.tensor_copy(GATE_OF, PA[:, 0, T * LISTED:2 * T * LISTED].rearrange("p (t n) -> p t n", t=T))
            v.tensor_copy(items[0:1, 0:LISTED], PB[0:1, 0, 2:2 + LISTED]).then_inc(items_ready, 1)

            def select(G):
                for t in range(T):
                    last = v.tensor_tensor(SELG[:, t], times(k_("iota")[:, 1:1 + SLOTS], 1, 2),
                                           times(SLOT_OF[:, t, bass.ds(2 * G, 2)], 2, SLOTS), ALU.is_equal)
                last.then_inc(S_["selected"], 1)
                dve.wait_ge(*pair_("selected", G, 1))
                for t in range(T):
                    last = v.tensor_tensor(WG[:, t], SELG[:, t], times(GATE_OF[:, t, bass.ds(2 * G, 2)], 2, SLOTS), ALU.mult)
                last.then_inc(S_["sel_ready"], 1)

            def take_rows(G):
                dve.wait_ge(*pair_("gathered", G, 2))
                for c in range(KD // 2):
                    b = c + KD // 2
                    last = v.tensor_scalar(XT[:, b, :], PA[:, 1, c * P:(c + 1) * P], cols[:, 2, b:b + 1],
                                           cols[:, 3, b:b + 1], ALU.mult, ALU.add)
                last.then_inc(S_["xt_dve"], 1)

            dve.wait_ge(items_ready, 1)
            pairs = dve.value_load(items[0:1, LISTED:LISTED + 1], min_val=1, max_val=PAIRS)
            select(0)
            take_rows(0)
            with dve.Fori(0, pairs) as G:
                for x in range(2):
                    dve.wait_ge(*pair_("gu_chunk", G, 4 * x + 4 + GU_CREDIT))
                    v.tensor_scalar(XG, PA[:, 0, :], LIMIT, None, ALU.min).then_inc(S_["clipped"], 1)
                    v.tensor_scalar(XL, PA[:, 1, :], -LIMIT, LIMIT, ALU.max, ALU.min).then_inc(S_["gu_drained"], 1)
                    dve.wait_ge(*pair_("gu_drained", G, x + 1))
                    v.scalar_tensor_tensor(XL, XL, 1.0, XG, ALU.add, ALU.mult).then_inc(S_["gated"], 1)
                    dve.wait_ge(*pair_("sig_ready", G, x + 1))
                    dve.wait_ge(*pair_("gated", G, x + 1))
                    if x:
                        dve.wait_ge(*pair_("act_t", G, 1))
                    v.tensor_tensor(ACTV, XL, SIG, ALU.mult).then_inc(S_["actv_ready"], 1)
                    dve.wait_ge(*pair_("actv_ready", G, x + 1))
                    if x == 0:
                        dve.wait_ge(*pair_("wt_t", G, 1))
                        select(G + 1)
                take_rows(G + 1)
                dve.wait_ge(*pair_("dn_chunk", G, 2 + DN_CREDIT))
                v.tensor_copy(YP[:, BANK:D], PB[:, 1, :]).then_inc(S_["yp_dve"], 1)
            residual(L, POST_FFN, 4, 1)

        @block.tensor
        def _(pe):
            mm = nc.tensor.matmul

            def weights(l, i):
                s, j = i % DENSE_SLOTS, i // DENSE_SLOTS
                pe.wait_ge(wfull[s], l * (32 * USES) + 32 * (j + 1))
                return ring[:, s, :]

            def transposes(l, n):
                pe.wait_ge(*upto("xn_ready", l, n + 1))
                for c in range(KD):
                    pair, b = (PA, c) if c < KD // 2 else (PB, c - KD // 2)
                    for t in range(T):
                        last = nc.tensor.transpose(pair[:, b // 2, (b % 2) * S + t * P:(b % 2) * S + (t + 1) * P],
                                                   XN[:, t, c * P:(c + 1) * P], ident)
                    if c == KD // 2 - 1:
                        last.then_inc(S_["transposed_a"], 1)
                last.then_inc(S_["transposed_b"], 1)

            def ht_ready(l, n):
                pe.wait_ge(*upto("ht_act", l, n + 1))
                pe.wait_ge(*upto("ht_dve", l, n + 1))

            def project_t(l, i, pair, done):
                w = weights(l, i)
                w = w.rearrange("p (c n) -> p c n", n=BANK)
                for b in range(4):
                    for c in range(KD):
                        last = mm(pair[:, b // 2, (b % 2) * S:(b % 2 + 1) * S], w[:, c, b * P:(b + 1) * P],
                                  HT[:, c, :], start=c == 0, stop=c == KD - 1)
                last.then_inc(S_[done], 1)

            def project(l, i, pair, done):
                w = weights(l, i)
                w = w.rearrange("p (c n) -> p c n", n=BANK)
                for t in range(T):
                    for c in range(KD):
                        last = mm(pair[:, t, :], HT[:, c, t * P:(t + 1) * P], w[:, c, :], start=c == 0,
                                  stop=c == KD - 1)
                last.then_inc(S_[done], 1)

            def rotate(l, raw, pair, done):
                for b in range(2):
                    last = mm(pair[:, b, :], k_("rotate"), raw[:, 2 * b:2 * b + 2, :].rearrange("p b s -> p (b s)"),
                              start=True, stop=True)
                last.then_inc(S_[done], 1)

            def score(l, h, q=None, k=None):
                if h >= 2:
                    pe.wait_ge(*upto("logits", l, h - 1))
                q, k = (QT[:, h // 2, :], KT[:, h, :]) if q is None else (q, k)
                for t in range(T):
                    part = slice(0, P) if t == 0 else slice(P, 3 * P)
                    last = mm(PD[:, h % 2, part], q[:, t * P:(t + 1) * P], k[:, 0:(t + 1) * P],
                              start=True, stop=True)
                last.then_inc(S_["scores"], 1)

            def transpose_probs(l, h):
                pe.wait_ge(*upto("probs", l, h + 1))
                if h >= 2:
                    pe.wait_ge(*upto("probs_ready", l, h - 1))
                for b in range(3):
                    last = nc.tensor.transpose(PA[:, h % 2, b * P:(b + 1) * P], prob[:, h % 2, b * P:(b + 1) * P], ident)
                last.then_inc(S_["probs_t"], 1)

            def attend(l, h, val=None, pair=PC):
                pe.wait_ge(*upto("probs_ready", l, h + 1))
                pt = prob[:, 2 + h % 2, :]
                to = slice(h % AH * HD, (h % AH + 1) * HD)
                val = [V[0][:, to], V[1][:, to]] if val is None else val
                mm(pair[:, 0, to], pt[:, 0:P], val[0], start=True, stop=True)
                mm(pair[:, 1, to], pt[:, P:2 * P], val[0], start=True, stop=False)
                mm(pair[:, 1, to], pt[:, 2 * P:3 * P], val[1], start=False, stop=True).then_inc(S_["attended"], 1)

            def level(l, n):
                if n >= 0:
                    pe.wait_ge(*upto("gla_qe", l, n + 1))
                    pe.wait_ge(*upto("gla_ke", l, n + 1))
                    pe.wait_ge(*upto("gla_merged", l, n + 1))
                q, k = (GQ, GKT) if n < 0 else (QE[:, n % 2], KE[:, n % 2])
                for h in range(GH):
                    if n == LEVELS - 1:
                        last = mm(PB[:, 0, h * P:(h + 1) * P], k[:, h, 0:P], q[:, h // 2, P:S], start=True, stop=True)
                        continue
                    for t in range(T):
                        cols = slice(t * P, (t + 1) * P)
                        last = mm(PB[:, t, h * P:(h + 1) * P], k[:, h, cols], q[:, h // 2, cols], start=True, stop=True)
                last.then_inc(S_["gla_scores"], 1)

            pe.wait_ge(const_loaded, 16)
            pe.wait_ge(ones_set, 1)
            pe.sem_inc(S_["dn_done"], DN_CHUNKS)
            pe.sem_inc(S_["gu_chunk"], GU_CREDIT)
            pe.sem_inc(S_["dn_chunk"], DN_CREDIT)
            pe.wait_ge(rel_one, 1)
            pe.wait_ge(rel_loaded, 16)
            mm(PA[0:AH, 0, :], REL[:, :], k_("bucket", BUCKETS + 1), start=True, stop=True).then_inc(dist_done, 1)
            pe.wait_ge(dist_copied, 1)
            with pe.Fori(0, L) as l:
                transposes(l, 0)
                ht_ready(l, 0)
                project_t(l, 0, PC, "q_proj")
                project_t(l, 1, PA, "k_proj")
                pe.wait_ge(*upto("q_raw", l, 1))
                rotate(l, QRAW, PD, "q_rot")
                project(l, 2, PC, "v_proj")
                pe.wait_ge(*upto("k_raw", l, 1))
                rotate(l, KRAW, PB, "k_rot")
                pe.wait_ge(*upto("q_ready", l, 1))
                project_t(l, 3, PD, "gqk_proj")
                pe.wait_ge(*upto("gate_weights", l, 48))
                for c in range(KD):
                    last = mm(PA[0:GR, 0, 0:S], WLOW[:, c, :], HT[:, c, :], start=c == 0, stop=c == KD - 1)
                last.then_inc(S_["low_proj"], 1)
                pe.wait_ge(*upto("k_ready", l, 1))
                project(l, 4, PB, "gv_proj")
                pe.wait_ge(*upto("low_ready", l, 1))
                for a in range(2):
                    last = mm(PA[:, 1, a * S:(a + 1) * S], WGU[:, a * P:(a + 1) * P], LOW[:, :], start=True, stop=True)
                last.then_inc(S_["z_proj"], 1)
                pe.wait_ge(*upto("v_ready", l, 1))
                project(l, 5, PC, "gr_proj")
                pe.wait_ge(*upto("gqk_ready", l, 1))
                score(l, 0)
                pe.wait_ge(*upto("gv_ready", l, 1))
                level(l, -1)
                pe.wait_ge(*upto("decay_sum", l, 1))
                pe.wait_ge(*upto("gr_ready", l, 1))
                for h in range(AH):
                    if h + 1 < AH:
                        score(l, h + 1)
                    level(l, h)
                    transpose_probs(l, h)
                    if h:
                        attend(l, h - 1)
                attend(l, AH - 1)
                pe.wait_ge(*upto("gla_merged", l, LEVELS + 1))
                for h in range(GH):
                    cols = slice(h * P, (h + 1) * P)
                    mm(PD[:, 0, cols], MERGED[:, 0, h, :], GV[:, 0, cols], start=True, stop=True)
                    mm(PD[:, 1, cols], ACROSS[:, h, :], GV[:, 0, cols], start=True, stop=False)
                    last = mm(PD[:, 1, cols], MERGED[:, 1, h, :], GV[:, 1, cols], start=False, stop=True)
                last.then_inc(S_["gla_done"], 1)
                transposes(l, 1)
                ht_ready(l, 1)
                for n in range(OUT_CHUNKS):
                    w = weights(l, IN_CHUNKS + n)
                    w = w.rearrange("p (c n) -> p c n", n=BANK)
                    for t in range(T):
                        for c in range(KD):
                            last = mm((PC, PD)[t][:, n, :], HT[:, c, t * P:(t + 1) * P], w[:, c, :], start=c == 0,
                                      stop=c == KD - 1)
                    last.then_inc(S_["mix_done"], 1)
                transposes(l, 2)
                ht_ready(l, 2)
                for i in range(GU_CHUNKS):
                    w = weights(l, IN_CHUNKS + OUT_CHUNKS + i)
                    w = w.rearrange("p (u c n) -> p u c n", u=2, c=KD)
                    if i >= 2:
                        pe.wait_ge(*upto("act_done", l, i - 1))
                    for u, pair in enumerate((PA, PB)):
                        for b in range(2):
                            for c in range(KD):
                                last = mm(pair[:, i % 2, b * S:(b + 1) * S], w[:, u, c, b * P:(b + 1) * P], HT[:, c, :],
                                          start=c == 0, stop=c == KD - 1)
                    last.then_inc(S_["gu_done"], 1)
                pe.wait_ge(*upto("act_done", l, GU_CHUNKS))
                pe.wait_ge(*upto("ada_used", l, ADA_STEPS))
                for n in range(2 * KD):
                    mm(PA[:, 0, n:n + 1], ASUM[:, n * P:(n + 1) * P], ones[:, 0:1], start=True, stop=True)
                for n in range(2):
                    last = mm(PB[:, n, :], ones[:, :], ASUM[:, 2 * D + n * BANK:2 * D + (n + 1) * BANK], start=True,
                              stop=True)
                last.then_inc(S_["ada_mod"], 1)
                for f in range(FB):
                    if f % 4 == 0:
                        w = weights(l, IN_CHUNKS + OUT_CHUNKS + GU_CHUNKS + f // 4)
                        w = w.rearrange("p (c n) -> p c n", n=D)
                    for t in range(T):
                        for n in range(2):
                            last = mm((PC, PD)[t][:, n, :], ACTT[:, f, t * P:(t + 1) * P],
                                      w[:, f % 4, n * BANK:(n + 1) * BANK], start=f == 0, stop=f == FB - 1)
                    if f % 4 == 3 or f == FB - 1:
                        last.then_inc(S_["dn_done"], 1)

            pe.wait_ge(flipped_loaded, 32)
            pe.wait_ge(*upto("x_ready", L, 1))
            for n, pair in enumerate((PC, PD, PA)):
                for b in range(2):
                    at = (2 * n + b) * BANK
                    last = mm(pair[:, b, :], k_("flip"), FLIPPED.rearrange("p h n -> p (h n)")[:, at:at + BANK], start=True,
                              stop=True)
                last.then_inc(flipped_done, 1)
            pe.wait_ge(bias_b_act, 1)
            pe.wait_ge(bias_b_dve, 1)
            transposes(L, 0)
            ht_ready(L, 0)
            for t in range(T):
                for c in range(KD):
                    last = mm(PB[:, 0, t * AH:(t + 1) * AH], HT[:, c, t * P:(t + 1) * P], WF[:, c, :], start=c == 0,
                              stop=c == KD - 1)
            last.then_inc(forget_logits, 1)
            project_t(L, 0, PC, "q_proj")
            project_t(L, 1, PA, "k_proj")
            pe.wait_ge(log_forget, 1)
            upto_, lf = k_("upto"), LF[:, 0]
            mm(PB[:, 0, 0:AH], upto_, lf[:, 0, :], start=True, stop=True)
            mm(PB[:, 0, AH:2 * AH], ones[:, :], lf[:, 0, :], start=True, stop=False)
            mm(PB[:, 0, AH:2 * AH], upto_, lf[:, 1, :], start=False, stop=True).then_inc(forget_sums, 1)
            pe.wait_ge(forget_cum, 1)
            for h in range(AH):
                row = (PD, PB)[h // 4][:, h % 4 // 2, (h % 2) * S:(h % 2 + 1) * S]
                w = [lf[:, t, h:h + 1].broadcast_to((P, P)) for t in range(T)]
                mm(row[:, 0:P], w[0], upto_, start=True, stop=True)
                mm(row[:, P:S], w[0], ones[:, :], start=True, stop=False)
                last = mm(row[:, P:S], w[1], upto_, start=False, stop=True)
                if h % 4 == 3:
                    last.then_inc(forget_rows, 1)
            pe.wait_ge(*upto("q_ready", L, 1))
            project(L, 2, PC, "v_proj")
            pe.wait_ge(bias_f, 1)
            project_t(L, 3, PD, "q_proj")
            pe.wait_ge(bias_f, 2)
            project_t(L, 4, PB, "k_proj")
            pe.wait_ge(*upto("k_ready", L, 1))
            project(L, 5, PA, "v_proj")
            pe.wait_ge(*upto("v_ready", L, 1))
            pe.wait_ge(*upto("q_ready", L, 2))
            for h in range(2 * AH):
                if h == 0:
                    score(L, 0, *attention(0)[0:2])
                    pe.wait_ge(*upto("v_ready", L, 2))
                    pe.wait_ge(*upto("k_ready", L, 2))
                if h + 1 < 2 * AH:
                    score(L, h + 1, *attention(h + 1)[0:2])
                transpose_probs(L, h)
                if h:
                    attend(L, h - 1, attention(h - 1)[2], attention(h - 1)[4])
            attend(L, 2 * AH - 1, attention(2 * AH - 1)[2], PB)
            transposes(L, 1)
            ht_ready(L, 1)
            for n in range(OUT_CHUNKS):
                w = weights(L, IN_CHUNKS + n).rearrange("p (c n) -> p c n", n=BANK)
                for t in range(T):
                    for c in range(KD):
                        last = mm((PC, PD)[t][:, n, :], HT[:, c, t * P:(t + 1) * P], w[:, c, :], start=c == 0,
                                  stop=c == KD - 1)
                last.then_inc(S_["mix_done"], 1)
            transposes(L, 2)
            ht_ready(L, 2)
            for t in range(T):
                for c in range(KD):
                    last = mm(PA[:, 0, t * NE:(t + 1) * NE], HT[:, c, t * P:(t + 1) * P], WR[:, c, :], start=c == 0,
                              stop=c == KD - 1)
            last.then_inc(router_done, 1)
            pe.wait_ge(mask_ready, 1)
            mm(PA[:, 0, 0:NE], k_("before"), MASK(0)[:, 0:NE], start=True, stop=True)
            mm(PA[:, 0, NE:2 * NE], ones[:, :], MASK(0)[:, 0:NE], start=True, stop=False)
            mm(PA[:, 0, NE:2 * NE], k_("before"), MASK(1)[:, 0:NE], start=False, stop=True)
            for t in range(T):
                last = mm(PA[:, 0, 2 * NE:2 * NE + 1], MASK(t), ones[:, 0:1], start=t == 0, stop=t == T - 1)
            last.then_inc(ranks_done, 1)
            pe.wait_ge(flags_ready, 1)
            pe.wait_ge(*upto("ht_dve", L, 3))
            mm(PB[:, 0, 0:1], k_("before"), FLAG, start=True, stop=True)
            mm(PB[:, 0, 1:2], ones[:, :], FLAG, start=True, stop=True).then_inc(places_done, 1)
            pe.wait_ge(routed, 1)
            for t in range(T):
                nc.tensor.transpose(PA[:, 1, t * P:(t + 1) * P], RK[:, t, :], ident)
                last = nc.tensor.transpose(PA[:, 1, S + t * P:S + (t + 1) * P], GATE[:, t, :], ident)
            last.then_inc(parted_t, 1)
            pe.wait_ge(parted, 1)
            pe.wait_ge(perm_ready, 1)
            for u in range(2):
                for t in range(T):
                    mm(PA[:, 0, (T * u + t) * LISTED:(T * u + t + 1) * LISTED], PARTED[:, u, t * P:(t + 1) * P], PERM,
                       start=True, stop=True)
            mm(PB[0:1, 0, 2:2 + LISTED], k_("expert"), PERM, start=True, stop=True).then_inc(items_done, 1)
            pe.wait_ge(bd_loaded, 16)
            pe.wait_ge(*upto("x_ready", L, 3))
            for t in range(T):
                for n in range(2):
                    mm((PC, PD)[t][:, n, :], PARTED[0:NE, 1, t * P:(t + 1) * P], BD[:, n * BANK:(n + 1) * BANK], start=True,
                       stop=True, skip_group_check=True)

            def gather(G):
                pe.wait_ge(*pair_("sel_ready", G, 1))
                for q in range(2):
                    for c in range(KD // 2):
                        d = KD // 2 * q + c
                        for t in range(T):
                            last = mm(PA[:, q, c * P:(c + 1) * P], XN[:, t, d * P:(d + 1) * P],
                                      SELG[:, t].rearrange("p e n -> p (e n)"), start=t == 0, stop=t == T - 1)
                    last.then_inc(S_["gathered"], 1)

            def gate_up(G, x):
                pe.wait_ge(bfull[x], G * 16 + 16)
                for u in range(2):
                    for h in range(2):
                        at = (2 * u + h) * BANK
                        mm(PA[h * SLOTS:(h + 1) * SLOTS, u, :], ones[:, 0:SLOTS], BZ[x][:, at:at + BANK], start=True, stop=False)
                for c in range(KD):
                    n = 4 * x + c // 2
                    s = n % RING
                    if c % 2 == 0:
                        pe.wait_ge(efull[s], G * 64 + 32 * (n // RING + 1))
                    for u in range(2):
                        for h in range(2):
                            at = (c % 2) * 2 * D + (2 * u + h) * BANK
                            last = mm(PA[h * SLOTS:(h + 1) * SLOTS, u, :], XT[:, c, x * SLOTS:(x + 1) * SLOTS],
                                      ring[:, s, at:at + BANK], start=False, stop=c == KD - 1)
                    if c % 2:
                        last.then_inc(S_["gu_chunk"], 1)

            def down(G):
                for q in range(2):
                    for x in range(2):
                        pe.wait_ge(efull[2 + 2 * q + x], G * 64 + 64)
                    for j in range(4):
                        for n in range(2):
                            for x in range(2):
                                last = mm(PB[x * SLOTS:(x + 1) * SLOTS, n, :], ATT[x][:, j, q, :],
                                          ring[:, 2 + 2 * q + x, j * D + n * BANK:j * D + (n + 1) * BANK],
                                          start=q + j == 0, stop=q + j == 4)
                    last.then_inc(S_["dn_chunk"], 1)

            pe.wait_ge(items_ready, 1)
            pairs = pe.value_load(items[0:1, LISTED:LISTED + 1], min_val=1, max_val=PAIRS)
            gather(0)
            with pe.Fori(0, pairs) as G:
                pe.wait_ge(*pair_("xt_act", G, 1))
                pe.wait_ge(*pair_("xt_dve", G, 1))
                for t in range(T):
                    last = nc.tensor.transpose(PA[:, 0, t * P:(t + 1) * P], WG[:, t].rearrange("p e n -> p (e n)"), ident)
                last.then_inc(S_["wt_t"], 1)
                pe.wait_ge(*pair_("wt_ready", G, 1))
                gate_up(G, 0)
                pe.wait_ge(*pair_("gu_drained", G, 1))
                gate_up(G, 1)
                for x in range(2):
                    pe.wait_ge(*pair_("actv_ready", G, x + 1))
                    for j in range(4):
                        last = nc.tensor.transpose(PB[:, x, j * P:(j + 1) * P], ACTV[:, j * P:(j + 1) * P], ident)
                    last.then_inc(S_["act_t"], 1)
                pe.wait_ge(*pair_("gu_drained", G, 2))
                gather(G + 1)
                pe.wait_ge(*pair_("att_ready", G, 2))
                down(G)
                pe.wait_ge(*pair_("yp_act", G, 1))
                pe.wait_ge(*pair_("yp_dve", G, 1))
                for t in range(T):
                    for n in range(2):
                        last = mm((PC, PD)[t][:, n, :], WT[:, t * P:(t + 1) * P], YP[:, n * BANK:(n + 1) * BANK], start=False,
                                  stop=True, skip_group_check=True)
                last.then_inc(S_["combined"], 1)


_INS = ["x", "mix_pre_norm", "mix_post_norm", "ffn_pre_norm", "ffn_post_norm", "w_in", "gla_w_gate_up",
        "gla_b_gate", "gla_out_norm", "attn_out_norm", "w_out", "w_gate", "w_up", "w_down", "c_2", "w_ada_2",
        "b_ada_2", "g_pre_mix_2", "g_post_mix_2", "w_in_2", "b_forget_2", "rel_bias_2", "w_out_2", "g_pre_ffn_2",
        "g_post_ffn_2", "w_router_2", "b_router_2", "w_gate_up_2", "b_gate_up_2", "w_down_2", "b_down_2"]


def kernel(**inputs):
    import concourse.bacc as bacc
    from concourse.bass_utils import run_bass_kernel_spmd

    nc = bacc.Bacc("TRN2", target_bir_lowering=False, num_devices=1)
    arrays, A = {}, {}
    for name in _INS:
        a = np.ascontiguousarray(inputs[name])
        arrays[name] = a
        A[name] = nc.dram_tensor(name, a.shape, mybir.dt.from_np(a.dtype), kind="ExternalInput").ap()
    arrays["constants"] = constants()
    const = nc.dram_tensor("constants", arrays["constants"].shape, F32, kind="ExternalInput").ap()
    out = nc.dram_tensor("out", (1, S, D), F32, kind="ExternalOutput").ap()
    program(nc, A, const, out)
    return run_bass_kernel_spmd(nc, [arrays], core_ids=[0]).results[0]["out"]
```

```python
from contextlib import ExitStack

import concourse.bass as bass
import numpy as np
from concourse import mybir

P = 128
S = 256
T = S // P
D = 1024
KD = D // P
L = 2
HD = 64
AH = 8
AW = AH * HD
GH, GDV = 4, 128
GK = GH * HD
GR = 16
TAU = 16.0
F = 2816
FB = F // P
NE, TOPK = 32, 4
SLOTS = 64
PARTS = S // SLOTS
FIRST = 2
MIXED = (NE + FIRST * (PARTS - 1)) // 2
SAME = S * TOPK // (SLOTS + 1)
LEAD = (NE - SAME) // 2
LISTED = 2 * (MIXED + SAME + 1)
LIMIT, ALPHA = 7.0, 1.702
EPS = 1e-6
SCALE = HD ** -0.5
OFF = 1e30
ROPE = 16
THETA = 500000.0
BUCKETS, MAXDIST = 32, 128

ALIGN = 32
BANK = 512
SLOT = 4096
DENSE_SLOTS = 3
RING = 6
IN_CHUNKS, OUT_CHUNKS = 6, 2
GU_CHUNKS = FB // 2
DN_BLOCKS = 3
DN_CHUNKS = -(-FB // DN_BLOCKS)
CHUNKS = IN_CHUNKS + OUT_CHUNKS + GU_CHUNKS + DN_CHUNKS
USES = CHUNKS // DENSE_SLOTS
assert USES * DENSE_SLOTS == CHUNKS
ADA_W = 512
ADA_BUFFERS = 3
ADA_STEPS = 3 * D // ADA_W * KD
LEVELS = 8

F32 = mybir.dt.float32
F32R = mybir.dt.float32r
U32 = mybir.dt.uint32
I32 = mybir.dt.int32
ALU = mybir.AluOpType
ACT = mybir.ActivationFunctionType
X_AXIS = mybir.AxisListType.X

CONST = {}
_at = 0
for _name, _n in (("ident", P), ("rotate", P), ("upto", P), ("before", P), ("flip", P),
                  ("cos_q", S), ("sin_q", S), ("cos_k", S), ("sin_k", S),
                  ("dilated", 3 * P), ("causal", 3 * P), ("level", LEVELS * P),
                  ("bucket", 2 * S), ("iota", LISTED), ("before_pair", P), ("over", 1), ("upto_full", 1), ("over_full", 1), ("odd", 1), ("expert", 1),
                  ("pairs", MIXED)):
    CONST[_name] = (_at, _at + _n)
    _at += _n
NCONST = _at


def constants():
    c = {k: np.zeros((P, b - a), np.float32) for k, (a, b) in CONST.items()}
    i = np.arange(P)
    c["ident"][i, i] = 1
    half = ROPE // 2
    for h in range(0, P, HD):
        for d in range(half):
            c["rotate"][h + d + half, h + d] = -1
            c["rotate"][h + d, h + d + half] = 1
    c["upto"][:] = i[:, None] <= i[None, :]
    c["before"][:] = i[:, None] < i[None, :]
    c["flip"][i, P - 1 - i] = 1
    inv = np.float32(THETA) ** (-(np.arange(half, dtype=np.float32) * np.float32(2)) / np.float32(ROPE))
    angle = np.arange(S, dtype=np.float32)[None, :] * inv.astype(np.float32)[:, None]
    cos, sin = np.ones((HD, S)), np.zeros((HD, S))
    cos[:ROPE] = np.tile(np.cos(angle.astype(np.float64)), (2, 1))
    sin[:ROPE] = np.tile(np.sin(angle.astype(np.float64)), (2, 1))
    for name, sign in (("q", -SCALE), ("k", 1.0)):
        c["cos_" + name][:] = np.tile(cos, (2, 1)) * sign
        c["sin_" + name][:] = np.tile(sin, (2, 1)) * sign
    for t in range(T):
        to = slice(0, P) if t == 0 else slice(P, 3 * P)
        d = (t * P + i)[:, None] - np.arange((t + 1) * P)[None, :]
        seen = sum(((d >= 0) & (d <= w) & (d % r == 0)).astype(int) for w, r in ((128, 1), (512, 4), (2048, 16)))
        c["dilated"][:, to] = np.where(seen > 0, -np.log(np.maximum(seen, 1)), OFF)
        c["causal"][:, to] = np.where(d >= 0, 0, OFF)
    for n in range(LEVELS):
        b = 2 << n
        if b <= P:
            m = (i[:, None] // b == i[None, :] // b) & (i[:, None] % b < b // 2) & (i[None, :] % b >= b // 2)
        else:
            m = i[:, None] == i[None, :]
        c["level"][:, n * P:(n + 1) * P] = m
    d = S - 1 - np.arange(2 * S)
    exact = BUCKETS // 2
    far = exact + (np.log(np.maximum(d, 1).astype(np.float32) / np.float32(exact))
                   / np.float32(np.log(MAXDIST / exact)) * np.float32(BUCKETS - exact)).astype(np.int32)
    bucket = np.where(d < exact, np.maximum(d, 0), np.minimum(far, BUCKETS - 1))
    c["bucket"][np.where(d >= 0, bucket, BUCKETS), np.arange(2 * S)] = np.where(d >= 0, -1, OFF)
    c["iota"][:] = np.arange(LISTED)
    part, e, never = i // NE, i % NE, 4.0 * S
    c["over"][:, 0] = np.where(part == 0, -1, np.where(e < FIRST, part * SLOTS, never))
    c["upto_full"][:, 0] = np.where((part == 0) & (e >= FIRST), SLOTS, never)
    c["over_full"][:, 0] = np.where(e < FIRST, never, np.maximum(part // 2 * 2, 1) * SLOTS)
    order = part // 2 * NE + e
    c["before_pair"][:] = order[:, None] < order[None, :]
    c["odd"][:, 0] = 2 * LEAD + part % 2
    c["expert"][:, 0] = e
    c["pairs"][:] = np.arange(MIXED) * 2
    return np.concatenate([c[k] for k in CONST], axis=1).astype(np.float32)


PER = dict(
    x_ready=2 * T, sq_post=2 * T, sq_pre=2 * T, rstd_post=2 * T, rstd_pre=2 * T, pre_ready=2 * T,
    sq_attn=1, sq_gla=1, rstd_attn=1, rstd_gla=1, mixed_ready=1, transposed_a=3, transposed_b=3,
    ht_act=6, ht_dve=6, gains_ready=1, post_gains=32, gate_weights=48,
    q_proj=1, q_raw=1, q_rot=1, q_ready=1, k_proj=1, k_raw=1, k_rot=1, k_ready=1,
    v_proj=1, v_ready=1, gqk_proj=1, gqk_ready=1, low_proj=1, low_ready=1, z_proj=1, z_step=3,
    decay_sum=1, gv_proj=1, gv_ready=1, gr_proj=1, gr_ready=1,
    scores=AH, logits=AH, probs=AH, probs_t=AH, probs_ready=AH, attended=AH, attn_out=1,
    gla_diff=LEVELS, gla_abs=LEVELS, gla_decay=LEVELS, gla_qe=LEVELS, gla_ke=LEVELS,
    gla_scores=LEVELS + 1, gla_merged=LEVELS + 1, gla_done=1, gla_square=1, zeros_set=1,
    mix_done=OUT_CHUNKS + 1, dn_done=DN_CHUNKS + 1, gu_done=GU_CHUNKS, silu_done=GU_CHUNKS, act_done=GU_CHUNKS,
    ht_fine=1, w_coarse=GU_CHUNKS + DN_CHUNKS, w_fine=GU_CHUNKS + DN_CHUNKS, hidden_t=GU_CHUNKS,
    hidden_coarse=GU_CHUNKS, hidden_fine=GU_CHUNKS,
    c_silu=1, ada_used=ADA_STEPS, ada_mod=2, ada_rows=1, ada_cols=1,
    dve_step=12, pool_step=2 + 4 * T,
)
PERG = dict(
    sel_ready=1, selected=1, gathered=2, xt_act=1, xt_dve=1, wt_t=1, wt_ready=1, gu_ready=2, gu_drained=2, clipped=2,
    sig_ready=2, gated=2, actv_ready=2, act_t=2, att_ready=2, dn_chunk=2, yp_act=1, yp_dve=1, combined=1,
)
DN_CREDIT = PERG["dn_chunk"]
GU_MIXED, GU_SAME = 8, 4
MIX_AT, MIX_TILE = (1, OUT_CHUNKS + 1), (OUT_CHUNKS, OUT_CHUNKS + 1)
DN_TAIL = DN_CHUNKS - 2
DN_AT, DN_TILE = [n + 1 + (n >= DN_TAIL) for n in range(DN_CHUNKS)], (DN_TAIL + 1, DN_CHUNKS + 1)
PRE_MIX, ATTN, GLA, POST_MIX, PRE_FFN, POST_FFN = range(6)
IN_ORDER_2 = (0, 1, 2, 3, 5, 4)
USED_2 = [("q_proj", L, 1), ("k_proj", L, 1), ("v_proj", L, 1), ("q_proj", L, 2), ("v_proj", L, 2)]
FREED_2 = [("k_proj", L, 2), ("k_proj", L, 2), ("k_proj", L, 2), ("attended", L, 2 * AH),
           ("mix_done", L, MIX_AT[0]), ("mix_done", L, MIX_AT[1])]
EXPERT_SLOT = [3, 4, 2, 5, 0, 1]
USED = ([(n, 1) for n in ("q_proj", "k_proj", "v_proj", "gqk_proj", "gv_proj", "gr_proj")]
        + [("mix_done", n) for n in MIX_AT] + [("gu_done", n + 1) for n in range(GU_CHUNKS)]
        + [("dn_done", PER["dn_done"] + n) for n in DN_AT])

GAINS = (("mix_pre_norm", 0, KD), ("attn_out_norm", KD, 4), ("gla_out_norm", KD + 4, 4), ("ffn_pre_norm", 2 * KD, KD))


def times(ap, axis, n):
    return ap.unsqueeze(axis).broadcast_to(tuple(ap.shape[:axis]) + (n,) + tuple(ap.shape[axis:]))


def program(nc, A, const, out):
    ctx = ExitStack()
    with ctx:
        place = {}

        def sb(name, shape, dt=F32):
            place[name] = -(-nc.sbuf_base // ALIGN) * ALIGN
            return ctx.enter_context(nc.sbuf_tensor(name, shape, dt, align_bytes=ALIGN))

        def rounded(name, shape):
            return nc.alloc_sbuf_tensor_at(name + "_rounded", shape, F32R, offset=place[name])

        def pb(name):
            return ctx.enter_context(nc.psum_tensor(name, [P, 2, BANK], F32))

        X = sb("X", [P, T, D])
        XN = sb("XN", [P, T, D])
        HT = sb("HT", [P, KD, S])
        ring = sb("ring", [P, RING, SLOT])
        K = sb("K", [P, NCONST])
        arena = sb("arena", [P, FB * S])
        gla = sb("gla", [P, 7 * 1024])
        prob = sb("prob", [P, 4, 3 * P])
        POSTG = sb("POSTG", [P, 2, D])
        gain_all = sb("gain_all", [P, L * 3 * KD])
        GC = sb("GC", [P, 3 * KD])
        WLOW = sb("WLOW", [P, KD, GR])
        WGU = sb("WGU", [GR, GK])
        BGATE = sb("BGATE", [P, 2])
        LOW = sb("LOW", [GR, S])
        ones = sb("ones", [P, P])
        stat = sb("stat", [P, 3, 8 * 6])
        eps, half = sb("eps", [P, 8]), sb("half", [P, 8])
        wait_col = sb("wait_col", [P, 3])
        soft = sb("soft", [P, 3, 2 * 2 * AH])
        cc = sb("cc", [P, 2, KD])
        modc = sb("modc", [P, L, 2 * KD])
        PA, PB, PC, PD = (pb(n) for n in ("PA", "PB", "PC", "PD"))

        def k_(name, rows=P):
            a, b = CONST[name]
            return K[0:rows, a:b]

        ident = k_("ident")
        ar = lambda a, n: arena[:, a:a + n]
        QRAW, KRAW = (ar(1024 * n, 1024).rearrange("p (b s) -> p b s", s=S) for n in (0, 1))
        QT = ar(2048, 1024).rearrange("p (b s) -> p b s", s=S)
        KT = ar(3072, 2048).rearrange("p (h s) -> p h s", s=S)
        gl = lambda a, n: gla[:, a:a + n]
        V = [ar(5120, AW), gl(6656, AW)]
        GKT = gl(0, 1024).rearrange("p (h s) -> p h s", s=S)
        GQ, GB, DIFF, EDEC = (gl(1024 + 512 * n, 512).rearrange("p (a s) -> p a s", a=2) for n in range(4))
        LA = EDEC
        QE = gl(3072, 1024).rearrange("p (u a s) -> p u a s", u=2, a=2)
        KE = ring[:, 5, 1024:3072].rearrange("p (u h s) -> p u h s", u=2, s=S)
        GV, GRS = (gl(4096 + 1024 * n, 1024).rearrange("p (t n) -> p t n", t=T) for n in (0, 1))
        MERGED = ring[:, 5, 0:T * GH * P].rearrange("p (t h n) -> p t h n", t=T, h=GH)
        ACROSS = gl(6144, 512).rearrange("p (h n) -> p h n", h=GH)
        HTC, HTF = (rounded(n, [P, KD, S]) for n in ("HT", "XN"))
        ACTC, ACTF = (rounded(n, [P, FB, S]) for n in ("arena", "gla"))
        ring_r = rounded("ring", [P, RING, SLOT])
        SG = gl(FB * S, 2 * P * T).rearrange("p (t n) -> p t n", t=T)
        HID = gl(FB * S + 2 * P * T, 4 * P * T).rearrange("p (u t n) -> p u t n", u=2, t=T)
        ADAB = prob[:, :, :].rearrange("p a n -> p (a n)").rearrange("p (u n) -> p u n", u=ADA_BUFFERS)
        ASUM = ring[:, 5, 0:3 * D]
        JUNK = [gl(FB * S, D), prob[:, :, :].rearrange("p a n -> p (a n)")[:, 0:D]]
        MINMAX, SUM, RSUM = (soft[:, n, :] for n in range(3))

        QF, KF, VF = (ar(0, 1024).rearrange("p (b s) -> p b s", s=S), ar(1024, 2048).rearrange("p (h s) -> p h s", s=S),
                      [ar(3072 + AW * t, AW) for t in range(T)])
        r5 = lambda a, n: ring[:, 5, a:a + n]
        GATES = [r5(3 * D, D), r5(2 * D, D)]
        QB, KB, VB = (r5(0, 1024).rearrange("p (b s) -> p b s", s=S), r5(1024, 2048).rearrange("p (h s) -> p h s", s=S),
                      [r5(3072 + AW * t, AW) for t in range(T)])
        BIAS_B = gl(0, AH * 3 * P).rearrange("p (h n) -> p h n", h=AH)
        BIAS_F = gl(AH * 3 * P, AH * 3 * P).rearrange("p (h n) -> p h n", h=AH)
        FLIPPED = BIAS_F
        ADAROWS = gl(0, 2 * D)
        WF = sb("WF", [P, KD, AH])
        WR = sb("WR", [P, KD, NE])
        REL = sb("REL", [BUCKETS + 1, AH])
        DIST = gla[0:AH, 2 * D:2 * D + 2 * S]
        badac = sb("badac", [P, 6 * KD])
        gpre = sb("gpre", [P, 2, KD])
        cols = sb("cols", [P, 4, KD])
        brow = sb("brow", [P, NE + AH])
        LF = sb("LF", [P, 3, T, AH])
        XT = ar(0, 1024).rearrange("p (c n) -> p c n", c=KD)
        YP = ar(1024, D)
        WT = ar(2048, S)
        SELG = ar(2304, S).rearrange("p (t e n) -> p t e n", t=T, e=2)
        WG = ar(2560, S).rearrange("p (t e n) -> p t e n", t=T, e=2)
        ATT = [ar(2816 + 512 * n, 512).rearrange("p (h j n) -> p j h n", h=2, n=SLOTS) for n in (0, 1)]
        BZ = [gl(2 * D * n, 2 * D) for n in (0, 1)]
        XG, XL, SIG, ACTV = (gl(4 * D + BANK * n, BANK) for n in range(4))
        BD = prob[0:NE, 0:3, :].rearrange("p a n -> p (a n)")[:, 0:D]
        PARTED = ar(3840, 2 * S).rearrange("p (u s) -> p u s", u=2)
        SLOT_OF, GATE_OF = (gl(6144 + T * LISTED * n, T * LISTED).rearrange("p (t n) -> p t n", t=T) for n in (0, 1))
        RK = gl(6432, T * P).rearrange("p (t n) -> p t n", t=T)
        GATE = gl(6688, T * P).rearrange("p (t n) -> p t n", t=T)
        PERM = gl(6944, LISTED)
        FLAGS, PLACES, NPAIRS = gl(7016, 2), gl(7018, 4), gl(7022, 2)
        PAIRF = gl(7024, MIXED)
        OTHER = gl(7048, LISTED)
        rt = gl(4 * D, T * (5 * NE + 32 + P)).rearrange("p (t n) -> p t n", t=T)
        LOG = lambda t: rt[:, t, 0:NE]
        HOT = lambda t: rt[:, t, NE:5 * NE].rearrange("p (j e) -> p j e", j=TOPK)
        TOP = lambda t: rt[:, t, 5 * NE:5 * NE + 8]
        TOPF = lambda t: rt[:, t, 5 * NE + 8:5 * NE + 8 + TOPK]
        PROBS = lambda t: rt[:, t, 5 * NE + 16:5 * NE + 16 + TOPK]
        TSUM = lambda t, n: rt[:, t, 5 * NE + 24 + n:5 * NE + 25 + n]
        MASK = lambda t: rt[:, t, 5 * NE + 32:5 * NE + 32 + P]
        topi = sb("topi", [P, T, 8], U32)
        items = sb("items", [P, LISTED + 2], I32)
        dist_dram = nc.dram_tensor("dist", (AH, 2 * S), F32, kind="Internal").ap()

        S_ = {}

        def sem(name):
            S_[name] = ctx.enter_context(nc.semaphore(name))
            return S_[name]

        for name in (*PER, *PERG, "gu_chunk"):
            sem(name)
        efull = [sem(f"expert_loaded_{s}") for s in range(RING)]
        bfull = [sem(f"expert_bias_loaded_{s}") for s in range(2)]
        (rel_loaded, rel_one, small_loaded, dist_done, dist_copied, dist_stored, flipped_loaded, flipped_done, bias_b_ready,
         ada_rows_loaded, gates_loaded, gates_biased, gates_ready, cols_ready, kf_zeros, kb_zeros, forget_logits,
         forget_in, forget_step, log_forget, forget_sums, forget_cum, forget_rows, bias_f,
         router_done, top_ready, top_exp, mask_ready, ranks_done, flags_ready, routed, places_done, parted_t, parted, perm_ready, items_done,
         items_ready, bz_zeroed, bd_loaded) = (sem(n) for n in (
             "rel_loaded rel_one small_loaded dist_done dist_copied dist_stored flipped_loaded flipped_done bias_b_ready "
             "ada_rows_loaded gates_loaded gates_biased gates_ready cols_ready kf_zeros kb_zeros "
             "forget_logits forget_in forget_step log_forget forget_sums forget_cum forget_rows "
             "bias_f router_done top_ready top_exp mask_ready ranks_done flags_ready routed places_done "
             "parted_t parted perm_ready items_done items_ready bz_zeroed bd_loaded").split())
        wfull = [sem(f"weights_loaded_{s}") for s in range(DENSE_SLOTS)]
        afull = [sem(f"ada_loaded_{s}") for s in range(ADA_BUFFERS)]
        ident_loaded, const_loaded, x_loaded, gains_loaded, c_loaded = (
            sem(n) for n in ("ident_loaded", "const_loaded", "x_loaded", "gains_loaded", "c_loaded"))
        ones_set, half_set = (sem(n) for n in ("ones_set", "half_set"))
        stored = sem("stored")

        def upto(name, l, k):
            return S_[name], l * PER[name] + k

        def pair_(name, G, k):
            return S_[name], G * PERG[name] + k

        def pair_counts(eng):
            eng.wait_ge(items_ready, 1)
            return (eng.value_load(items[0:1, LISTED:LISTED + 1], min_val=1, max_val=MIXED),
                    eng.value_load(items[0:1, LISTED + 1:LISTED + 2], min_val=0, max_val=SAME))

        def chunk_loaded(l, i):
            return wfull[i % DENSE_SLOTS], l * (32 * USES) + 32 * (i // DENSE_SLOTS + 1)

        def split(k):
            i = IN_CHUNKS + OUT_CHUNKS + k
            width = SLOT if k < GU_CHUNKS else min(DN_BLOCKS, FB - DN_BLOCKS * (k - GU_CHUNKS)) * D
            return (i, ring[:, i % DENSE_SLOTS, 0:width], ring_r[:, i % DENSE_SLOTS, 0:width],
                    ring_r[:, DENSE_SLOTS + k % 2, 0:width])

        def banks(pair):
            return pair[:, :, :].rearrange("p a n -> p (a n)")

        def st(row, ev, a, b):
            return stat[:, row, 8 * ev + a:8 * ev + b]

        def of_head(blocks, r):
            return blocks[r * HD:(r + 1) * HD].rearrange("p (a r) s -> p a r s", r=2)[:, :, r, :]

        def attention(h):
            n = h % AH
            q, k, val, bias, pair = (QF, KF, VF, BIAS_F, PC) if h < AH else (QB, KB, VB, BIAS_B, PB)
            return q[:, n // 2, :], k[:, n, :], [x[:, n * HD:(n + 1) * HD] for x in val], bias[:, n, :], pair

        block = ctx.enter_context(nc.Block())

        def layer_chunk(l, i):
            w = lambda name: A[name][bass.ds(l, 1), :, :].rearrange("l (c p) n -> p (l c) n", p=P)
            if i < IN_CHUNKS + OUT_CHUNKS:
                name, n = ("w_in", i) if i < IN_CHUNKS else ("w_out", i - IN_CHUNKS)
                src, rows, width = w(name)[:, :, n * BANK:(n + 1) * BANK], KD, BANK
            elif i < IN_CHUNKS + OUT_CHUNKS + GU_CHUNKS:
                n = i - IN_CHUNKS - OUT_CHUNKS
                return [(w(name)[:, :, n * S:(n + 1) * S], h * KD * S, KD, S)
                        for h, name in enumerate(("w_gate", "w_up"))]
            else:
                n = DN_BLOCKS * (i - IN_CHUNKS - OUT_CHUNKS - GU_CHUNKS)
                rows, width = min(DN_BLOCKS, FB - n), D
                src = w("w_down")[:, n:n + rows, :]
                if rows == 1:
                    return [(src[:, :, h * BANK:(h + 1) * BANK], h * BANK, 1, BANK) for h in range(2)]
            h = rows // 2
            return [(src[:, 0:h, :], 0, h, width), (src[:, h:rows, :], h * width, rows - h, width)]

        @block.sync
        def _(sp):
            sp.dma_start(X[:, :, :], A["x"][0].rearrange("(t p) d -> p t d", p=P)).then_inc(x_loaded, 16)
            with sp.Fori(0, L) as l:
                for i in range(CHUNKS):
                    s = i % DENSE_SLOTS
                    if i >= DENSE_SLOTS:
                        sp.wait_ge(*upto(USED[i - DENSE_SLOTS][0], l, USED[i - DENSE_SLOTS][1]))
                    else:
                        sp.wait_ge(*upto("dn_done", l, DN_AT[DN_CHUNKS - DENSE_SLOTS + i]))
                    for src, at, rows, width in layer_chunk(l, i):
                        sp.dma_start(ring[:, s, at:at + rows * width].rearrange("p (c n) -> p c n", n=width),
                                     src).then_inc(wfull[s], 16)
            for i in range(IN_CHUNKS + OUT_CHUNKS):
                s = i % DENSE_SLOTS
                if i >= DENSE_SLOTS:
                    sp.wait_ge(*upto(*USED_2[i - DENSE_SLOTS]))
                else:
                    sp.wait_ge(*upto("dn_done", L, DN_AT[DN_CHUNKS - DENSE_SLOTS + i]))
                name, n = ("w_in_2", IN_ORDER_2[i]) if i < IN_CHUNKS else ("w_out_2", i - IN_CHUNKS)
                src = A[name][0].rearrange("(c p) n -> p c n", p=P)[:, :, n * BANK:(n + 1) * BANK]
                for h in range(2):
                    rows = slice(h * KD // 2, (h + 1) * KD // 2)
                    sp.dma_start(ring[:, s, :].rearrange("p (c n) -> p c n", n=BANK)[:, rows, :], src[:, rows, :]) \
                        .then_inc(wfull[s], 16)

            def load_gate_up(e, x, first, waits, bias_free):
                w = A["w_gate_up_2"][0, bass.ds(e, 1), :, :].rearrange("e (c p) n -> p (e c) n", p=P)
                for c in range(4):
                    load_slot(first + c, w[:, 2 * c:2 * c + 2, :], waits[c])
                    if c == 2:
                        sp.wait_ge(*bias_free)
                        sp.dma_start(BZ[x][0:1, :], A["b_gate_up_2"][0, bass.ds(e, 1), :]).then_inc(bfull[x], 16)

            def load_down(e, q, n, wait):
                w = A["w_down_2"][0, bass.ds(e, 1), :, :].rearrange("e (c p) n -> p (e c) n", p=P)
                load_slot(n, w[:, 4 * q:4 * q + 4, :], wait)

            def load_slot(n, src, wait):
                sp.wait_ge(*wait)
                s, rows = EXPERT_SLOT[n % RING], src.shape[1]
                dst = ring[:, s, :].rearrange("p (c n) -> p c n", c=rows)
                for h in range(2):
                    part = slice(h * rows // 2, (h + 1) * rows // 2)
                    sp.dma_start(dst[:, part, :], src[:, part, :]).then_inc(efull[s], 16)

            def load_mixed(chunks, experts, waits, bias_free):
                waits = waits + [(S_["gu_chunk"], chunks + n + 1) for n in range(RING)]
                for x, e in enumerate(experts):
                    load_gate_up(e, x, 4 * x, waits[4 * x:4 * x + 4], bias_free[x])
                for q in range(2):
                    for x, e in enumerate(experts):
                        load_down(e, q, 8 + 2 * q + x, waits[8 + 2 * q + x])

            load_mixed(0, (0, 1), [upto(*x) for x in FREED_2], [(bz_zeroed, 1)] * 2)
            mixed, same = pair_counts(sp)

            def expert(G, x):
                return sp.value_load(items[0:1, bass.ds(2 * G + x, 1)], min_val=0, max_val=NE - 1)

            def load_next(m, others):
                G, chunks = m + others, m * GU_MIXED + others * GU_SAME
                load_mixed(chunks, [expert(G, x) for x in range(2)],
                           [(S_["gu_chunk"], chunks - 1 + n) for n in range(2)]
                           + [pair_("dn_chunk", G, n // 4 + 1) for n in range(2, RING)], [pair_("gu_ready", G, 0)] * 2)

            with sp.Fori(1, LEAD) as m:
                load_next(m, 0)
            with sp.Fori(0, same) as h:
                G = h + LEAD
                e = expert(G, 0)
                used = [(S_["gu_chunk"], LEAD * GU_MIXED + h * GU_SAME)] * 2 \
                    + [pair_("dn_chunk", G, n // 4 + 1) for n in range(2, RING)]
                load_gate_up(e, 0, 0, used[0:4], pair_("gu_ready", G, 0))
                for q in range(2):
                    load_down(e, q, 4 + q, used[4 + q])
            with sp.Fori(LEAD, mixed) as m:
                load_next(m, same)
            for t in range(T):
                sp.wait_ge(*upto("x_ready", L, T + t + 1))
                sp.dma_start(out[0, t * P:(t + 1) * P, :], X[:, t, :]).then_inc(stored, 16)
            sp.wait_ge(stored, 16 * T)

        @block.gpsimd
        def _(pool):
            steps = [0]

            def inverse_rms(l, ev, a, b, squares, ready):
                pool.wait_ge(*squares)
                nc.gpsimd.tensor_tensor(st(1, ev, a, b), st(0, ev, a, b), eps[:, a:b], ALU.add) \
                    .then_inc(S_["pool_step"], 1)
                steps[0] += 1
                pool.wait_ge(*upto("pool_step", l, steps[0]))
                nc.gpsimd.tensor_tensor(st(2, ev, a, b), st(1, ev, a, b), half[:, a:b], ALU.pow).then_inc(ready, 1)

            def norms(l, n, post, pre):
                for t in range(T):
                    inverse_rms(l, post, t, t + 1, upto("sq_post", l, T * n + t + 1), S_["rstd_post"])
                    if pre is not None:
                        inverse_rms(l, pre, t, t + 1, upto("sq_pre", l, T + T * n + t + 1), S_["rstd_pre"])

            nc.gpsimd.memset(eps[:, :], EPS)
            nc.gpsimd.memset(half[:, :], -0.5).then_inc(half_set, 1)
            nc.gpsimd.memset(ones[:, :], 1.0).then_inc(ones_set, 1)
            pool.wait_ge(half_set, 1)
            for t in range(T):
                inverse_rms(0, PRE_MIX, t, t + 1, upto("sq_pre", 0, t + 1), S_["rstd_pre"])
            pool.wait_ge(gains_loaded, 64)
            with pool.Fori(0, L) as l:
                steps[0] = T
                pool.wait_ge(*upto("ada_cols", l, 1))
                pool.wait_ge(*upto("pre_ready", l, T))
                for _, at, n in GAINS:
                    last = nc.gpsimd.tensor_copy(GC[:, at:at + n], gain_all[:, bass.ds(l * n + L * at, n)])
                last.then_inc(S_["gains_ready"], 1)
                nc.gpsimd.memset(gl(0, 1024), 0.0)
                nc.gpsimd.memset(ar(3072, 2048), 0.0)
                nc.gpsimd.memset(ring[:, 5, 0:3072], 0.0).then_inc(S_["zeros_set"], 1)
                row = lambda name: A[name][bass.ds(l, 1), :]
                pool.dma_start(WLOW[:, :, :], A["w_in"][bass.ds(l, 1), :, IN_CHUNKS * BANK:]
                               .rearrange("l (c p) n -> p (l c) n", p=P)).then_inc(S_["gate_weights"], 16)
                pool.dma_start(WGU[:, :], A["gla_w_gate_up"][bass.ds(l, 1), :, :].rearrange("l r n -> (l r) n")) \
                    .then_inc(S_["gate_weights"], 16)
                pool.dma_start(BGATE[:, :], row("gla_b_gate").rearrange("l (a p) -> p (l a)", p=P),
                               allow_slow_non_contiguous=True) \
                    .then_inc(S_["gate_weights"], 16)
                pool.dma_start(POSTG[:, 0, :], row("mix_post_norm").broadcast_to((P, D))).then_inc(S_["post_gains"], 16)
                pool.dma_start(POSTG[:, 1, :], row("ffn_post_norm").broadcast_to((P, D))).then_inc(S_["post_gains"], 16)
                for n in range(LEVELS):
                    pool.wait_ge(*upto("gla_decay", l, n + 1))
                    if n >= 2:
                        pool.wait_ge(*upto("gla_scores", l, n))
                    for r in range(2):
                        last = nc.gpsimd.tensor_tensor(of_head(KE[:, n % 2], r), of_head(GKT, r),
                                                       EDEC[r * HD:(r + 1) * HD], ALU.mult)
                    last.then_inc(S_["gla_ke"], 1)
                inverse_rms(l, ATTN, 0, T, upto("sq_attn", l, 1), S_["rstd_attn"])
                inverse_rms(l, GLA, 0, T * GH, upto("sq_gla", l, 1), S_["rstd_gla"])
                norms(l, 0, POST_MIX, PRE_FFN)
                for s in range(ADA_STEPS):
                    j, kc = divmod(s, KD)
                    if s >= ADA_BUFFERS:
                        pool.wait_ge(*upto("ada_used", l, s - ADA_BUFFERS + 1))
                    pool.dma_start(ADAB[:, s % ADA_BUFFERS, :], A["w_ada_2"][0, kc * P:(kc + 1) * P,
                                                                   bass.ds(l * (3 * D) + j * ADA_W, ADA_W)]) \
                        .then_inc(afull[s % ADA_BUFFERS], 16)
                norms(l, 1, POST_FFN, PRE_MIX)
                assert steps[0] == T + PER["pool_step"]
            steps[0] = T
            for n in range(2):
                pool.dma_start(ADAROWS[:, n * D:(n + 1) * D], A["b_ada_2"][0:1, (3 * n + 2) * D:(3 * n + 3) * D]
                               .broadcast_to((P, D))).then_inc(ada_rows_loaded, 16)
            pool.dma_start(POSTG[:, 0, :], A["g_post_mix_2"].broadcast_to((P, D))).then_inc(gates_loaded, 16)
            pool.dma_start(POSTG[:, 1, :], A["g_post_ffn_2"].broadcast_to((P, D))).then_inc(gates_loaded, 16)
            nc.gpsimd.memset(ar(1024, 2048), 0.0).then_inc(kf_zeros, 1)
            pool.wait_ge(dist_copied, 1)
            pool.dma_start(dist_dram, DIST).then_inc(dist_stored, 16)
            pool.wait_ge(dist_stored, 16)
            for t in range(T):
                pool.dma_start(FLIPPED[:, :, t * P:P + 2 * t * P],
                               bass.AP(tensor=dist_dram.tensor, offset=P - P * t, ap=[[1, P], [2 * S, AH], [1, (t + 1) * P]])) \
                    .then_inc(flipped_loaded, 16)
            pool.wait_ge(gates_ready, 1)
            nc.gpsimd.memset(r5(1024, 2048), 0.0).then_inc(kb_zeros, 1)
            pool.wait_ge(*upto("logits", L, 2 * AH))
            for n in range(2):
                last = nc.gpsimd.memset(BZ[n], 0.0)
            last.then_inc(bz_zeroed, 1)
            norms(L, 0, POST_MIX, PRE_FFN)
            pool.wait_ge(*upto("attended", L, 2 * AH))
            pool.dma_start(BD, A["b_down_2"][0]).then_inc(bd_loaded, 16)
            norms(L, 1, POST_FFN, None)

        @block.scalar
        def _(act):
            A_ = nc.scalar.activation
            rest = CONST["ident"][1]
            act.dma_start(K[:, 0:rest], const[:, 0:rest]).then_inc(ident_loaded, 16)
            for name, at, n in GAINS:
                act.dma_start(gain_all[:, L * at:L * (at + n)], A[name].rearrange("l (c p) -> p (l c)", p=P),
                              allow_slow_non_contiguous=True).then_inc(gains_loaded, 16)
            act.dma_start(K[:, rest:], const[:, rest:]).then_inc(const_loaded, 16)
            act.dma_start(cc[:, 0, :], A["c_2"][0].rearrange("(c p) -> p c", p=P), allow_slow_non_contiguous=True).then_inc(c_loaded, 16)
            act.dma_start(REL[0:BUCKETS, :], A["rel_bias_2"]).then_inc(rel_loaded, 16)
            act.dma_start(WF[:, :, :], A["w_in_2"][0, :, IN_CHUNKS * BANK:].rearrange("(c p) n -> p c n", p=P)) \
                .then_inc(small_loaded, 16)
            act.dma_start(WR[:, :, :], A["w_router_2"][0].rearrange("(c p) n -> p c n", p=P)).then_inc(small_loaded, 16)
            act.dma_start(badac[:, :], A["b_ada_2"][0].rearrange("(c p) -> p c", p=P), allow_slow_non_contiguous=True) \
                .then_inc(small_loaded, 16)
            for n, name in enumerate(("g_pre_mix_2", "g_pre_ffn_2")):
                act.dma_start(gpre[:, n, :], A[name][0].rearrange("(c p) -> p c", p=P), allow_slow_non_contiguous=True) \
                    .then_inc(small_loaded, 16)
            act.dma_start(brow[:, 0:NE], A["b_router_2"].broadcast_to((P, NE))).then_inc(small_loaded, 16)
            act.dma_start(brow[:, NE:NE + AH], A["b_forget_2"].broadcast_to((P, AH))).then_inc(small_loaded, 16)

            def square(src, t, ev, done):
                A_(JUNK[t], src, ACT.Square, scale=D ** -0.5, accum_out=st(0, ev, t, t + 1)).then_inc(S_[done], 1)

            def norms(l, n, rows_ready, post, pre):
                for t in range(T):
                    act.wait_ge(*rows_ready[t])
                    square(banks((PC, PD)[t]), t, post, "sq_post")
                    if pre is not None:
                        act.wait_ge(*upto("x_ready", l, T * n + t + 1))
                        square(X[:, t, :], t, pre, "sq_pre")

            def fill_ht(l, n):
                for half in range(2):
                    act.wait_ge(*upto(("transposed_a", "transposed_b")[half], l, n + 1))
                    if half == 0 and l is not L:
                        act.wait_ge(*upto("gains_ready", l, 1))
                    elif half == 0:
                        act.wait_ge(cols_ready, 1)
                    for b in range(2):
                        c, src = 4 * half + b, (PA, PB)[half][:, 0, b * S:(b + 1) * S]
                        if l is not L:
                            last = A_((HTC if n == 2 else HT)[:, c, :], src, ACT.Copy, scale=GC[:, n * KD + c:n * KD + c + 1])
                        elif n == 1:
                            last = A_(HT[:, c, :], src, ACT.Copy)
                        else:
                            last = A_(HT[:, c, :], src, ACT.Identity, scale=cols[:, n, c:c + 1], bias=cols[:, n + 1, c:c + 1])
                    last.then_inc(S_["ht_act"], 1)

            def coarse(l, k):
                i, w, _, to = split(k)
                act.wait_ge(*chunk_loaded(l, i))
                if k >= 2:
                    act.wait_ge(*upto(USED[i - 2][0], l, USED[i - 2][1]))
                A_(to, w, ACT.Copy).then_inc(S_["w_coarse"], 1)

            def hidden_coarse(l, i):
                act.wait_ge(*upto("hidden_t", l, i + 1))
                A_(ACTC[:, 2 * i:2 * i + 2, :].rearrange("p f s -> p (f s)"), PB[:, i % 2, :], ACT.Copy) \
                    .then_inc(S_["hidden_coarse"], 1)

            def softmax_exp(h, e, at):
                for t in range(T):
                    part = e[:, 0:P] if t == 0 else e[:, P:3 * P]
                    last = A_(part, part, ACT.Exp, scale=-1.0, bias=MINMAX[:, at + t * AH:at + t * AH + 1],
                              accum_out=SUM[:, at + t * AH:at + t * AH + 1])
                last.then_inc(S_["probs"], 1)

            def decay(l, n):
                act.wait_ge(*upto("gla_diff", l, n + 1))
                A_(DIFF[:, :, :], DIFF[:, :, :], ACT.Abs).then_inc(S_["gla_abs"], 1)
                act.wait_ge(*upto("gla_abs", l, n + 1))
                if n:
                    act.wait_ge(*upto("gla_qe", l, n))
                    act.wait_ge(*upto("gla_ke", l, n))
                A_(EDEC[:, :, :], DIFF[:, :, :], ACT.Exp, scale=-1.0 / TAU).then_inc(S_["gla_decay"], 1)

            act.wait_ge(x_loaded, 16)
            for t in range(T):
                square(X[:, t, :], t, PRE_MIX, "sq_pre")
            with act.Fori(0, L) as l:
                fill_ht(l, 0)
                act.wait_ge(*upto("q_proj", l, 1))
                A_(QRAW.rearrange("p b s -> p (b s)"), banks(PC), ACT.Copy).then_inc(S_["q_raw"], 1)
                act.wait_ge(*upto("k_proj", l, 1))
                A_(KRAW.rearrange("p b s -> p (b s)"), banks(PA), ACT.Copy).then_inc(S_["k_raw"], 1)
                act.wait_ge(*upto("v_proj", l, 1))
                for t in range(T):
                    last = A_(V[t], PC[:, t, :], ACT.Copy)
                last.then_inc(S_["v_ready"], 1)
                act.wait_ge(*upto("gqk_proj", l, 1))
                A_(GQ.rearrange("p a s -> p (a s)"), PD[:, 0, :], ACT.Copy, scale=SCALE)
                act.wait_ge(*upto("zeros_set", l, 1))
                for r in range(2):
                    last = A_(of_head(GKT, r), PD[r * HD:(r + 1) * HD, 1, :].rearrange("p (a s) -> p a s", s=S), ACT.Copy)
                last.then_inc(S_["gqk_ready"], 1)
                act.wait_ge(*upto("z_proj", l, 1))
                act.wait_ge(*upto("gate_weights", l, 48))
                for a in range(2):
                    last = A_(DIFF[:, a, :], PA[:, 1, a * S:(a + 1) * S], ACT.Abs, bias=BGATE[:, a:a + 1])
                last.then_inc(S_["z_step"], 1)
                act.wait_ge(*upto("z_step", l, 1))
                A_(DIFF[:, :, :], DIFF[:, :, :], ACT.Exp, scale=-1.0).then_inc(S_["z_step"], 1)
                act.wait_ge(*upto("z_step", l, 2))
                A_(DIFF[:, :, :], DIFF[:, :, :], ACT.Ln, bias=1.0).then_inc(S_["z_step"], 1)
                act.wait_ge(*upto("gv_proj", l, 1))
                A_(GV, PB[:, :, :], ACT.Copy).then_inc(S_["gv_ready"], 1)
                act.wait_ge(*upto("gr_proj", l, 1))
                A_(GRS, PC[:, :, :], ACT.Silu).then_inc(S_["gr_ready"], 1)
                decay(l, 0)
                for h in range(AH):
                    act.wait_ge(*upto("logits", l, h + 1))
                    softmax_exp(h, prob[:, h % 2, :], h)
                    if h + 1 < LEVELS:
                        decay(l, h + 1)
                    act.wait_ge(*upto("probs_t", l, h + 1))
                    if h >= 2:
                        act.wait_ge(*upto("attended", l, h - 1))
                    A_(prob[:, 2 + h % 2, :], PA[:, h % 2, 0:3 * P], ACT.Copy).then_inc(S_["probs_ready"], 1)
                act.wait_ge(*upto("attn_out", l, 1))
                for t in range(T):
                    last = A_(ar(AW * t, AW), XN[:, t, 0:AW], ACT.Square, scale=AW ** -0.5, accum_out=st(0, ATTN, t, t + 1))
                last.then_inc(S_["sq_attn"], 1)
                act.wait_ge(*upto("gla_done", l, 1))
                A_(ar(1024, 1024), banks(PD), ACT.Square, scale=GDV ** -0.5).then_inc(S_["gla_square"], 1)
                fill_ht(l, 1)
                coarse(l, 0)
                norms(l, 0, [upto("mix_done", l, n) for n in MIX_TILE], POST_MIX, PRE_FFN)
                fill_ht(l, 2)
                coarse(l, 1)
                act.wait_ge(c_loaded, 16)
                A_(cc[:, 1, :], cc[:, 0, :], ACT.Silu).then_inc(S_["c_silu"], 1)
                for i in range(GU_CHUNKS):
                    act.wait_ge(*upto("gu_done", l, i + 1))
                    if i:
                        act.wait_ge(*upto("act_done", l, i))
                    A_(SG, (PD, PA)[i % 2][:, :, 0:S], ACT.Silu).then_inc(S_["silu_done"], 1)
                    if i:
                        hidden_coarse(l, i - 1)
                    coarse(l, i + 2)
                hidden_coarse(l, GU_CHUNKS - 1)
                for k in range(GU_CHUNKS + 2, GU_CHUNKS + DN_CHUNKS):
                    coarse(l, k)
                norms(l, 1, [upto("dn_done", l, PER["dn_done"] + n) for n in DN_TILE], POST_FFN, PRE_MIX)
                act.wait_ge(*upto("ada_mod", l, 2))
                A_(modc[:, bass.ds(l, 1), :], PC[:, 0:1, 0:2 * KD], ACT.Copy).then_inc(S_["ada_cols"], 1)

            fill_ht(L, 0)
            def take(pair, done, n, q, k, val, zeros):
                if q is not None:
                    act.wait_ge(*upto("q_proj", L, n))
                    A_(q.rearrange("p b s -> p (b s)"), banks(pair), ACT.Copy, scale=-SCALE).then_inc(S_["q_ready"], 1)
                elif k is not None:
                    act.wait_ge(*upto("k_proj", L, n))
                    act.wait_ge(zeros, 1)
                    for r in range(2):
                        last = A_(of_head(k, r), banks(pair)[r * HD:(r + 1) * HD].rearrange("p (b s) -> p b s", s=S), ACT.Copy)
                    last.then_inc(S_["k_ready"], 1)
                else:
                    act.wait_ge(*upto("v_proj", L, n))
                    for t in range(T):
                        last = A_(val[t], pair[:, t, :], ACT.Copy)
                    last.then_inc(S_["v_ready"], 1)

            def take_flipped(n):
                act.wait_ge(flipped_done, n + 1)
                act.wait_ge(gates_biased, 1)
                A_(BIAS_B.rearrange("p h n -> p (h n)")[:, n * D:(n + 1) * D], banks(PD), ACT.Copy).then_inc(bias_b_ready, 1)

            take(PC, "q_proj", 1, QF, None, None, None)
            act.wait_ge(forget_in, 1)
            A_(LF[:, 1], LF[:, 0], ACT.Abs).then_inc(forget_step, 1)
            act.wait_ge(forget_step, 1)
            A_(LF[:, 1], LF[:, 1], ACT.Exp, scale=-1.0).then_inc(forget_step, 1)
            act.wait_ge(forget_step, 2)
            A_(LF[:, 1], LF[:, 1], ACT.Ln, bias=1.0).then_inc(forget_step, 1)
            act.wait_ge(dist_done, 1)
            A_(DIST, PD[0:AH, 0, :], ACT.Copy).then_inc(dist_copied, 1)
            take(PA, "k_proj", 1, None, KF, None, kf_zeros)
            take_flipped(0)
            take(PC, "v_proj", 1, None, None, VF, None)
            take_flipped(1)
            act.wait_ge(gates_ready, 1)
            take(PA, "q_proj", 2, QB, None, None, None)
            take_flipped(2)
            take(PC, "v_proj", 2, None, None, VB, None)
            take(PA, "k_proj", 2, None, KB, None, kb_zeros)
            for h in range(2 * AH):
                act.wait_ge(*upto("logits", L, h + 1))
                softmax_exp(h, prob[:, h % 2, :], (h // AH) * T * AH + h % AH)
                act.wait_ge(*upto("probs_t", L, h + 1))
                if h >= 2:
                    act.wait_ge(*upto("attended", L, h - 1))
                A_(prob[:, 2 + h % 2, :], PA[:, h % 2, 0:3 * P], ACT.Copy).then_inc(S_["probs_ready"], 1)
            fill_ht(L, 1)
            norms(L, 0, [upto("mix_done", L, n) for n in MIX_TILE], POST_MIX, PRE_FFN)
            fill_ht(L, 2)
            act.wait_ge(top_ready, 1)
            for t in range(T):
                last = A_(PROBS(t), TOP(t)[:, 0:TOPK], ACT.Exp, bias=TSUM(t, 0), accum_out=TSUM(t, 1))
            last.then_inc(top_exp, 1)
            act.wait_ge(parted_t, 1)
            A_(PARTED.rearrange("p u s -> p (u s)"), PA[:, 1, :], ACT.Copy).then_inc(parted, 1)

            def take_rows(G):
                act.wait_ge(*pair_("gathered", G, 1))
                for c in range(KD // 2):
                    last = A_(XT[:, c, :], PA[:, 0, c * P:(c + 1) * P], ACT.Identity, scale=cols[:, 2, c:c + 1],
                              bias=cols[:, 3, c:c + 1])
                last.then_inc(S_["xt_act"], 1)

            mixed, same = pair_counts(act)
            take_rows(0)
            with act.Fori(0, mixed + same) as G:
                act.wait_ge(*pair_("wt_t", G, 1))
                A_(WT, PA[:, 0, 0:S], ACT.Copy).then_inc(S_["wt_ready"], 1)
                for x in range(2):
                    act.wait_ge(*pair_("clipped", G, x + 1))
                    A_(SIG, XG, ACT.Sigmoid, scale=ALPHA).then_inc(S_["sig_ready"], 1)
                for x in range(2):
                    act.wait_ge(*pair_("act_t", G, x + 1))
                    A_(ATT[x], PB[:, x, :].rearrange("p (j h n) -> p j h n", j=4, n=SLOTS), ACT.Copy) \
                        .then_inc(S_["att_ready"], 1)
                take_rows(G + 1)
                act.wait_ge(*pair_("dn_chunk", G, 2 + DN_CREDIT))
                A_(YP[:, 0:BANK], PB[:, 0, :], ACT.Copy).then_inc(S_["yp_act"], 1)
            norms(L, 1, [pair_("combined", mixed + same, 0)] * T, POST_FFN, None)

        @block.vector
        def _(dve):
            v = nc.vector
            steps = [0]

            def then(l, ins):
                ins.then_inc(S_["dve_step"], 1)
                steps[0] += 1
                dve.wait_ge(*upto("dve_step", l, steps[0]))

            def normed(l, n, ev, t):
                dve.wait_ge(*upto("rstd_pre", l, T * n + t + 1))
                v.tensor_scalar(XN[:, t, :], X[:, t, :], st(2, ev, t, t + 1), None, ALU.mult).then_inc(S_["pre_ready"], 1)

            def residual(l, n, post, pre):
                for t in range(T):
                    if t == 0 and l is not L:
                        dve.wait_ge(*upto("post_gains", l, 32))
                    dve.wait_ge(*upto("sq_post", l, T * n + t + 1))
                    then(l, v.tensor_tensor(XN[:, t, :], banks((PC, PD)[t]), POSTG[:, n, :], ALU.mult))
                    dve.wait_ge(*upto("rstd_post", l, T * n + t + 1))
                    v.scalar_tensor_tensor(X[:, t, :], XN[:, t, :], st(2, post, t, t + 1), X[:, t, :], ALU.mult, ALU.add) \
                        .then_inc(S_["x_ready"], 1)
                    if pre is not None:
                        normed(l, n + 1, pre, t)

            def fill_ht(l, n):
                for half in range(2):
                    dve.wait_ge(*upto(("transposed_a", "transposed_b")[half], l, n + 1))
                    if half == 0 and l is not L:
                        dve.wait_ge(*upto("gains_ready", l, 1))
                    for b in range(2):
                        c, src = 4 * half + 2 + b, (PA, PB)[half][:, 1, b * S:(b + 1) * S]
                        if l is not L:
                            last = v.tensor_scalar((HTC if n == 2 else HT)[:, c, :], src, GC[:, n * KD + c:n * KD + c + 1],
                                                   None, ALU.mult)
                        elif n == 1:
                            last = v.tensor_copy(HT[:, c, :], src)
                        else:
                            last = v.tensor_scalar(HT[:, c, :], src, cols[:, n, c:c + 1], cols[:, n + 1, c:c + 1],
                                                   ALU.mult, ALU.add)
                    last.then_inc(S_["ht_dve"], 1)

            def fill_fine(l):
                dve.wait_ge(*upto("ht_dve", l, 6))
                dve.wait_ge(*upto("ht_act", l, 6))
                for c in range(KD):
                    pair, b = (PA, c) if c < KD // 2 else (PB, c - KD // 2)
                    last = v.scalar_tensor_tensor(HTF[:, c, :], pair[:, b // 2, (b % 2) * S:(b % 2 + 1) * S],
                                                  GC[:, 2 * KD + c:2 * KD + c + 1], HTC[:, c, :], ALU.mult, ALU.subtract)
                last.then_inc(S_["ht_fine"], 1)

            def fine(l, k):
                _, w, rest, rounding = split(k)
                dve.wait_ge(*upto("w_coarse", l, k + 1))
                v.tensor_tensor(rest, w, rounding, ALU.subtract).then_inc(S_["w_fine"], 1)

            def modulation(l, some):
                for s in some:
                    j, kc = divmod(s, KD)
                    acc, w = ASUM[:, j * ADA_W:(j + 1) * ADA_W], ADAB[:, s % ADA_BUFFERS, :]
                    dve.wait_ge(afull[s % ADA_BUFFERS], l * (16 * ADA_STEPS // ADA_BUFFERS) + 16 * (s // ADA_BUFFERS + 1))
                    if kc == 0:
                        ins = v.tensor_scalar(acc, w, cc[:, 1, kc:kc + 1], None, ALU.mult)
                    else:
                        dve.wait_ge(*upto("ada_used", l, s))
                        ins = v.scalar_tensor_tensor(acc, w, cc[:, 1, kc:kc + 1], acc, ALU.mult, ALU.add)
                    ins.then_inc(S_["ada_used"], 1)

            def hidden_fine(l, i):
                dve.wait_ge(*upto("hidden_coarse", l, i + 1))
                two = slice(2 * i, 2 * i + 2)
                v.tensor_tensor(ACTF[:, two, :].rearrange("p f s -> p (f s)"), PB[:, i % 2, :], ACTC[:, two, :].rearrange("p f s -> p (f s)"),
                                ALU.subtract).then_inc(S_["hidden_fine"], 1)

            def rope(l, raw, rot, cos, sin, tmp, add, ready):
                dve.wait_ge(const_loaded, 16)
                dve.wait_ge(*upto(ready[0] + "_raw", l, 1))
                v.tensor_tensor(tmp, raw, times(k_(cos), 1, 4), ALU.mult).then_inc(S_["dve_step"], 1)
                steps[0] += 1
                dve.wait_ge(*upto(ready[0] + "_rot", l, 1))
                dve.wait_ge(*upto("dve_step", l, steps[0]))
                then(l, v.tensor_tensor(raw, banks(rot).rearrange("p (b s) -> p b s", s=S), times(k_(sin), 1, 4),
                                        ALU.mult))
                add().then_inc(S_[ready], 1)

            def add_q():
                return v.tensor_tensor(QT, QT, QRAW, ALU.add)

            def add_k():
                for r in range(2):
                    rows = slice(r * HD, (r + 1) * HD)
                    last = v.tensor_tensor(of_head(KT, r), QRAW[rows], KRAW[rows], ALU.add)
                return last

            def logits(l, h, bias, at):
                dve.wait_ge(*upto("scores", l, h + 1))
                if h >= 2:
                    dve.wait_ge(*upto("probs_t", l, h - 1))
                v.memset(wait_col[:, h % 2:h % 2 + 1], 0.0)
                e = prob[:, h % 2, :]
                for t in range(T):
                    part = slice(0, P) if t == 0 else slice(P, 3 * P)
                    last = v.tensor_tensor_reduce(out=e[:, part], in0=PD[:, h % 2, part], in1=bias[:, part], scale=1.0,
                                                  scalar=3.0e38, op0=ALU.add, op1=ALU.min,
                                                  accum_out=MINMAX[:, at + t * AH:at + t * AH + 1])
                last.then_inc(S_["logits"], 1)

            def attended(l, at, pair, to):
                then(l, v.reciprocal(RSUM[:, at:at + T * AH], SUM[:, at:at + T * AH]))
                for t in range(T):
                    last = v.tensor_tensor(XN[:, t, to:to + AW].rearrange("p (h d) -> p h d", d=HD),
                                           pair[:, t, :].rearrange("p (h d) -> p h d", d=HD),
                                           times(RSUM[:, at + t * AH:at + (t + 1) * AH], 2, HD), ALU.mult)
                return last

            def difference(l, n):
                b = 2 << n
                view = GB.rearrange("p a s -> p (a s)").rearrange("p (m b) -> p m b", b=b)
                if n:
                    dve.wait_ge(*upto("gla_decay", l, n))
                v.tensor_tensor(DIFF.rearrange("p a s -> p (a s)").rearrange("p (m b) -> p m b", b=b), view,
                                view[:, :, b // 2 - 1:b // 2].broadcast_to(tuple(view.shape)), ALU.subtract) \
                    .then_inc(S_["gla_diff"], 1)

            def merge(l, n):
                dve.wait_ge(*upto("gla_scores", l, n + 2))
                v.memset(wait_col[:, 2:3], 0.0)
                if n == LEVELS - 1:
                    last = v.tensor_copy(ACROSS, PB[:, 0, :].rearrange("p (h n) -> p h n", h=GH))
                else:
                    m = k_("level")[:, (n % LEVELS) * P:(n % LEVELS + 1) * P].bitcast(U32)
                    for t in range(T):
                        last = v.copy_predicated(MERGED[:, t], times(m, 1, GH),
                                                 PB[:, t, :].rearrange("p (h n) -> p h n", h=GH))
                last.then_inc(S_["gla_merged"], 1)

            v.memset(REL[BUCKETS:BUCKETS + 1, :], 1.0).then_inc(rel_one, 1)
            v.memset(soft[:, :, :], 0.0)
            dve.wait_ge(x_loaded, 16)
            for t in range(T):
                normed(0, 0, PRE_MIX, t)
            dve.wait_ge(ones_set, 1)
            with dve.Fori(0, L) as l:
                steps[0] = 0
                fill_ht(l, 0)
                rope(l, QRAW, PD, "cos_q", "sin_q", QT, add_q, "q_ready")
                dve.wait_ge(*upto("q_ready", l, 1))
                dve.wait_ge(*upto("zeros_set", l, 1))
                rope(l, KRAW, PB, "cos_k", "sin_k", QRAW, add_k, "k_ready")
                dve.wait_ge(*upto("low_proj", l, 1))
                v.tensor_copy(LOW[:, :], PA[0:GR, 0, 0:S]).then_inc(S_["low_ready"], 1)
                dve.wait_ge(*upto("z_step", l, 1))
                dve.wait_ge(*upto("gate_weights", l, 48))
                for a in range(2):
                    last = v.tensor_scalar(LA[:, a, :], PA[:, 1, a * S:(a + 1) * S], BGATE[:, a:a + 1], 0.0,
                                           ALU.add, ALU.min)
                then(l, last)
                dve.wait_ge(*upto("z_step", l, 3))
                then(l, v.tensor_tensor(LA, LA, DIFF, ALU.subtract))
                for a in range(2):
                    last = v.tensor_tensor_scan(GB[:, a, :], ones[:, 0:1].broadcast_to((P, S)),
                                                LA[:, a, :], 0.0, ALU.mult, ALU.add)
                last.then_inc(S_["decay_sum"], 1)
                dve.wait_ge(*upto("decay_sum", l, 1))
                difference(l, 0)
                merge(l, -1)
                for h in range(AH):
                    logits(l, h, k_("dilated"), h)
                    n = h
                    dve.wait_ge(*upto("gla_decay", l, n + 1))
                    if n >= 2:
                        dve.wait_ge(*upto("gla_scores", l, n))
                    v.tensor_tensor(QE[:, n % 2], GQ, EDEC, ALU.mult).then_inc(S_["gla_qe"], 1)
                    if n + 1 < LEVELS:
                        difference(l, n + 1)
                    if n:
                        merge(l, n - 1)
                merge(l, LEVELS - 1)
                dve.wait_ge(*upto("attended", l, AH))
                attended(l, 0, PC, 0).then_inc(S_["attn_out"], 1)
                dve.wait_ge(*upto("gla_square", l, 1))
                v.tensor_reduce(st(0, GLA, 0, T * GH), ar(1024, 1024).rearrange("p (g n) -> p g n", n=GDV), X_AXIS,
                                ALU.add).then_inc(S_["sq_gla"], 1)
                dve.wait_ge(*upto("gr_ready", l, 1))
                for t in range(T):
                    last = v.tensor_tensor(XN[:, t, AW:D], PD[:, t, :], GRS[:, t, :], ALU.mult)
                dve.wait_ge(*upto("rstd_attn", l, 1))
                dve.wait_ge(*upto("attn_out", l, 1))
                for t in range(T):
                    last = v.tensor_scalar(XN[:, t, 0:AW], XN[:, t, 0:AW], st(2, ATTN, t, t + 1), None, ALU.mult)
                then(l, last)
                dve.wait_ge(*upto("rstd_gla", l, 1))
                for t in range(T):
                    w = XN[:, t, AW:D].rearrange("p (h n) -> p h n", n=GDV)
                    last = v.tensor_tensor(w, w, times(st(2, GLA, t * GH, (t + 1) * GH), 2, GDV), ALU.mult)
                last.then_inc(S_["mixed_ready"], 1)
                fill_ht(l, 1)
                fine(l, 0)
                residual(l, 0, POST_MIX, PRE_FFN)
                fill_ht(l, 2)
                fill_fine(l)
                fine(l, 1)
                dve.wait_ge(*upto("c_silu", l, 1))
                for i in range(GU_CHUNKS):
                    dve.wait_ge(*upto("silu_done", l, i + 1))
                    if i >= 2:
                        dve.wait_ge(*upto("hidden_t", l, i - 1))
                    v.tensor_tensor(HID[:, i % 2], SG, (PD, PA)[i % 2][:, :, S:2 * S], ALU.mult).then_inc(S_["act_done"], 1)
                    if i:
                        hidden_fine(l, i - 1)
                    fine(l, i + 2)
                    modulation(l, range(ADA_STEPS)[ADA_BUFFERS * i:ADA_BUFFERS * (i + 1)])
                hidden_fine(l, GU_CHUNKS - 1)
                for i in range(GU_CHUNKS, GU_CHUNKS + DN_CHUNKS - 2):
                    fine(l, i + 2)
                    modulation(l, range(ADA_STEPS)[ADA_BUFFERS * i:ADA_BUFFERS * (i + 1)])
                dve.wait_ge(*upto("ada_mod", l, 1))
                v.tensor_copy(ring[:, 5, bass.ds(3 * D - l * D, D)], banks(PA)).then_inc(S_["ada_rows"], 1)
                residual(l, 1, POST_FFN, PRE_MIX)
                assert steps[0] == PER["dve_step"], steps
            steps[0] = 0
            dve.wait_ge(small_loaded, 16 * 7)
            dve.wait_ge(*upto("ada_cols", L, 1))
            dve.wait_ge(*upto("ada_rows", L, 0))
            for n in range(2):
                for m in range(2):
                    last = v.tensor_tensor(modc[:, n, m * KD:(m + 1) * KD], modc[:, n, m * KD:(m + 1) * KD],
                                           badac[:, (3 * n + m) * KD:(3 * n + m + 1) * KD], ALU.add)
            then(L, last)
            for n in range(2):
                v.scalar_tensor_tensor(cols[:, 2 * n, :], modc[:, n, KD:2 * KD], 1.0, gpre[:, n, :], ALU.add, ALU.mult)
                last = v.tensor_copy(cols[:, 2 * n + 1, :], modc[:, n, 0:KD])
            last.then_inc(cols_ready, 1)
            dve.wait_ge(cols_ready, 1)
            fill_ht(L, 0)
            dve.wait_ge(ada_rows_loaded, 32)
            for n in range(2):
                last = v.tensor_tensor(GATES[n], GATES[n], ADAROWS[:, n * D:(n + 1) * D], ALU.add)
            last.then_inc(gates_biased, 1)
            dve.wait_ge(gates_biased, 1)
            dve.wait_ge(gates_loaded, 32)
            for n in range(2):
                last = v.tensor_tensor(POSTG[:, n, :], POSTG[:, n, :], GATES[n], ALU.mult)
            last.then_inc(gates_ready, 1)
            dve.wait_ge(forget_logits, 1)
            v.tensor_tensor(LF[:, 0], PB[:, 0, 0:T * AH].rearrange("p (t h) -> p t h", t=T),
                            times(brow[:, NE:NE + AH], 1, T), ALU.add).then_inc(forget_in, 1)
            dve.wait_ge(forget_step, 3)
            then(L, v.tensor_scalar(LF[:, 0], LF[:, 0], 0.0, None, ALU.min))
            v.tensor_tensor(LF[:, 0], LF[:, 0], LF[:, 1], ALU.subtract).then_inc(log_forget, 1)
            dve.wait_ge(forget_sums, 1)
            v.tensor_copy(LF[:, 2], PB[:, 0, 0:T * AH].rearrange("p (t h) -> p t h", t=T)).then_inc(forget_cum, 1)
            dve.wait_ge(forget_cum, 1)
            for h in range(AH):
                if h == 0:
                    dve.wait_ge(flipped_done, 3)
                dve.wait_ge(forget_rows, h // 4 + 1)
                row = (PD, PB)[h // 4][:, h % 4 // 2, (h % 2) * S:(h % 2 + 1) * S]
                for t in range(T):
                    part = slice(0, P) if t == 0 else slice(P, 3 * P)
                    last = v.scalar_tensor_tensor(BIAS_F[:, h, part], row[:, 0:(t + 1) * P], LF[:, 2, t, h:h + 1],
                                                  k_("causal")[:, part], ALU.subtract, ALU.add)
                if h % 4 == 3:
                    last.then_inc(bias_f, 1)
            dve.wait_ge(bias_f, 2)
            for h in range(2 * AH):
                logits(L, h, attention(h)[3], (h // AH) * T * AH + h % AH)
                if h == AH + 1:
                    dve.wait_ge(*upto("attended", L, AH))
                    attended(L, 0, PC, 0)
            dve.wait_ge(*upto("attended", L, 2 * AH))
            attended(L, T * AH, PB, AW).then_inc(S_["mixed_ready"], 1)
            fill_ht(L, 1)
            residual(L, 0, POST_MIX, PRE_FFN)
            fill_ht(L, 2)
            dve.wait_ge(router_done, 1)
            for t in range(T):
                last = v.tensor_tensor(LOG(t), PA[:, 0, t * NE:(t + 1) * NE], brow[:, 0:NE], ALU.add)
            then(L, last)
            for t in range(T):
                last = v.max(TOP(t), LOG(t))
            then(L, last)
            for t in range(T):
                v.tensor_scalar(TSUM(t, 0), TOP(t)[:, 0:1], -1.0, None, ALU.mult)
                last = v.max_index(topi[:, t, :], TOP(t), LOG(t))
            last.then_inc(top_ready, 1)
            dve.wait_ge(top_ready, 1)
            for t in range(T):
                last = v.tensor_copy(TOPF(t), topi[:, t, 0:TOPK])
            then(L, last)
            for t in range(T):
                last = v.tensor_tensor(HOT(t), times(k_("iota")[:, 0:NE], 1, TOPK), times(TOPF(t), 2, NE), ALU.is_equal)
            then(L, last)
            for t in range(T):
                last = v.tensor_reduce(MASK(t).rearrange("p (r e) -> p r e", e=NE),
                                       times(HOT(t).rearrange("p j e -> p e j"), 1, PARTS), X_AXIS, ALU.add)
            last.then_inc(mask_ready, 1)
            dve.wait_ge(mask_ready, 1)
            dve.wait_ge(top_exp, 1)
            for t in range(T):
                last = v.reciprocal(TSUM(t, 2), TSUM(t, 1))
            then(L, last)
            for t in range(T):
                last = v.tensor_scalar(PROBS(t), PROBS(t), TSUM(t, 2), None, ALU.mult)
            then(L, last)
            for t in range(T):
                last = v.tensor_tensor(HOT(t), HOT(t), times(PROBS(t), 2, NE), ALU.mult)
            then(L, last)
            for t in range(T):
                last = v.tensor_reduce(GATE[:, t, :].rearrange("p (r e) -> p r e", e=NE),
                                       times(HOT(t).rearrange("p j e -> p e j"), 1, PARTS), X_AXIS, ALU.add)
            then(L, last)
            dve.wait_ge(ranks_done, 1)
            count = PA[:, 0, 2 * NE:2 * NE + 1]
            then(L, v.tensor_tensor(OTHER[:, 0:1], count, k_("upto_full"), ALU.is_le))
            v.scalar_tensor_tensor(FLAGS[:, 0:1], count, k_("over"), OTHER[:, 0:1], ALU.is_gt, ALU.mult)
            v.tensor_tensor(FLAGS[:, 1:2], count, k_("over_full"), ALU.is_gt).then_inc(flags_ready, 1)
            for t in range(T):
                last = v.scalar_tensor_tensor(RK[:, t, 0:NE], PA[:, 0, t * NE:(t + 1) * NE], 1.0, MASK(t)[:, 0:NE], ALU.add, ALU.mult)
            then(L, last)
            for t in range(T):
                for r in range(1, PARTS):
                    last = v.tensor_scalar(RK[:, t, r * NE:(r + 1) * NE], RK[:, t, 0:NE], float(-r * SLOTS), None, ALU.add)
            last.then_inc(routed, 1)
            dve.wait_ge(places_done, 1)
            then(L, v.tensor_copy(PLACES, PB[:, 0, 0:4]))
            v.tensor_tensor(PLACES[:, 1:2], PLACES[:, 1:2], k_("odd"), ALU.add)
            then(L, v.tensor_scalar(OTHER[:, 0:1], PLACES[:, 0:1], 2.0 * LEAD, PLACES[:, 3:4], ALU.is_ge, ALU.mult))
            then(L, v.tensor_tensor(PLACES[:, 0:1], PLACES[:, 0:1], OTHER[:, 0:1], ALU.add))
            v.tensor_scalar(PERM, k_("iota"), PLACES[:, 0:1], FLAGS[:, 0:1], ALU.is_equal, ALU.mult)
            then(L, v.tensor_scalar(OTHER, k_("iota"), PLACES[:, 1:2], FLAGS[:, 1:2], ALU.is_equal, ALU.mult))
            v.tensor_tensor(PERM, PERM, OTHER, ALU.add).then_inc(perm_ready, 1)
            then(L, v.tensor_scalar(PAIRF, k_("pairs"), PLACES[:, 2:3], None, ALU.is_lt))
            v.tensor_scalar(NPAIRS[:, 1:2], PLACES[:, 3:4], 0.5, None, ALU.mult)
            then(L, v.tensor_reduce(NPAIRS[:, 0:1], PAIRF, X_AXIS, ALU.add))
            v.tensor_copy(items[:, LISTED:LISTED + 2], NPAIRS)
            dve.wait_ge(items_done, 1)
            v.tensor_copy(SLOT_OF, PA[:, 0, 0:T * LISTED].rearrange("p (t n) -> p t n", t=T))
            v.tensor_copy(GATE_OF, PA[:, 0, T * LISTED:2 * T * LISTED].rearrange("p (t n) -> p t n", t=T))
            v.tensor_copy(items[0:1, 0:LISTED], PB[0:1, 0, 4:4 + LISTED]).then_inc(items_ready, 1)

            def select(G):
                for t in range(T):
                    last = v.tensor_tensor(SELG[:, t], times(k_("iota")[:, 1:1 + SLOTS], 1, 2),
                                           times(SLOT_OF[:, t, bass.ds(2 * G, 2)], 2, SLOTS), ALU.is_equal)
                last.then_inc(S_["selected"], 1)
                dve.wait_ge(*pair_("selected", G, 1))
                for t in range(T):
                    last = v.tensor_tensor(WG[:, t], SELG[:, t], times(GATE_OF[:, t, bass.ds(2 * G, 2)], 2, SLOTS), ALU.mult)
                last.then_inc(S_["sel_ready"], 1)

            def take_rows(G):
                dve.wait_ge(*pair_("gathered", G, 2))
                for c in range(KD // 2):
                    b = c + KD // 2
                    last = v.tensor_scalar(XT[:, b, :], PA[:, 1, c * P:(c + 1) * P], cols[:, 2, b:b + 1],
                                           cols[:, 3, b:b + 1], ALU.mult, ALU.add)
                last.then_inc(S_["xt_dve"], 1)

            mixed, same = pair_counts(dve)
            select(0)
            take_rows(0)
            with dve.Fori(0, mixed + same) as G:
                for x in range(2):
                    dve.wait_ge(*pair_("gu_ready", G, x + 1))
                    v.tensor_scalar(XG, PA[:, 0, :], LIMIT, None, ALU.min).then_inc(S_["clipped"], 1)
                    v.tensor_scalar(XL, PA[:, 1, :], -LIMIT, LIMIT, ALU.max, ALU.min).then_inc(S_["gu_drained"], 1)
                    dve.wait_ge(*pair_("gu_drained", G, x + 1))
                    v.scalar_tensor_tensor(XL, XL, 1.0, XG, ALU.add, ALU.mult).then_inc(S_["gated"], 1)
                    dve.wait_ge(*pair_("sig_ready", G, x + 1))
                    dve.wait_ge(*pair_("gated", G, x + 1))
                    if x:
                        dve.wait_ge(*pair_("act_t", G, 1))
                    v.tensor_tensor(ACTV, XL, SIG, ALU.mult).then_inc(S_["actv_ready"], 1)
                    dve.wait_ge(*pair_("actv_ready", G, x + 1))
                    if x == 0:
                        dve.wait_ge(*pair_("wt_t", G, 1))
                        select(G + 1)
                take_rows(G + 1)
                dve.wait_ge(*pair_("dn_chunk", G, 2 + DN_CREDIT))
                v.tensor_copy(YP[:, BANK:D], PB[:, 1, :]).then_inc(S_["yp_dve"], 1)
            residual(L, 1, POST_FFN, None)

        @block.tensor
        def _(pe):
            mm = nc.tensor.matmul

            def weights(l, i):
                pe.wait_ge(*chunk_loaded(l, i))
                return ring[:, i % DENSE_SLOTS, :]

            def transposes(l, n):
                for t in range(T):
                    if n == 1:
                        pe.wait_ge(*upto("mixed_ready", l, 1))
                    else:
                        pe.wait_ge(*upto("pre_ready", l, T * (n // 2) + t + 1))
                    for c in range(KD):
                        pair, b = (PA, c) if c < KD // 2 else (PB, c - KD // 2)
                        last = nc.tensor.transpose(pair[:, b // 2, (b % 2) * S + t * P:(b % 2) * S + (t + 1) * P],
                                                   XN[:, t, c * P:(c + 1) * P], ident)
                        if t == T - 1 and c == KD // 2 - 1:
                            last.then_inc(S_["transposed_a"], 1)
                last.then_inc(S_["transposed_b"], 1)

            def ht_ready(l, n, c):
                if c % 4 == 0:
                    pe.wait_ge(*upto("ht_act", l, 2 * n + c // 4 + 1))
                    pe.wait_ge(*upto("ht_dve", l, 2 * n + c // 4 + 1))

            def project_t(l, i, pair, done):
                w = weights(l, i)
                w = w.rearrange("p (c n) -> p c n", n=BANK)
                for b in range(4):
                    for c in range(KD):
                        if i == 0 and b == 0:
                            ht_ready(l, 0, c)
                        last = mm(pair[:, b // 2, (b % 2) * S:(b % 2 + 1) * S], w[:, c, b * P:(b + 1) * P],
                                  HT[:, c, :], start=c == 0, stop=c == KD - 1)
                last.then_inc(S_[done], 1)

            def project(l, i, pair, done):
                w = weights(l, i)
                w = w.rearrange("p (c n) -> p c n", n=BANK)
                for t in range(T):
                    for c in range(KD):
                        last = mm(pair[:, t, :], HT[:, c, t * P:(t + 1) * P], w[:, c, :], start=c == 0,
                                  stop=c == KD - 1)
                last.then_inc(S_[done], 1)

            def project_out(l):
                transposes(l, 1)
                for n in range(OUT_CHUNKS):
                    w = weights(l, IN_CHUNKS + n).rearrange("p (c n) -> p c n", n=BANK)
                    for t in range(T):
                        for c in range(KD):
                            if n + t == 0:
                                ht_ready(l, 1, c)
                            last = mm((PC, PD)[t][:, n, :], HT[:, c, t * P:(t + 1) * P], w[:, c, :], start=c == 0,
                                      stop=c == KD - 1)
                        if t == T - 1 or n == OUT_CHUNKS - 1:
                            last.then_inc(S_["mix_done"], 1)

            def transpose_hidden(l, i):
                pe.wait_ge(*upto("act_done", l, i + 1))
                if i >= 2:
                    pe.wait_ge(*upto("hidden_fine", l, i - 1))
                for b in range(2):
                    for t in range(T):
                        last = nc.tensor.transpose(PB[:, i % 2, b * S + t * P:b * S + (t + 1) * P],
                                                   HID[:, i % 2, t, b * P:(b + 1) * P], ident)
                last.then_inc(S_["hidden_t"], 1)

            def rotate(l, raw, pair, done):
                for b in range(2):
                    last = mm(pair[:, b, :], k_("rotate"), raw[:, 2 * b:2 * b + 2, :].rearrange("p b s -> p (b s)"),
                              start=True, stop=True)
                last.then_inc(S_[done], 1)

            def score(l, h, q=None, k=None):
                if h >= 2:
                    pe.wait_ge(*upto("logits", l, h - 1))
                q, k = (QT[:, h // 2, :], KT[:, h, :]) if q is None else (q, k)
                for t in range(T):
                    part = slice(0, P) if t == 0 else slice(P, 3 * P)
                    last = mm(PD[:, h % 2, part], q[:, t * P:(t + 1) * P], k[:, 0:(t + 1) * P],
                              start=True, stop=True)
                last.then_inc(S_["scores"], 1)

            def transpose_probs(l, h):
                pe.wait_ge(*upto("probs", l, h + 1))
                if h >= 2:
                    pe.wait_ge(*upto("probs_ready", l, h - 1))
                for b in range(3):
                    last = nc.tensor.transpose(PA[:, h % 2, b * P:(b + 1) * P], prob[:, h % 2, b * P:(b + 1) * P], ident)
                last.then_inc(S_["probs_t"], 1)

            def attend(l, h, val=None, pair=PC):
                pe.wait_ge(*upto("probs_ready", l, h + 1))
                pt = prob[:, 2 + h % 2, :]
                to = slice(h % AH * HD, (h % AH + 1) * HD)
                val = [V[0][:, to], V[1][:, to]] if val is None else val
                mm(pair[:, 0, to], pt[:, 0:P], val[0], start=True, stop=True)
                mm(pair[:, 1, to], pt[:, P:2 * P], val[0], start=True, stop=False)
                mm(pair[:, 1, to], pt[:, 2 * P:3 * P], val[1], start=False, stop=True).then_inc(S_["attended"], 1)

            def level(l, n):
                if n >= 0:
                    pe.wait_ge(*upto("gla_qe", l, n + 1))
                    pe.wait_ge(*upto("gla_ke", l, n + 1))
                    pe.wait_ge(*upto("gla_merged", l, n + 1))
                q, k = (GQ, GKT) if n < 0 else (QE[:, n % 2], KE[:, n % 2])
                for h in range(GH):
                    if n == LEVELS - 1:
                        last = mm(PB[:, 0, h * P:(h + 1) * P], k[:, h, 0:P], q[:, h // 2, P:S], start=True, stop=True)
                        continue
                    for t in range(T):
                        cols = slice(t * P, (t + 1) * P)
                        last = mm(PB[:, t, h * P:(h + 1) * P], k[:, h, cols], q[:, h // 2, cols], start=True, stop=True)
                last.then_inc(S_["gla_scores"], 1)

            pe.sem_inc(S_["dn_done"], PER["dn_done"])
            pe.sem_inc(S_["dn_chunk"], DN_CREDIT)
            pe.sem_inc(S_["ada_cols"], 1)
            pe.wait_ge(ident_loaded, 16)
            pe.wait_ge(ones_set, 1)
            with pe.Fori(0, L) as l:
                transposes(l, 0)
                pe.wait_ge(*upto("ada_cols", l, 1))
                project_t(l, 0, PC, "q_proj")
                project_t(l, 1, PA, "k_proj")
                pe.wait_ge(const_loaded, 16)
                pe.wait_ge(*upto("q_raw", l, 1))
                rotate(l, QRAW, PD, "q_rot")
                project(l, 2, PC, "v_proj")
                pe.wait_ge(*upto("k_raw", l, 1))
                rotate(l, KRAW, PB, "k_rot")
                pe.wait_ge(*upto("q_ready", l, 1))
                project_t(l, 3, PD, "gqk_proj")
                pe.wait_ge(*upto("gate_weights", l, 48))
                for c in range(KD):
                    last = mm(PA[0:GR, 0, 0:S], WLOW[:, c, :], HT[:, c, :], start=c == 0, stop=c == KD - 1)
                last.then_inc(S_["low_proj"], 1)
                pe.wait_ge(*upto("k_ready", l, 1))
                project(l, 4, PB, "gv_proj")
                pe.wait_ge(*upto("low_ready", l, 1))
                for a in range(2):
                    last = mm(PA[:, 1, a * S:(a + 1) * S], WGU[:, a * P:(a + 1) * P], LOW[:, :], start=True, stop=True)
                last.then_inc(S_["z_proj"], 1)
                pe.wait_ge(*upto("v_ready", l, 1))
                project(l, 5, PC, "gr_proj")
                pe.wait_ge(*upto("gqk_ready", l, 1))
                score(l, 0)
                pe.wait_ge(*upto("gv_ready", l, 1))
                level(l, -1)
                pe.wait_ge(*upto("decay_sum", l, 1))
                pe.wait_ge(*upto("gr_ready", l, 1))
                for h in range(AH):
                    if h + 1 < AH:
                        score(l, h + 1)
                    level(l, h)
                    transpose_probs(l, h)
                    if h:
                        attend(l, h - 1)
                attend(l, AH - 1)
                pe.wait_ge(*upto("gla_merged", l, LEVELS + 1))
                for h in range(GH):
                    cols = slice(h * P, (h + 1) * P)
                    mm(PD[:, 0, cols], MERGED[:, 0, h, :], GV[:, 0, cols], start=True, stop=True)
                    mm(PD[:, 1, cols], ACROSS[:, h, :], GV[:, 0, cols], start=True, stop=False)
                    last = mm(PD[:, 1, cols], MERGED[:, 1, h, :], GV[:, 1, cols], start=False, stop=True)
                last.then_inc(S_["gla_done"], 1)
                project_out(l)
                transposes(l, 2)
                for i in range(GU_CHUNKS):
                    pe.wait_ge(*upto("w_fine", l, i + 1))
                    wf, wc = (w.rearrange("p (u c n) -> p c u n", u=2, c=KD) for w in split(i)[2:])
                    if i >= 2:
                        pe.wait_ge(*upto("act_done", l, i - 1))
                    for t in range(T):
                        acc = (PD, PA)[i % 2][:, t, :].rearrange("p (u n) -> p u n", u=2)
                        rows = slice(t * P, (t + 1) * P)
                        for c in range(KD):
                            if i + t == 0:
                                ht_ready(l, 2, c)
                            mm(acc, HTC[:, c, rows], wc[:, c], start=c == 0, stop=False)
                            mm(acc, HTC[:, c, rows], wf[:, c], start=False, stop=False)
                        if i + t == 0:
                            pe.wait_ge(*upto("ht_fine", l, 1))
                        for c in range(KD):
                            last = mm(acc, HTF[:, c, rows], wc[:, c], start=False, stop=c == KD - 1)
                    last.then_inc(S_["gu_done"], 1)
                    if i:
                        transpose_hidden(l, i - 1)
                tail, one, both = DN_BLOCKS * DN_TAIL, ((0,), (1,)), range(T)
                for tiles, blocks in (*((t, range(DN_BLOCKS)) for t in one), (both, range(DN_BLOCKS, tail)),
                                      *((t, range(tail, FB)) for t in one)):
                    if tiles == (1,) and blocks[0] == 0:
                        transpose_hidden(l, GU_CHUNKS - 1)
                    for f in blocks:
                        if f % 2 == 0 and tiles != (1,):
                            pe.wait_ge(*upto("hidden_fine", l, f // 2 + 1))
                        if f == FB - 2 and tiles == (0,):
                            pe.wait_ge(*upto("ada_used", l, ADA_STEPS))
                            for n in range(2):
                                last = mm(PA[:, n, :], ones[:, :], ASUM[:, 2 * D + n * BANK:2 * D + (n + 1) * BANK],
                                          start=True, stop=True)
                            last.then_inc(S_["ada_mod"], 1)
                        if f % DN_BLOCKS == 0 and tiles != (1,):
                            pe.wait_ge(*upto("w_fine", l, GU_CHUNKS + f // DN_BLOCKS + 1))
                        wf, wc = (w.rearrange("p (f n) -> p f n", n=D)[:, f % DN_BLOCKS]
                                  for w in split(GU_CHUNKS + f // DN_BLOCKS)[2:])
                        for t in tiles:
                            rows = slice(t * P, (t + 1) * P)
                            for n in range(2):
                                acc, at = (PC, PD)[t][:, n, :], slice(n * BANK, (n + 1) * BANK)
                                mm(acc, ACTC[:, f, rows], wc[:, at], start=f == 0, stop=False)
                                mm(acc, ACTC[:, f, rows], wf[:, at], start=False, stop=False)
                                last = mm(acc, ACTF[:, f, rows], wc[:, at], start=False, stop=f == FB - 1)
                        if f == FB - 1 or f % DN_BLOCKS == DN_BLOCKS - 1 and tiles != (0,):
                            last.then_inc(S_["dn_done"], 1)
                pe.wait_ge(*upto("x_ready", l, T + 1))
                for n in range(2 * KD):
                    last = mm(PC[:, 0, n:n + 1], ASUM[:, n * P:(n + 1) * P], ones[:, 0:1], start=True, stop=True)
                last.then_inc(S_["ada_mod"], 1)
                pe.wait_ge(*upto("ada_rows", l, 1))

            transposes(L, 0)
            pe.wait_ge(*upto("ada_cols", L, 1))
            def flip(n):
                if n == 0:
                    pe.wait_ge(dist_copied, 1)
                    pe.wait_ge(flipped_loaded, 32)
                else:
                    pe.wait_ge(bias_b_ready, n)
                for b in range(2):
                    at = (2 * n + b) * BANK
                    last = mm(PD[:, b, :], k_("flip"), FLIPPED.rearrange("p h n -> p (h n)")[:, at:at + BANK], start=True,
                              stop=True)
                last.then_inc(flipped_done, 1)

            project_t(L, 0, PC, "q_proj")
            for t in range(T):
                for c in range(KD):
                    last = mm(PB[:, 0, t * AH:(t + 1) * AH], HT[:, c, t * P:(t + 1) * P], WF[:, c, :], start=c == 0,
                              stop=c == KD - 1)
            last.then_inc(forget_logits, 1)
            pe.wait_ge(rel_one, 1)
            pe.wait_ge(rel_loaded, 16)
            mm(PD[0:AH, 0, :], REL[:, :], k_("bucket", BUCKETS + 1), start=True, stop=True).then_inc(dist_done, 1)
            project_t(L, 1, PA, "k_proj")
            flip(0)
            pe.wait_ge(log_forget, 1)
            upto_, lf = k_("upto"), LF[:, 0]
            mm(PB[:, 0, 0:AH], upto_, lf[:, 0, :], start=True, stop=True)
            mm(PB[:, 0, AH:2 * AH], ones[:, :], lf[:, 0, :], start=True, stop=False)
            mm(PB[:, 0, AH:2 * AH], upto_, lf[:, 1, :], start=False, stop=True).then_inc(forget_sums, 1)
            pe.wait_ge(*upto("q_ready", L, 1))
            project(L, 2, PC, "v_proj")
            flip(1)
            pe.wait_ge(*upto("k_ready", L, 1))
            project_t(L, 3, PA, "q_proj")
            flip(2)
            pe.wait_ge(*upto("v_ready", L, 1))
            project(L, 4, PC, "v_proj")
            pe.wait_ge(bias_b_ready, 3)
            pe.wait_ge(forget_cum, 1)
            for h in range(AH):
                row = (PD, PB)[h // 4][:, h % 4 // 2, (h % 2) * S:(h % 2 + 1) * S]
                w = [lf[:, t, h:h + 1].broadcast_to((P, P)) for t in range(T)]
                mm(row[:, 0:P], w[0], upto_, start=True, stop=True)
                mm(row[:, P:S], w[0], ones[:, :], start=True, stop=False)
                last = mm(row[:, P:S], w[1], upto_, start=False, stop=True)
                if h % 4 == 3:
                    last.then_inc(forget_rows, 1)
            pe.wait_ge(*upto("q_ready", L, 2))
            project_t(L, 5, PA, "k_proj")
            pe.wait_ge(bias_f, 2)
            for h in range(2 * AH):
                if h == 0:
                    score(L, 0, *attention(0)[0:2])
                    pe.wait_ge(*upto("v_ready", L, 2))
                    pe.wait_ge(*upto("k_ready", L, 2))
                if h + 1 < 2 * AH:
                    score(L, h + 1, *attention(h + 1)[0:2])
                transpose_probs(L, h)
                if h:
                    attend(L, h - 1, attention(h - 1)[2], attention(h - 1)[4])
            attend(L, 2 * AH - 1, attention(2 * AH - 1)[2], PB)
            project_out(L)
            transposes(L, 2)
            for t in range(T):
                for c in range(KD):
                    if t == 0:
                        ht_ready(L, 2, c)
                    last = mm(PA[:, 0, t * NE:(t + 1) * NE], HT[:, c, t * P:(t + 1) * P], WR[:, c, :], start=c == 0,
                              stop=c == KD - 1)
            last.then_inc(router_done, 1)
            pe.wait_ge(mask_ready, 1)
            mm(PA[:, 0, 0:NE], k_("before"), MASK(0)[:, 0:NE], start=True, stop=True)
            mm(PA[:, 0, NE:2 * NE], ones[:, :], MASK(0)[:, 0:NE], start=True, stop=False)
            mm(PA[:, 0, NE:2 * NE], k_("before"), MASK(1)[:, 0:NE], start=False, stop=True)
            for t in range(T):
                last = mm(PA[:, 0, 2 * NE:2 * NE + 1], MASK(t), ones[:, 0:1], start=t == 0, stop=t == T - 1)
            last.then_inc(ranks_done, 1)
            pe.wait_ge(flags_ready, 1)
            mm(PB[:, 0, 0:1], k_("before"), FLAGS[:, 0:1], start=True, stop=True)
            mm(PB[:, 0, 1:2], k_("before_pair"), FLAGS[:, 1:2], start=True, stop=True)
            mm(PB[:, 0, 2:4], ones[:, :], FLAGS, start=True, stop=True).then_inc(places_done, 1)
            pe.wait_ge(routed, 1)
            for t in range(T):
                nc.tensor.transpose(PA[:, 1, t * P:(t + 1) * P], RK[:, t, :], ident)
                last = nc.tensor.transpose(PA[:, 1, S + t * P:S + (t + 1) * P], GATE[:, t, :], ident)
            last.then_inc(parted_t, 1)
            pe.wait_ge(parted, 1)
            pe.wait_ge(perm_ready, 1)
            for u in range(2):
                for t in range(T):
                    mm(PA[:, 0, (T * u + t) * LISTED:(T * u + t + 1) * LISTED], PARTED[:, u, t * P:(t + 1) * P], PERM,
                       start=True, stop=True)
            mm(PB[0:1, 0, 4:4 + LISTED], k_("expert"), PERM, start=True, stop=True).then_inc(items_done, 1)
            def gather(G):
                pe.wait_ge(*pair_("sel_ready", G, 1))
                for q in range(2):
                    for c in range(KD // 2):
                        d = KD // 2 * q + c
                        for t in range(T):
                            last = mm(PA[:, q, c * P:(c + 1) * P], XN[:, t, d * P:(d + 1) * P],
                                      SELG[:, t].rearrange("p e n -> p (e n)"), start=t == 0, stop=t == T - 1)
                    last.then_inc(S_["gathered"], 1)

            def gate_up(x, slots, loaded, bias, biased, release):
                for c in range(KD):
                    s = slots[c // 2]
                    if c % 2 == 0:
                        pe.wait_ge(efull[s], loaded[c // 2])
                    for u in range(2):
                        for h in range(2):
                            at = (c % 2) * 2 * D + (2 * u + h) * BANK
                            last = mm(PA[h * SLOTS:(h + 1) * SLOTS, u, :], XT[:, c, x * SLOTS:(x + 1) * SLOTS],
                                      ring[:, s, at:at + BANK], start=c == 0, stop=False)
                    if c % 2 and release:
                        last.then_inc(S_["gu_chunk"], 1)
                pe.wait_ge(*biased)
                for u in range(2):
                    for h in range(2):
                        at = (2 * u + h) * BANK
                        last = mm(PA[h * SLOTS:(h + 1) * SLOTS, u, :], ones[:, 0:SLOTS], bias[:, at:at + BANK],
                                  start=False, stop=True)
                last.then_inc(S_["gu_ready"], 1)

            def down(slots, loaded):
                for q in range(2):
                    for x in range(2):
                        pe.wait_ge(efull[slots[q][x]], loaded)
                    for j in range(4):
                        for n in range(2):
                            for x in range(2):
                                last = mm(PB[x * SLOTS:(x + 1) * SLOTS, n, :], ATT[x][:, j, q, :],
                                          ring[:, slots[q][x], j * D + n * BANK:j * D + (n + 1) * BANK],
                                          start=q + j == 0, stop=q + j == 4)
                    last.then_inc(S_["dn_chunk"], 1)

            def items_pair(G, gate_ups, downs):
                pe.wait_ge(*pair_("xt_act", G, 1))
                pe.wait_ge(*pair_("xt_dve", G, 1))
                for t in range(T):
                    last = nc.tensor.transpose(PA[:, 0, t * P:(t + 1) * P], WG[:, t].rearrange("p e n -> p (e n)"), ident)
                last.then_inc(S_["wt_t"], 1)
                pe.wait_ge(*pair_("wt_ready", G, 1))
                gate_up(0, *gate_ups[0])
                pe.wait_ge(*pair_("gu_drained", G, 1))
                gate_up(1, *gate_ups[1])
                for x in range(2):
                    pe.wait_ge(*pair_("actv_ready", G, x + 1))
                    for j in range(4):
                        last = nc.tensor.transpose(PB[:, x, j * P:(j + 1) * P], ACTV[:, j * P:(j + 1) * P], ident)
                    last.then_inc(S_["act_t"], 1)
                pe.wait_ge(*pair_("gu_drained", G, 2))
                gather(G + 1)
                pe.wait_ge(*pair_("att_ready", G, 2))
                down(*downs)
                pe.wait_ge(*pair_("yp_act", G, 1))
                pe.wait_ge(*pair_("yp_dve", G, 1))
                for t in range(T):
                    for n in range(2):
                        last = mm((PC, PD)[t][:, n, :], WT[:, t * P:(t + 1) * P], YP[:, n * BANK:(n + 1) * BANK], start=False,
                                  stop=True, skip_group_check=True)
                last.then_inc(S_["combined"], 1)

            mixed, same = pair_counts(pe)
            gather(0)
            pe.wait_ge(bd_loaded, 16)
            pe.wait_ge(*upto("x_ready", L, T))
            for t in range(T):
                for n in range(2):
                    mm((PC, PD)[t][:, n, :], PARTED[0:NE, 1, t * P:(t + 1) * P], BD[:, n * BANK:(n + 1) * BANK], start=True,
                       stop=True, skip_group_check=True)
            def mixed_pair(m, others):
                ups = [(EXPERT_SLOT[n % RING], m * 64 + others * 32 + 32 * (n // RING + 1)) for n in range(8)]
                biased = [(bfull[0], m * 16 + others * 16 + 16), (bfull[1], m * 16 + 16)]
                items_pair(m + others, [([s for s, _ in ups[4 * x:4 * x + 4]], [w for _, w in ups[4 * x:4 * x + 4]], BZ[x],
                                         biased[x], True) for x in range(2)],
                           ([[EXPERT_SLOT[2 + 2 * q + x] for x in range(2)] for q in range(2)], m * 64 + others * 32 + 64))

            with pe.Fori(0, LEAD) as m:
                mixed_pair(m, 0)
            with pe.Fori(0, same) as h:
                loaded = LEAD * 64 + h * 32 + 32
                items_pair(h + LEAD, [(EXPERT_SLOT[0:4], [loaded] * 4, BZ[0], (bfull[0], LEAD * 16 + h * 16 + 16), x == 1)
                                   for x in range(2)],
                           ([[EXPERT_SLOT[4 + q]] * 2 for q in range(2)], loaded))
            with pe.Fori(LEAD, mixed) as m:
                mixed_pair(m, same)


_INS = ["x", "mix_pre_norm", "mix_post_norm", "ffn_pre_norm", "ffn_post_norm", "w_in", "gla_w_gate_up",
        "gla_b_gate", "gla_out_norm", "attn_out_norm", "w_out", "w_gate", "w_up", "w_down", "c_2", "w_ada_2",
        "b_ada_2", "g_pre_mix_2", "g_post_mix_2", "w_in_2", "b_forget_2", "rel_bias_2", "w_out_2", "g_pre_ffn_2",
        "g_post_ffn_2", "w_router_2", "b_router_2", "w_gate_up_2", "b_gate_up_2", "w_down_2", "b_down_2"]


def kernel(**inputs):
    import concourse.bacc as bacc
    from concourse.bass_utils import run_bass_kernel_spmd

    nc = bacc.Bacc("TRN2", target_bir_lowering=False, num_devices=1)
    arrays, A = {}, {}
    for name in _INS:
        a = np.ascontiguousarray(inputs[name])
        arrays[name] = a
        A[name] = nc.dram_tensor(name, a.shape, mybir.dt.from_np(a.dtype), kind="ExternalInput").ap()
    arrays["constants"] = constants()
    const = nc.dram_tensor("constants", arrays["constants"].shape, F32, kind="ExternalInput").ap()
    out = nc.dram_tensor("out", (1, S, D), F32, kind="ExternalOutput").ap()
    program(nc, A, const, out)
    return run_bass_kernel_spmd(nc, [arrays], core_ids=[0]).results[0]["out"]
```

```python
from contextlib import ExitStack

import concourse.bass as bass
import numpy as np
from concourse import mybir

P = 128
S = 256
T = S // P
D = 1024
KD = D // P
L = 2
HD = 64
AH = 8
AW = AH * HD
GH, GDV = 4, 128
GK = GH * HD
GR = 16
TAU = 16.0
F = 2816
FB = F // P
NE, TOPK = 32, 4
SLOTS = 64
PARTS = S // SLOTS
FIRST = 2
MIXED = (NE + FIRST * (PARTS - 1)) // 2
SAME = S * TOPK // (SLOTS + 1)
LEAD = (NE - SAME) // 2
LISTED = 2 * (MIXED + SAME + 1)
LIMIT, ALPHA = 7.0, 1.702
EPS = 1e-6
SCALE = HD ** -0.5
OFF = 1e30
ROPE = 16
THETA = 500000.0
BUCKETS, MAXDIST = 32, 128

ALIGN = 32
BANK = 512
SLOT = 4096
DENSE_SLOTS = 3
RING = 6
IN_CHUNKS, OUT_CHUNKS = 6, 2
GU_CHUNKS = FB // 2
DN_BLOCKS = 3
DN_CHUNKS = -(-FB // DN_BLOCKS)
CHUNKS = IN_CHUNKS + OUT_CHUNKS + GU_CHUNKS + DN_CHUNKS
USES = CHUNKS // DENSE_SLOTS
assert USES * DENSE_SLOTS == CHUNKS
ADA_W = 512
ADA_BUFFERS = 3
ADA_STEPS = 3 * D // ADA_W * KD
LEVELS = 8

F32 = mybir.dt.float32
F32R = mybir.dt.float32r
U32 = mybir.dt.uint32
I32 = mybir.dt.int32
ALU = mybir.AluOpType
ACT = mybir.ActivationFunctionType
X_AXIS = mybir.AxisListType.X

CONST = {}
_at = 0
for _name, _n in (("ident", P), ("rotate", P), ("upto", P), ("before", P), ("flip", P),
                  ("cos_q", S), ("sin_q", S), ("cos_k", S), ("sin_k", S),
                  ("dilated", 3 * P), ("causal", 3 * P), ("level", LEVELS * P),
                  ("bucket", 2 * S), ("iota", LISTED), ("before_pair", P), ("over", 1), ("upto_full", 1), ("over_full", 1), ("odd", 1), ("expert", 1),
                  ("pairs", MIXED)):
    CONST[_name] = (_at, _at + _n)
    _at += _n
NCONST = _at


def constants():
    c = {k: np.zeros((P, b - a), np.float32) for k, (a, b) in CONST.items()}
    i = np.arange(P)
    c["ident"][i, i] = 1
    half = ROPE // 2
    for h in range(0, P, HD):
        for d in range(half):
            c["rotate"][h + d + half, h + d] = -1
            c["rotate"][h + d, h + d + half] = 1
    c["upto"][:] = i[:, None] <= i[None, :]
    c["before"][:] = i[:, None] < i[None, :]
    c["flip"][i, P - 1 - i] = 1
    inv = np.float32(THETA) ** (-(np.arange(half, dtype=np.float32) * np.float32(2)) / np.float32(ROPE))
    angle = np.arange(S, dtype=np.float32)[None, :] * inv.astype(np.float32)[:, None]
    cos, sin = np.ones((HD, S)), np.zeros((HD, S))
    cos[:ROPE] = np.tile(np.cos(angle.astype(np.float64)), (2, 1))
    sin[:ROPE] = np.tile(np.sin(angle.astype(np.float64)), (2, 1))
    for name, sign in (("q", -SCALE), ("k", 1.0)):
        c["cos_" + name][:] = np.tile(cos, (2, 1)) * sign
        c["sin_" + name][:] = np.tile(sin, (2, 1)) * sign
    for t in range(T):
        to = slice(0, P) if t == 0 else slice(P, 3 * P)
        d = (t * P + i)[:, None] - np.arange((t + 1) * P)[None, :]
        seen = sum(((d >= 0) & (d <= w) & (d % r == 0)).astype(int) for w, r in ((128, 1), (512, 4), (2048, 16)))
        c["dilated"][:, to] = np.where(seen > 0, -np.log(np.maximum(seen, 1)), OFF)
        c["causal"][:, to] = np.where(d >= 0, 0, OFF)
    for n in range(LEVELS):
        b = 2 << n
        if b <= P:
            m = (i[:, None] // b == i[None, :] // b) & (i[:, None] % b < b // 2) & (i[None, :] % b >= b // 2)
        else:
            m = i[:, None] == i[None, :]
        c["level"][:, n * P:(n + 1) * P] = m
    d = S - 1 - np.arange(2 * S)
    exact = BUCKETS // 2
    far = exact + (np.log(np.maximum(d, 1).astype(np.float32) / np.float32(exact))
                   / np.float32(np.log(MAXDIST / exact)) * np.float32(BUCKETS - exact)).astype(np.int32)
    bucket = np.where(d < exact, np.maximum(d, 0), np.minimum(far, BUCKETS - 1))
    c["bucket"][np.where(d >= 0, bucket, BUCKETS), np.arange(2 * S)] = np.where(d >= 0, -1, OFF)
    c["iota"][:] = np.arange(LISTED)
    part, e, never = i // NE, i % NE, 4.0 * S
    c["over"][:, 0] = np.where(part == 0, -1, np.where(e < FIRST, part * SLOTS, never))
    c["upto_full"][:, 0] = np.where((part == 0) & (e >= FIRST), SLOTS, never)
    c["over_full"][:, 0] = np.where(e < FIRST, never, np.maximum(part // 2 * 2, 1) * SLOTS)
    order = part // 2 * NE + e
    c["before_pair"][:] = order[:, None] < order[None, :]
    c["odd"][:, 0] = 2 * LEAD + part % 2
    c["expert"][:, 0] = e
    c["pairs"][:] = np.arange(MIXED) * 2
    return np.concatenate([c[k] for k in CONST], axis=1).astype(np.float32)


IN_ORDER = (0, 2, 1, 4, 3, 5)
IN_SPLIT, IN_SPLIT_2 = (1, 3, 5), (2, 4)

PER = dict(
    x_ready=2 * T, sq_post=2 * T, sq_pre=2 * T, rstd_post=2 * T, rstd_pre=2 * T, pre_ready=2 * T,
    sq_attn=1, sq_gla=1, rstd_attn=1, rstd_gla=1, mixed_ready=2, transposed_a=3, transposed_b=3,
    ht_act=6, ht_dve=6, gains_ready=1, post_gains=32, gate_weights=48,
    q_proj=1, q_raw=1, q_rot=1, q_ready=1, k_proj=1, k_raw=1, k_rot=1, k_ready=1,
    v_proj=1, v_ready=1, gqk_proj=1, gqk_ready=1, low_proj=1, low_ready=1, z_proj=1, z_step=3,
    decay_sum=1, gv_proj=1, gv_ready=1, gr_proj=1, gr_ready=1,
    scores=AH, logits=AH, probs=AH, probs_t=AH, probs_ready=AH, attended=AH, attn_out=1,
    gla_diff=LEVELS, gla_abs=LEVELS, gla_decay=LEVELS, gla_qe=LEVELS, gla_ke=LEVELS,
    gla_scores=LEVELS + 1, gla_merged=LEVELS + 1, gla_done=1, gla_square=1, zeros_set=1,
    mix_done=OUT_CHUNKS + 1, dn_done=DN_CHUNKS + 1, gu_done=GU_CHUNKS, silu_done=GU_CHUNKS, act_done=GU_CHUNKS,
    ht_coarse=2, ht_fine=2 + T, w_coarse=len(IN_SPLIT) + 1 + GU_CHUNKS + DN_CHUNKS,
    w_fine=len(IN_SPLIT) + 1 + GU_CHUNKS + DN_CHUNKS, hidden_t=GU_CHUNKS,
    hidden_coarse=GU_CHUNKS, hidden_fine=GU_CHUNKS,
    c_silu=1, ada_used=ADA_STEPS, ada_mod=2, ada_rows=1, ada_cols=1,
    dve_step=12, pool_step=2 + 4 * T,
)
PERG = dict(
    sel_ready=1, selected=1, gathered=2, xt_act=1, xt_dve=1, wt_t=1, wt_ready=1, gu_ready=2, gu_drained=2, clipped=2,
    sig_ready=2, gated=2, actv_ready=2, act_t=2, att_ready=2, dn_chunk=2, yp_act=1, yp_dve=1, combined=T,
)
DN_CREDIT = PERG["dn_chunk"]
GU_MIXED, GU_SAME = 8, 4
MIX_AT, MIX_TILE = (1, OUT_CHUNKS + 1), (OUT_CHUNKS, OUT_CHUNKS + 1)
DN_TAIL = DN_CHUNKS - 2
DN_AT, DN_TILE = [n + 1 + (n >= DN_TAIL) for n in range(DN_CHUNKS)], (DN_TAIL + 1, DN_CHUNKS + 1)
PRE_MIX, ATTN, GLA, POST_MIX, PRE_FFN, POST_FFN = range(6)
IN_ORDER_2 = (0, 1, 2, 3, 5, 4)
USED_2 = [("q_proj", L, 1), ("k_proj", L, 1), ("v_proj", L, 1), ("q_proj", L, 2), ("v_proj", L, 2)]
FREED_2 = [("k_proj", L, 2), ("k_proj", L, 2), ("k_proj", L, 2), ("attended", L, 2 * AH),
           ("mix_done", L, MIX_AT[0]), ("mix_done", L, MIX_AT[1])]
EXPERT_SLOT = [3, 4, 2, 5, 0, 1]
USED = ([(n, 1) for n in ("q_proj", "v_proj", "k_proj", "gv_proj", "gqk_proj", "gr_proj")]
        + [("mix_done", n) for n in MIX_AT] + [("gu_done", n + 1) for n in range(GU_CHUNKS)]
        + [("dn_done", PER["dn_done"] + n) for n in DN_AT])

GAINS = (("mix_pre_norm", 0, KD), ("attn_out_norm", KD, 4), ("gla_out_norm", KD + 4, 4), ("ffn_pre_norm", 2 * KD, KD))


def times(ap, axis, n):
    return ap.unsqueeze(axis).broadcast_to(tuple(ap.shape[:axis]) + (n,) + tuple(ap.shape[axis:]))


def program(nc, A, const, out):
    ctx = ExitStack()
    with ctx:
        place = {}

        def sb(name, shape, dt=F32):
            place[name] = -(-nc.sbuf_base // ALIGN) * ALIGN
            return ctx.enter_context(nc.sbuf_tensor(name, shape, dt, align_bytes=ALIGN))

        def rounded(name, shape):
            return nc.alloc_sbuf_tensor_at(name + "_rounded", shape, F32R, offset=place[name])

        def pb(name):
            return ctx.enter_context(nc.psum_tensor(name, [P, 2, BANK], F32))

        X = sb("X", [P, T, D])
        XN = sb("XN", [P, T, D])
        HT = sb("HT", [P, KD, S])
        ring = sb("ring", [P, RING, SLOT])
        K = sb("K", [P, NCONST])
        arena = sb("arena", [P, FB * S])
        gla = sb("gla", [P, 7 * 1024])
        prob = sb("prob", [P, 4, 3 * P])
        POSTG = sb("POSTG", [P, 2, D])
        gain_all = sb("gain_all", [P, L * 3 * KD])
        GC = sb("GC", [P, 3 * KD])
        WLOW = sb("WLOW", [P, KD, GR])
        WGU = sb("WGU", [GR, GK])
        BGATE = sb("BGATE", [P, 2])
        LOW = sb("LOW", [GR, S])
        ones = sb("ones", [P, P])
        stat = sb("stat", [P, 3, 8 * 6])
        eps, half = sb("eps", [P, 8]), sb("half", [P, 8])
        wait_col = sb("wait_col", [P, 3])
        soft = sb("soft", [P, 3, 2 * 2 * AH])
        cc = sb("cc", [P, 2, KD])
        modc = sb("modc", [P, L, 2 * KD])
        PA, PB, PC, PD = (pb(n) for n in ("PA", "PB", "PC", "PD"))

        def k_(name, rows=P):
            a, b = CONST[name]
            return K[0:rows, a:b]

        ident = k_("ident")
        ar = lambda a, n: arena[:, a:a + n]
        QRAW, KRAW = (ar(1024 * n, 1024).rearrange("p (b s) -> p b s", s=S) for n in (0, 1))
        QT = ar(2048, 1024).rearrange("p (b s) -> p b s", s=S)
        KT = ar(3072, 2048).rearrange("p (h s) -> p h s", s=S)
        gl = lambda a, n: gla[:, a:a + n]
        V = [ar(5120, AW), gl(6656, AW)]
        GKT = gl(0, 1024).rearrange("p (h s) -> p h s", s=S)
        GQ, GB, DIFF, EDEC = (gl(1024 + 512 * n, 512).rearrange("p (a s) -> p a s", a=2) for n in range(4))
        LA = EDEC
        QE = gl(3072, 1024).rearrange("p (u a s) -> p u a s", u=2, a=2)
        KE = ring[:, 5, 1024:3072].rearrange("p (u h s) -> p u h s", u=2, s=S)
        GV, GRS = (gl(4096 + 1024 * n, 1024).rearrange("p (t n) -> p t n", t=T) for n in (0, 1))
        MERGED = ring[:, 5, 0:T * GH * P].rearrange("p (t h n) -> p t h n", t=T, h=GH)
        ACROSS = gl(6144, 512).rearrange("p (h n) -> p h n", h=GH)
        HTC, INF = (rounded(n, [P, KD, S])[:, :, :] for n in ("HT", "XN"))
        HTF = INF.rearrange("p c s -> p (c s)").rearrange("p (t c n) -> p t c n", t=T, c=KD)
        ACTC, ACTF = (rounded(n, [P, FB, S]) for n in ("arena", "gla"))
        ring_r = rounded("ring", [P, RING, SLOT])
        INC = ring_r[:, DENSE_SLOTS + 1, 0:KD * S].rearrange("p (c s) -> p c s", s=S)
        GROWS = ring[0:L * 3 * KD, RING - 1, 0:P]
        OUTC, OUTF = ACTC[:, KD:2 * KD, :], ACTF[:, 0:KD, :]
        SG = gl(FB * S, 2 * P * T).rearrange("p (t n) -> p t n", t=T)
        HID = gl(FB * S + 2 * P * T, 4 * P * T).rearrange("p (u t n) -> p u t n", u=2, t=T)
        ADAB = prob[:, :, :].rearrange("p a n -> p (a n)").rearrange("p (u n) -> p u n", u=ADA_BUFFERS)
        ASUM = ring[:, 5, 0:3 * D]
        JUNK = [gl(FB * S, D), prob[:, :, :].rearrange("p a n -> p (a n)")[:, 0:D]]
        MINMAX, SUM, RSUM = (soft[:, n, :] for n in range(3))

        QF, KF, VF = (ar(0, 1024).rearrange("p (b s) -> p b s", s=S), ar(1024, 2048).rearrange("p (h s) -> p h s", s=S),
                      [ar(3072 + AW * t, AW) for t in range(T)])
        r5 = lambda a, n: ring[:, 5, a:a + n]
        GATES = [r5(3 * D, D), r5(2 * D, D)]
        QB, KB, VB = (r5(0, 1024).rearrange("p (b s) -> p b s", s=S), r5(1024, 2048).rearrange("p (h s) -> p h s", s=S),
                      [r5(3072 + AW * t, AW) for t in range(T)])
        BIAS_B = gl(0, AH * 3 * P).rearrange("p (h n) -> p h n", h=AH)
        BIAS_F = gl(AH * 3 * P, AH * 3 * P).rearrange("p (h n) -> p h n", h=AH)
        FLIPPED = BIAS_F
        ADAROWS = gl(0, 2 * D)
        WF = sb("WF", [P, KD, AH])
        WR = sb("WR", [P, KD, NE])
        REL = sb("REL", [BUCKETS + 1, AH])
        DIST = gla[0:AH, 2 * D:2 * D + 2 * S]
        badac = sb("badac", [P, 6 * KD])
        gpre = sb("gpre", [P, 2, KD])
        cols = sb("cols", [P, 4, KD])
        brow = sb("brow", [P, NE + AH])
        LF = sb("LF", [P, 3, T, AH])
        XT = ar(0, 1024).rearrange("p (c n) -> p c n", c=KD)
        YP = ar(1024, D)
        WT = ar(2048, S)
        SELG = ar(2304, S).rearrange("p (t e n) -> p t e n", t=T, e=2)
        WG = ar(2560, S).rearrange("p (t e n) -> p t e n", t=T, e=2)
        ATT = [ar(2816 + 512 * n, 512).rearrange("p (h j n) -> p j h n", h=2, n=SLOTS) for n in (0, 1)]
        BZ = [gl(2 * D * n, 2 * D) for n in (0, 1)]
        XG, XL, SIG, ACTV = (gl(4 * D + BANK * n, BANK) for n in range(4))
        BD = prob[0:NE, 0:3, :].rearrange("p a n -> p (a n)")[:, 0:D]
        PARTED = ar(3840, 2 * S).rearrange("p (u s) -> p u s", u=2)
        SLOT_OF, GATE_OF = (gl(6144 + T * LISTED * n, T * LISTED).rearrange("p (t n) -> p t n", t=T) for n in (0, 1))
        RK = gl(6432, T * P).rearrange("p (t n) -> p t n", t=T)
        GATE = gl(6688, T * P).rearrange("p (t n) -> p t n", t=T)
        PERM = gl(6944, LISTED)
        FLAGS, PLACES, NPAIRS = gl(7016, 2), gl(7018, 4), gl(7022, 2)
        PAIRF = gl(7024, MIXED)
        OTHER = gl(7048, LISTED)
        LISTS = 4 + LISTED
        rt = gl(4 * D, T * (5 * NE + 32 + P)).rearrange("p (t n) -> p t n", t=T)
        LOG = lambda t: rt[:, t, 0:NE]
        HOT = lambda t: rt[:, t, NE:5 * NE].rearrange("p (j e) -> p j e", j=TOPK)
        TOP = lambda t: rt[:, t, 5 * NE:5 * NE + 8]
        TOPF = lambda t: rt[:, t, 5 * NE + 8:5 * NE + 8 + TOPK]
        PROBS = lambda t: rt[:, t, 5 * NE + 16:5 * NE + 16 + TOPK]
        TSUM = lambda t, n: rt[:, t, 5 * NE + 24 + n:5 * NE + 25 + n]
        MASK = lambda t: rt[:, t, 5 * NE + 32:5 * NE + 32 + P]
        topi = sb("topi", [P, T, 8], U32)
        items = sb("items", [P, LISTED + 2], I32)
        dist_dram = nc.dram_tensor("dist", (AH, 2 * S), F32, kind="Internal").ap()

        S_ = {}

        def sem(name):
            S_[name] = ctx.enter_context(nc.semaphore(name))
            return S_[name]

        for name in (*PER, *PERG, "gu_chunk"):
            sem(name)
        efull = [sem(f"expert_loaded_{s}") for s in range(RING)]
        bfull = [sem(f"expert_bias_loaded_{s}") for s in range(2)]
        (rel_ready, small_loaded, dist_done, dist_copied, dist_stored, flipped_loaded, flipped_done, bias_b_ready,
         ada_rows_loaded, gates_loaded, gates_biased, gates_ready, cols_ready, kf_zeros, kb_zeros, forget_logits,
         forget_in, forget_step, log_forget, forget_sums, forget_cum, forget_rows, bias_f,
         router_done, top_ready, top_exp, mask_ready, ranks_done, flags_ready, routed, places_done, parted_t, parted, perm_ready, items_done,
         items_ready, bz_zeroed, bd_loaded) = (sem(n) for n in (
             "rel_ready small_loaded dist_done dist_copied dist_stored flipped_loaded flipped_done bias_b_ready "
             "ada_rows_loaded gates_loaded gates_biased gates_ready cols_ready kf_zeros kb_zeros "
             "forget_logits forget_in forget_step log_forget forget_sums forget_cum forget_rows "
             "bias_f router_done top_ready top_exp mask_ready ranks_done flags_ready routed places_done "
             "parted_t parted perm_ready items_done items_ready bz_zeroed bd_loaded").split())
        wfull = [sem(f"weights_loaded_{s}") for s in range(DENSE_SLOTS)]
        afull = [sem(f"ada_loaded_{s}") for s in range(ADA_BUFFERS)]
        ident_loaded, const_loaded, x_loaded, gains_loaded, narrow_loaded = (
            sem(n) for n in ("ident_loaded", "const_loaded", "x_loaded", "gains_loaded", "narrow_loaded"))
        filled = sem("filled")
        gains_t, gains_kept = (sem(n) for n in ("gains_t", "gains_kept"))
        stored = sem("stored")

        def upto(name, l, k):
            return S_[name], l * PER[name] + k

        def pair_(name, G, k):
            return S_[name], G * PERG[name] + k

        def pair_counts(eng):
            eng.wait_ge(items_ready, 1)
            return (eng.value_load(items[0:1, LISTED:LISTED + 1], min_val=1, max_val=MIXED),
                    eng.value_load(items[0:1, LISTED + 1:LISTED + 2], min_val=0, max_val=SAME))

        def chunk_loaded(l, i):
            return wfull[i % DENSE_SLOTS], l * (32 * USES) + 32 * (i // DENSE_SLOTS + 1)

        OUT, GU, DN = len(IN_SPLIT), len(IN_SPLIT) + 1, len(IN_SPLIT) + 1 + GU_CHUNKS

        def split(l, k):
            width = SLOT
            if k < OUT:
                i, to = (IN_SPLIT_2 if l is L else IN_SPLIT)[k], DENSE_SLOTS
            elif k == OUT:
                i, to = IN_CHUNKS + OUT_CHUNKS - 1, DENSE_SLOTS + 1
            else:
                n = k - GU
                i, to = IN_CHUNKS + OUT_CHUNKS + n, DENSE_SLOTS + n % 2
                if k >= DN:
                    width = min(DN_BLOCKS, FB - DN_BLOCKS * (k - DN)) * D
            return i, ring[:, i % DENSE_SLOTS, 0:width], ring_r[:, i % DENSE_SLOTS, 0:width], ring_r[:, to, 0:width]

        def banks(pair):
            return pair[:, :, :].rearrange("p a n -> p (a n)")

        def gate_up_bank(i):
            return PC if i == 0 else (PD, PA)[i % 2]

        def st(row, ev, a, b):
            return stat[:, row, 8 * ev + a:8 * ev + b]

        def of_head(blocks, r):
            return blocks[r * HD:(r + 1) * HD].rearrange("p (a r) s -> p a r s", r=2)[:, :, r, :]

        def attention(h):
            n = h % AH
            q, k, val, bias, pair = (QF, KF, VF, BIAS_F, PC) if h < AH else (QB, KB, VB, BIAS_B, PB)
            return q[:, n // 2, :], k[:, n, :], [x[:, n * HD:(n + 1) * HD] for x in val], bias[:, n, :], pair

        def gain_rows(name, at, n):
            return GROWS[L * at:L * (at + n), :], A[name].rearrange("l (c p) -> (l c) p", p=P)

        block = ctx.enter_context(nc.Block())

        def layer_chunk(l, i):
            w = lambda name: A[name][bass.ds(l, 1), :, :].rearrange("l (c p) n -> p (l c) n", p=P)
            if i < IN_CHUNKS + OUT_CHUNKS:
                name, n = ("w_in", IN_ORDER[i]) if i < IN_CHUNKS else ("w_out", i - IN_CHUNKS)
                src, rows, width = w(name)[:, :, n * BANK:(n + 1) * BANK], KD, BANK
            elif i < IN_CHUNKS + OUT_CHUNKS + GU_CHUNKS:
                n = i - IN_CHUNKS - OUT_CHUNKS
                return [(w(name)[:, :, n * S:(n + 1) * S], h * KD * S, KD, S)
                        for h, name in enumerate(("w_gate", "w_up"))]
            else:
                n = DN_BLOCKS * (i - IN_CHUNKS - OUT_CHUNKS - GU_CHUNKS)
                rows, width = min(DN_BLOCKS, FB - n), D
                src = w("w_down")[:, n:n + rows, :]
                if rows == 1:
                    return [(src[:, :, h * BANK:(h + 1) * BANK], h * BANK, 1, BANK) for h in range(2)]
            h = rows // 2
            return [(src[:, 0:h, :], 0, h, width), (src[:, h:rows, :], h * width, rows - h, width)]

        @block.sync
        def _(sp):
            sp.dma_start(X[:, :, :], A["x"][0].rearrange("(t p) d -> p t d", p=P)).then_inc(x_loaded, 16)
            for name, at, n in GAINS[2:]:
                sp.dma_start(*gain_rows(name, at, n)).then_inc(gains_loaded, 16)
            with sp.Fori(0, L) as l:
                for i in range(CHUNKS):
                    s = i % DENSE_SLOTS
                    if i >= DENSE_SLOTS:
                        sp.wait_ge(*upto(USED[i - DENSE_SLOTS][0], l, USED[i - DENSE_SLOTS][1]))
                    else:
                        sp.wait_ge(*upto("dn_done", l, DN_AT[DN_CHUNKS - DENSE_SLOTS + i]))
                    for src, at, rows, width in layer_chunk(l, i):
                        sp.dma_start(ring[:, s, at:at + rows * width].rearrange("p (c n) -> p c n", n=width),
                                     src).then_inc(wfull[s], 16)
            for i in range(IN_CHUNKS + OUT_CHUNKS):
                s = i % DENSE_SLOTS
                if i >= DENSE_SLOTS:
                    sp.wait_ge(*upto(*USED_2[i - DENSE_SLOTS]))
                else:
                    sp.wait_ge(*upto("dn_done", L, DN_AT[DN_CHUNKS - DENSE_SLOTS + i]))
                name, n = ("w_in_2", IN_ORDER_2[i]) if i < IN_CHUNKS else ("w_out_2", i - IN_CHUNKS)
                src = A[name][0].rearrange("(c p) n -> p c n", p=P)[:, :, n * BANK:(n + 1) * BANK]
                for h in range(2):
                    rows = slice(h * KD // 2, (h + 1) * KD // 2)
                    sp.dma_start(ring[:, s, :].rearrange("p (c n) -> p c n", n=BANK)[:, rows, :], src[:, rows, :]) \
                        .then_inc(wfull[s], 16)

            def load_gate_up(e, x, first, waits, bias_free):
                w = A["w_gate_up_2"][0, bass.ds(e, 1), :, :].rearrange("e (c p) n -> p (e c) n", p=P)
                for c in range(4):
                    load_slot(first + c, w[:, 2 * c:2 * c + 2, :], waits[c])
                    if c == 2:
                        sp.wait_ge(*bias_free)
                        sp.dma_start(BZ[x][0:1, :], A["b_gate_up_2"][0, bass.ds(e, 1), :]).then_inc(bfull[x], 16)

            def load_down(e, q, n, wait):
                w = A["w_down_2"][0, bass.ds(e, 1), :, :].rearrange("e (c p) n -> p (e c) n", p=P)
                load_slot(n, w[:, 4 * q:4 * q + 4, :], wait)

            def load_slot(n, src, wait):
                sp.wait_ge(*wait)
                s, rows = EXPERT_SLOT[n % RING], src.shape[1]
                dst = ring[:, s, :].rearrange("p (c n) -> p c n", c=rows)
                for h in range(2):
                    part = slice(h * rows // 2, (h + 1) * rows // 2)
                    sp.dma_start(dst[:, part, :], src[:, part, :]).then_inc(efull[s], 16)

            def load_mixed(chunks, experts, waits, bias_free):
                waits = waits + [(S_["gu_chunk"], chunks + n + 1) for n in range(RING)]
                for x, e in enumerate(experts):
                    load_gate_up(e, x, 4 * x, waits[4 * x:4 * x + 4], bias_free[x])
                for q in range(2):
                    for x, e in enumerate(experts):
                        load_down(e, q, 8 + 2 * q + x, waits[8 + 2 * q + x])

            load_mixed(0, (0, 1), [upto(*x) for x in FREED_2], [(bz_zeroed, 1)] * 2)
            mixed, same = pair_counts(sp)

            def expert(G, x):
                return sp.value_load(items[0:1, bass.ds(2 * G + x, 1)], min_val=0, max_val=NE - 1)

            def load_next(m, others):
                G, chunks = m + others, m * GU_MIXED + others * GU_SAME
                load_mixed(chunks, [expert(G, x) for x in range(2)],
                           [(S_["gu_chunk"], chunks - 1 + n) for n in range(2)]
                           + [pair_("dn_chunk", G, n // 4 + 1) for n in range(2, RING)], [pair_("gu_ready", G, 0)] * 2)

            with sp.Fori(1, LEAD) as m:
                load_next(m, 0)
            with sp.Fori(0, same) as h:
                G = h + LEAD
                e = expert(G, 0)
                used = [(S_["gu_chunk"], LEAD * GU_MIXED + h * GU_SAME)] * 2 \
                    + [pair_("dn_chunk", G, n // 4 + 1) for n in range(2, RING)]
                load_gate_up(e, 0, 0, used[0:4], pair_("gu_ready", G, 0))
                for q in range(2):
                    load_down(e, q, 4 + q, used[4 + q])
            with sp.Fori(LEAD, mixed) as m:
                load_next(m, same)
            for t in range(T):
                sp.wait_ge(*upto("x_ready", L, T + t + 1))
                sp.dma_start(out[0, t * P:(t + 1) * P, :], X[:, t, :]).then_inc(stored, 16)
            sp.wait_ge(stored, 16 * T)

        @block.gpsimd
        def _(pool):
            steps = [0]

            def inverse_rms(l, ev, a, b, squares, ready):
                pool.wait_ge(*squares)
                nc.gpsimd.tensor_tensor(st(1, ev, a, b), st(0, ev, a, b), eps[:, a:b], ALU.add) \
                    .then_inc(S_["pool_step"], 1)
                steps[0] += 1
                pool.wait_ge(*upto("pool_step", l, steps[0]))
                nc.gpsimd.tensor_tensor(st(2, ev, a, b), st(1, ev, a, b), half[:, a:b], ALU.pow).then_inc(ready, 1)

            def norms(l, n, post, pre):
                for t in range(T):
                    inverse_rms(l, post, t, t + 1, upto("sq_post", l, T * n + t + 1), S_["rstd_post"])
                    if pre is not None:
                        inverse_rms(l, pre, t, t + 1, upto("sq_pre", l, T + T * n + t + 1), S_["rstd_pre"])

            nc.gpsimd.memset(eps[:, :], EPS)
            nc.gpsimd.memset(half[:, :], -0.5).then_inc(filled, 1)
            nc.gpsimd.memset(ones[:, :], 1.0).then_inc(filled, 1)
            pool.wait_ge(filled, 1)
            for t in range(T):
                inverse_rms(0, PRE_MIX, t, t + 1, upto("sq_pre", 0, t + 1), S_["rstd_pre"])
            pool.dma_start(cc[:, 0, :], A["c_2"][0].rearrange("(c p) -> p c", p=P), allow_slow_non_contiguous=True).then_inc(narrow_loaded, 16)
            pool.dma_start(WF[:, :, :], A["w_in_2"][0, :, IN_CHUNKS * BANK:].rearrange("(c p) n -> p c n", p=P)) \
                .then_inc(narrow_loaded, 16)
            pool.dma_start(WR[:, :, :], A["w_router_2"][0].rearrange("(c p) n -> p c n", p=P)).then_inc(narrow_loaded, 16)
            pool.wait_ge(gains_kept, 1)
            with pool.Fori(0, L) as l:
                steps[0] = T
                pool.wait_ge(*upto("ada_cols", l, 1))
                pool.wait_ge(*upto("pre_ready", l, T))
                for _, at, n in GAINS:
                    last = nc.gpsimd.tensor_copy(GC[:, at:at + n], gain_all[:, bass.ds(l * n + L * at, n)])
                last.then_inc(S_["gains_ready"], 1)
                nc.gpsimd.memset(gl(0, 1024), 0.0)
                nc.gpsimd.memset(ar(3072, 2048), 0.0)
                nc.gpsimd.memset(ring[:, 5, 0:3072], 0.0).then_inc(S_["zeros_set"], 1)
                row = lambda name: A[name][bass.ds(l, 1), :]
                pool.dma_start(WLOW[:, :, :], A["w_in"][bass.ds(l, 1), :, IN_CHUNKS * BANK:]
                               .rearrange("l (c p) n -> p (l c) n", p=P)).then_inc(S_["gate_weights"], 16)
                pool.dma_start(WGU[:, :], A["gla_w_gate_up"][bass.ds(l, 1), :, :].rearrange("l r n -> (l r) n")) \
                    .then_inc(S_["gate_weights"], 16)
                pool.dma_start(BGATE[:, :], row("gla_b_gate").rearrange("l (a p) -> p (l a)", p=P),
                               allow_slow_non_contiguous=True) \
                    .then_inc(S_["gate_weights"], 16)
                pool.dma_start(POSTG[:, 0, :], row("mix_post_norm").broadcast_to((P, D))).then_inc(S_["post_gains"], 16)
                pool.dma_start(POSTG[:, 1, :], row("ffn_post_norm").broadcast_to((P, D))).then_inc(S_["post_gains"], 16)
                for n in range(LEVELS):
                    if n == 0:
                        pool.wait_ge(*upto("gqk_ready", l, 1))
                    pool.wait_ge(*upto("gla_decay", l, n + 1))
                    if n >= 2:
                        pool.wait_ge(*upto("gla_scores", l, n))
                    for r in range(2):
                        last = nc.gpsimd.tensor_tensor(of_head(KE[:, n % 2], r), of_head(GKT, r),
                                                       EDEC[r * HD:(r + 1) * HD], ALU.mult)
                    last.then_inc(S_["gla_ke"], 1)
                inverse_rms(l, ATTN, 0, T, upto("sq_attn", l, 1), S_["rstd_attn"])
                inverse_rms(l, GLA, 0, T * GH, upto("sq_gla", l, 1), S_["rstd_gla"])
                norms(l, 0, POST_MIX, PRE_FFN)
                for s in range(ADA_STEPS):
                    j, kc = divmod(s, KD)
                    if s >= ADA_BUFFERS:
                        pool.wait_ge(*upto("ada_used", l, s - ADA_BUFFERS + 1))
                    pool.dma_start(ADAB[:, s % ADA_BUFFERS, :], A["w_ada_2"][0, kc * P:(kc + 1) * P,
                                                                   bass.ds(l * (3 * D) + j * ADA_W, ADA_W)]) \
                        .then_inc(afull[s % ADA_BUFFERS], 16)
                norms(l, 1, POST_FFN, PRE_MIX)
                assert steps[0] == T + PER["pool_step"]
            steps[0] = T
            for n in range(2):
                pool.dma_start(ADAROWS[:, n * D:(n + 1) * D], A["b_ada_2"][0:1, (3 * n + 2) * D:(3 * n + 3) * D]
                               .broadcast_to((P, D))).then_inc(ada_rows_loaded, 16)
            pool.dma_start(POSTG[:, 0, :], A["g_post_mix_2"].broadcast_to((P, D))).then_inc(gates_loaded, 16)
            pool.dma_start(POSTG[:, 1, :], A["g_post_ffn_2"].broadcast_to((P, D))).then_inc(gates_loaded, 16)
            nc.gpsimd.memset(ar(1024, 2048), 0.0).then_inc(kf_zeros, 1)
            pool.wait_ge(dist_copied, 1)
            pool.dma_start(dist_dram, DIST).then_inc(dist_stored, 16)
            pool.wait_ge(dist_stored, 16)
            for t in range(T):
                pool.dma_start(FLIPPED[:, :, t * P:P + 2 * t * P],
                               bass.AP(tensor=dist_dram.tensor, offset=P - P * t, ap=[[1, P], [2 * S, AH], [1, (t + 1) * P]])) \
                    .then_inc(flipped_loaded, 16)
            pool.wait_ge(gates_ready, 1)
            nc.gpsimd.memset(r5(1024, 2048), 0.0).then_inc(kb_zeros, 1)
            pool.wait_ge(*upto("logits", L, 2 * AH))
            for n in range(2):
                last = nc.gpsimd.memset(BZ[n], 0.0)
            last.then_inc(bz_zeroed, 1)
            norms(L, 0, POST_MIX, PRE_FFN)
            pool.wait_ge(*upto("attended", L, 2 * AH))
            pool.dma_start(BD, A["b_down_2"][0]).then_inc(bd_loaded, 16)
            norms(L, 1, POST_FFN, None)

        @block.scalar
        def _(act):
            A_ = nc.scalar.activation
            rest = CONST["ident"][1]
            act.dma_start(K[:, 0:rest], const[:, 0:rest]).then_inc(ident_loaded, 16)
            for name, at, n in GAINS[:2]:
                act.dma_start(*gain_rows(name, at, n)).then_inc(gains_loaded, 16)

            def square(src, t, ev, done):
                A_(JUNK[t], src, ACT.Square, scale=D ** -0.5, accum_out=st(0, ev, t, t + 1)).then_inc(S_[done], 1)

            def norms(l, n, rows_ready, post, pre):
                for t in range(T):
                    act.wait_ge(*rows_ready[t])
                    square(banks((PC, PD)[t]), t, post, "sq_post")
                    if t and n == 0:
                        fill_rows(l, t - 1)
                    if pre is not None:
                        act.wait_ge(*upto("x_ready", l, T * n + t + 1))
                        square(X[:, t, :], t, pre, "sq_pre")

            def fill_rows(l, t):
                act.wait_ge(*upto(("transposed_a", "transposed_b")[t], l, 3))
                for c in range(KD // 2):
                    rows, src = slice(t * P, (t + 1) * P), (PA, PB)[t][:, 0, c * P:(c + 1) * P]
                    if l is not L:
                        last = A_(HTC[:, c, rows], src, ACT.Copy, scale=GC[:, 2 * KD + c:2 * KD + c + 1])
                    else:
                        last = A_(HT[:, c, rows], src, ACT.Identity, scale=cols[:, 2, c:c + 1], bias=cols[:, 3, c:c + 1])
                last.then_inc(S_["ht_act"], 1)

            def fill_ht(l, n, halves=range(2)):
                for half in halves:
                    act.wait_ge(*upto(("transposed_a", "transposed_b")[half], l, n + 1))
                    if half == 0 and l is not L:
                        act.wait_ge(*upto("gains_ready", l, 1))
                    elif half == 0:
                        act.wait_ge(cols_ready, 1)
                    for b in range(2):
                        c, src = 4 * half + b, (PA, PB)[half][:, 0, b * S:(b + 1) * S]
                        if l is not L:
                            last = A_(HT[:, c, :], src, ACT.Copy, scale=GC[:, n * KD + c:n * KD + c + 1])
                        elif n == 1:
                            last = A_(HT[:, c, :], src, ACT.Copy)
                        else:
                            last = A_(HT[:, c, :], src, ACT.Identity, scale=cols[:, n, c:c + 1], bias=cols[:, n + 1, c:c + 1])
                    last.then_inc(S_["ht_act"], 1)

            def coarse(l, k):
                i, w, _, to = split(l, k)
                act.wait_ge(*chunk_loaded(l, i))
                if 0 < k < OUT or k >= GU + 2:
                    name, count = USED[i - 2] if l is not L else USED_2[i - 2][::2]
                    act.wait_ge(*upto(name, l, count))
                A_(to, w, ACT.Copy).then_inc(S_["w_coarse"], 1)

            def rows_coarse(l, n, to):
                act.wait_ge(*upto("ht_act", l, 2 * n + 2))
                act.wait_ge(*upto("ht_dve", l, 2 * n + 2))
                A_(to, HT[:, :, :], ACT.Copy).then_inc(S_["ht_coarse"], 1)

            def hidden_coarse(l, i):
                act.wait_ge(*upto("hidden_t", l, i + 1))
                A_(ACTC[:, 2 * i:2 * i + 2, :].rearrange("p f s -> p (f s)"), PB[:, i % 2, :], ACT.Copy) \
                    .then_inc(S_["hidden_coarse"], 1)

            def softmax_exp(h, e, at):
                for t in range(T):
                    part = e[:, 0:P] if t == 0 else e[:, P:3 * P]
                    last = A_(part, part, ACT.Exp, scale=-1.0, bias=MINMAX[:, at + t * AH:at + t * AH + 1],
                              accum_out=SUM[:, at + t * AH:at + t * AH + 1])
                last.then_inc(S_["probs"], 1)

            def decay(l, n):
                act.wait_ge(*upto("gla_diff", l, n + 1))
                A_(DIFF[:, :, :], DIFF[:, :, :], ACT.Abs).then_inc(S_["gla_abs"], 1)
                act.wait_ge(*upto("gla_abs", l, n + 1))
                if n:
                    act.wait_ge(*upto("gla_qe", l, n))
                    act.wait_ge(*upto("gla_ke", l, n))
                A_(EDEC[:, :, :], DIFF[:, :, :], ACT.Exp, scale=-1.0 / TAU).then_inc(S_["gla_decay"], 1)

            act.wait_ge(x_loaded, 16)
            for t in range(T):
                square(X[:, t, :], t, PRE_MIX, "sq_pre")
            act.dma_start(K[:, rest:], const[:, rest:]).then_inc(const_loaded, 16)
            act.dma_start(REL[0:BUCKETS, :], A["rel_bias_2"]).then_inc(rel_ready, 16)
            act.dma_start(badac[:, :], A["b_ada_2"][0].rearrange("(c p) -> p c", p=P), allow_slow_non_contiguous=True) \
                .then_inc(small_loaded, 16)
            for n, name in enumerate(("g_pre_mix_2", "g_pre_ffn_2")):
                act.dma_start(gpre[:, n, :], A[name][0].rearrange("(c p) -> p c", p=P), allow_slow_non_contiguous=True) \
                    .then_inc(small_loaded, 16)
            act.dma_start(brow[:, 0:NE], A["b_router_2"].broadcast_to((P, NE))).then_inc(small_loaded, 16)
            act.dma_start(brow[:, NE:NE + AH], A["b_forget_2"].broadcast_to((P, AH))).then_inc(small_loaded, 16)
            with act.Fori(0, L) as l:
                fill_ht(l, 0)
                rows_coarse(l, 0, INC)
                coarse(l, 0)
                act.wait_ge(*upto("q_proj", l, 1))
                A_(QRAW.rearrange("p b s -> p (b s)"), banks(PC), ACT.Copy).then_inc(S_["q_raw"], 1)
                act.wait_ge(*upto("v_proj", l, 1))
                for t in range(T):
                    last = A_(V[t], PD[:, t, :], ACT.Copy)
                last.then_inc(S_["v_ready"], 1)
                coarse(l, 1)
                act.wait_ge(*upto("k_proj", l, 1))
                A_(KRAW.rearrange("p b s -> p (b s)"), banks(PA), ACT.Copy).then_inc(S_["k_raw"], 1)
                act.wait_ge(*upto("gv_proj", l, 1))
                A_(GV, PC[:, :, :], ACT.Copy).then_inc(S_["gv_ready"], 1)
                act.wait_ge(*upto("z_proj", l, 1))
                act.wait_ge(*upto("gate_weights", l, 48))
                for a in range(2):
                    last = A_(DIFF[:, a, :], PA[:, 1, a * S:(a + 1) * S], ACT.Abs, bias=BGATE[:, a:a + 1])
                last.then_inc(S_["z_step"], 1)
                act.wait_ge(*upto("z_step", l, 1))
                A_(DIFF[:, :, :], DIFF[:, :, :], ACT.Exp, scale=-1.0).then_inc(S_["z_step"], 1)
                act.wait_ge(*upto("z_step", l, 2))
                A_(DIFF[:, :, :], DIFF[:, :, :], ACT.Ln, bias=1.0).then_inc(S_["z_step"], 1)
                coarse(l, 2)
                decay(l, 0)
                act.wait_ge(*upto("gqk_proj", l, 1))
                A_(GQ.rearrange("p a s -> p (a s)"), PB[:, 0, :], ACT.Copy, scale=SCALE)
                act.wait_ge(*upto("zeros_set", l, 1))
                for r in range(2):
                    last = A_(of_head(GKT, r), PB[r * HD:(r + 1) * HD, 1, :].rearrange("p (a s) -> p a s", s=S), ACT.Copy)
                last.then_inc(S_["gqk_ready"], 1)
                act.wait_ge(*upto("gr_proj", l, 1))
                A_(GRS, PC[:, :, :], ACT.Silu).then_inc(S_["gr_ready"], 1)
                for h in range(AH):
                    act.wait_ge(*upto("logits", l, h + 1))
                    softmax_exp(h, prob[:, h % 2, :], h)
                    if h + 1 < LEVELS:
                        decay(l, h + 1)
                    act.wait_ge(*upto("probs_t", l, h + 1))
                    if h >= 2:
                        act.wait_ge(*upto("attended", l, h - 1))
                    A_(prob[:, 2 + h % 2, :], PA[:, h % 2, 0:3 * P], ACT.Copy).then_inc(S_["probs_ready"], 1)
                act.wait_ge(*upto("attn_out", l, 1))
                for t in range(T):
                    last = A_(ar(AW * t, AW), XN[:, t, 0:AW], ACT.Square, scale=AW ** -0.5, accum_out=st(0, ATTN, t, t + 1))
                last.then_inc(S_["sq_attn"], 1)
                act.wait_ge(*upto("gla_done", l, 1))
                A_(ar(1024, 1024), banks(PD), ACT.Square, scale=GDV ** -0.5).then_inc(S_["gla_square"], 1)
                fill_ht(l, 1, (0,))
                coarse(l, OUT)
                coarse(l, GU)
                fill_ht(l, 1, (1,))
                rows_coarse(l, 1, OUTC)
                norms(l, 0, [upto("mix_done", l, n) for n in MIX_TILE], POST_MIX, PRE_FFN)
                coarse(l, GU + 1)
                fill_rows(l, T - 1)
                act.wait_ge(narrow_loaded, 48)
                A_(cc[:, 1, :], cc[:, 0, :], ACT.Silu).then_inc(S_["c_silu"], 1)
                for i in range(GU_CHUNKS):
                    act.wait_ge(*upto("gu_done", l, i + 1))
                    if i:
                        act.wait_ge(*upto("act_done", l, i))
                    A_(SG, gate_up_bank(i)[:, :, 0:S], ACT.Silu).then_inc(S_["silu_done"], 1)
                    if i:
                        hidden_coarse(l, i - 1)
                    coarse(l, GU + i + 2)
                hidden_coarse(l, GU_CHUNKS - 1)
                for k in range(DN + 2, DN + DN_CHUNKS):
                    coarse(l, k)
                norms(l, 1, [upto("dn_done", l, PER["dn_done"] + n) for n in DN_TILE], POST_FFN, PRE_MIX)
                act.wait_ge(*upto("ada_mod", l, 2))
                A_(modc[:, bass.ds(l, 1), :], PC[:, 0:1, 0:2 * KD], ACT.Copy).then_inc(S_["ada_cols"], 1)

            fill_ht(L, 0)
            rows_coarse(L, 0, INC)
            coarse(L, 0)

            def take(pair, done, n, q, k, val, zeros):
                if q is not None:
                    act.wait_ge(*upto("q_proj", L, n))
                    A_(q.rearrange("p b s -> p (b s)"), banks(pair), ACT.Copy, scale=-SCALE).then_inc(S_["q_ready"], 1)
                elif k is not None:
                    act.wait_ge(*upto("k_proj", L, n))
                    act.wait_ge(zeros, 1)
                    for r in range(2):
                        last = A_(of_head(k, r), banks(pair)[r * HD:(r + 1) * HD].rearrange("p (b s) -> p b s", s=S), ACT.Copy)
                    last.then_inc(S_["k_ready"], 1)
                else:
                    act.wait_ge(*upto("v_proj", L, n))
                    for t in range(T):
                        last = A_(val[t], pair[:, t, :], ACT.Copy)
                    last.then_inc(S_["v_ready"], 1)

            def take_flipped(n):
                act.wait_ge(flipped_done, n + 1)
                act.wait_ge(gates_biased, 1)
                A_(BIAS_B.rearrange("p h n -> p (h n)")[:, n * D:(n + 1) * D], banks(PD), ACT.Copy).then_inc(bias_b_ready, 1)

            take(PC, "q_proj", 1, QF, None, None, None)
            act.wait_ge(forget_in, 1)
            A_(LF[:, 1], LF[:, 0], ACT.Abs).then_inc(forget_step, 1)
            act.wait_ge(forget_step, 1)
            A_(LF[:, 1], LF[:, 1], ACT.Exp, scale=-1.0).then_inc(forget_step, 1)
            act.wait_ge(forget_step, 2)
            A_(LF[:, 1], LF[:, 1], ACT.Ln, bias=1.0).then_inc(forget_step, 1)
            act.wait_ge(dist_done, 1)
            A_(DIST, PD[0:AH, 0, :], ACT.Copy).then_inc(dist_copied, 1)
            take(PA, "k_proj", 1, None, KF, None, kf_zeros)
            take_flipped(0)
            take(PC, "v_proj", 1, None, None, VF, None)
            coarse(L, 1)
            take_flipped(1)
            act.wait_ge(gates_ready, 1)
            take(PA, "q_proj", 2, QB, None, None, None)
            take_flipped(2)
            take(PC, "v_proj", 2, None, None, VB, None)
            take(PA, "k_proj", 2, None, KB, None, kb_zeros)
            for h in range(2 * AH):
                act.wait_ge(*upto("logits", L, h + 1))
                softmax_exp(h, prob[:, h % 2, :], (h // AH) * T * AH + h % AH)
                act.wait_ge(*upto("probs_t", L, h + 1))
                if h >= 2:
                    act.wait_ge(*upto("attended", L, h - 1))
                A_(prob[:, 2 + h % 2, :], PA[:, h % 2, 0:3 * P], ACT.Copy).then_inc(S_["probs_ready"], 1)
            fill_ht(L, 1)
            norms(L, 0, [upto("mix_done", L, n) for n in MIX_TILE], POST_MIX, PRE_FFN)
            fill_rows(L, T - 1)
            act.wait_ge(top_ready, 1)
            for t in range(T):
                last = A_(PROBS(t), TOP(t)[:, 0:TOPK], ACT.Exp, bias=TSUM(t, 0), accum_out=TSUM(t, 1))
            last.then_inc(top_exp, 1)
            act.wait_ge(parted_t, 1)
            A_(PARTED.rearrange("p u s -> p (u s)"), PB[:, 1, :], ACT.Copy).then_inc(parted, 1)

            def take_rows(G):
                act.wait_ge(*pair_("gathered", G, 1))
                for c in range(KD // 2):
                    last = A_(XT[:, c, :], PA[:, 0, c * P:(c + 1) * P], ACT.Identity, scale=cols[:, 2, c:c + 1],
                              bias=cols[:, 3, c:c + 1])
                last.then_inc(S_["xt_act"], 1)

            take_rows(0)
            mixed, same = pair_counts(act)
            with act.Fori(0, mixed + same) as G:
                act.wait_ge(*pair_("wt_t", G, 1))
                A_(WT, PA[:, 0, 0:S], ACT.Copy).then_inc(S_["wt_ready"], 1)
                for x in range(2):
                    act.wait_ge(*pair_("clipped", G, x + 1))
                    A_(SIG, XG, ACT.Sigmoid, scale=ALPHA).then_inc(S_["sig_ready"], 1)
                for x in range(2):
                    act.wait_ge(*pair_("act_t", G, x + 1))
                    A_(ATT[x], PB[:, x, :].rearrange("p (j h n) -> p j h n", j=4, n=SLOTS), ACT.Copy) \
                        .then_inc(S_["att_ready"], 1)
                take_rows(G + 1)
                act.wait_ge(*pair_("dn_chunk", G, 2 + DN_CREDIT))
                A_(YP[:, 0:BANK], PB[:, 0, :], ACT.Copy).then_inc(S_["yp_act"], 1)
            norms(L, 1, [pair_("combined", mixed + same, t + 1) for t in range(T)], POST_FFN, None)

        @block.vector
        def _(dve):
            v = nc.vector
            steps = [0]

            def then(l, ins):
                ins.then_inc(S_["dve_step"], 1)
                steps[0] += 1
                dve.wait_ge(*upto("dve_step", l, steps[0]))

            def normed(l, n, ev, t):
                dve.wait_ge(*upto("rstd_pre", l, T * n + t + 1))
                v.tensor_scalar(XN[:, t, :], X[:, t, :], st(2, ev, t, t + 1), None, ALU.mult).then_inc(S_["pre_ready"], 1)

            def fill_rows(l, t):
                dve.wait_ge(*upto(("transposed_a", "transposed_b")[t], l, 3))
                for c in range(KD // 2, KD):
                    rows, src = slice(t * P, (t + 1) * P), (PA, PB)[t][:, 1, (c - KD // 2) * P:(c - KD // 2 + 1) * P]
                    if l is not L:
                        last = v.tensor_scalar(HTC[:, c, rows], src, GC[:, 2 * KD + c:2 * KD + c + 1], None, ALU.mult)
                    else:
                        last = v.tensor_scalar(HT[:, c, rows], src, cols[:, 2, c:c + 1], cols[:, 3, c:c + 1], ALU.mult, ALU.add)
                last.then_inc(S_["ht_dve"], 1)

            def fill_fine(l, t):
                dve.wait_ge(*upto("ht_dve", l, 4 + t + 1))
                dve.wait_ge(*upto("ht_act", l, 4 + t + 1))
                for c in range(KD):
                    at = slice((c % 4) * P, (c % 4 + 1) * P)
                    last = v.scalar_tensor_tensor(HTF[:, t, c, :], (PA, PB)[t][:, c // 4, at],
                                                  GC[:, 2 * KD + c:2 * KD + c + 1], HTC[:, c, t * P:(t + 1) * P],
                                                  ALU.mult, ALU.subtract)
                last.then_inc(S_["ht_fine"], 1)

            def residual(l, n, post, pre):
                for t in range(T):
                    if t == 0 and l is not L:
                        dve.wait_ge(*upto("post_gains", l, 32))
                    dve.wait_ge(*upto("sq_post", l, T * n + t + 1))
                    then(l, v.tensor_tensor(XN[:, t, :], banks((PC, PD)[t]), POSTG[:, n, :], ALU.mult))
                    behind = t and n == 0
                    if behind:
                        fill_rows(l, t - 1)
                    dve.wait_ge(*upto("rstd_post", l, T * n + t + 1))
                    v.scalar_tensor_tensor(X[:, t, :], XN[:, t, :], st(2, post, t, t + 1), X[:, t, :], ALU.mult, ALU.add) \
                        .then_inc(S_["x_ready"], 1)
                    if behind and l is not L:
                        fill_fine(l, t - 1)
                    if pre is not None:
                        normed(l, n + 1, pre, t)

            def fill_ht(l, n, halves=range(2)):
                for half in halves:
                    dve.wait_ge(*upto(("transposed_a", "transposed_b")[half], l, n + 1))
                    if half == 0 and l is not L:
                        dve.wait_ge(*upto("gains_ready", l, 1))
                    for b in range(2):
                        c, src = 4 * half + 2 + b, (PA, PB)[half][:, 1, b * S:(b + 1) * S]
                        if l is not L:
                            last = v.tensor_scalar(HT[:, c, :], src, GC[:, n * KD + c:n * KD + c + 1],
                                                   None, ALU.mult)
                        elif n == 1:
                            last = v.tensor_copy(HT[:, c, :], src)
                        else:
                            last = v.tensor_scalar(HT[:, c, :], src, cols[:, n, c:c + 1], cols[:, n + 1, c:c + 1],
                                                   ALU.mult, ALU.add)
                    last.then_inc(S_["ht_dve"], 1)

            def rows_fine(l, n, rest, rounding):
                dve.wait_ge(*upto("ht_coarse", l, n + 1))
                v.tensor_tensor(rest, HT[:, :, :], rounding, ALU.subtract).then_inc(S_["ht_fine"], 1)

            def fine(l, k):
                _, w, rest, rounding = split(l, k)
                dve.wait_ge(*upto("w_coarse", l, k + 1))
                v.tensor_tensor(rest, w, rounding, ALU.subtract).then_inc(S_["w_fine"], 1)

            def modulation(l, some):
                for s in some:
                    j, kc = divmod(s, KD)
                    acc, w = ASUM[:, j * ADA_W:(j + 1) * ADA_W], ADAB[:, s % ADA_BUFFERS, :]
                    dve.wait_ge(afull[s % ADA_BUFFERS], l * (16 * ADA_STEPS // ADA_BUFFERS) + 16 * (s // ADA_BUFFERS + 1))
                    if kc == 0:
                        ins = v.tensor_scalar(acc, w, cc[:, 1, kc:kc + 1], None, ALU.mult)
                    else:
                        dve.wait_ge(*upto("ada_used", l, s))
                        ins = v.scalar_tensor_tensor(acc, w, cc[:, 1, kc:kc + 1], acc, ALU.mult, ALU.add)
                    ins.then_inc(S_["ada_used"], 1)

            def hidden_fine(l, i):
                dve.wait_ge(*upto("hidden_coarse", l, i + 1))
                two = slice(2 * i, 2 * i + 2)
                v.tensor_tensor(ACTF[:, two, :].rearrange("p f s -> p (f s)"), PB[:, i % 2, :], ACTC[:, two, :].rearrange("p f s -> p (f s)"),
                                ALU.subtract).then_inc(S_["hidden_fine"], 1)

            def rope(l, raw, rot, cos, sin, tmp, add, ready):
                dve.wait_ge(const_loaded, 16)
                dve.wait_ge(*upto(ready[0] + "_raw", l, 1))
                v.tensor_tensor(tmp, raw, times(k_(cos), 1, 4), ALU.mult).then_inc(S_["dve_step"], 1)
                steps[0] += 1
                dve.wait_ge(*upto(ready[0] + "_rot", l, 1))
                dve.wait_ge(*upto("dve_step", l, steps[0]))
                then(l, v.tensor_tensor(raw, banks(rot).rearrange("p (b s) -> p b s", s=S), times(k_(sin), 1, 4),
                                        ALU.mult))
                add().then_inc(S_[ready], 1)

            def add_q():
                return v.tensor_tensor(QT, QT, QRAW, ALU.add)

            def add_k():
                for r in range(2):
                    rows = slice(r * HD, (r + 1) * HD)
                    last = v.tensor_tensor(of_head(KT, r), QRAW[rows], KRAW[rows], ALU.add)
                return last

            def logits(l, h, bias, at):
                dve.wait_ge(*upto("scores", l, h + 1))
                if h >= 2:
                    dve.wait_ge(*upto("probs_t", l, h - 1))
                v.memset(wait_col[:, h % 2:h % 2 + 1], 0.0)
                e = prob[:, h % 2, :]
                for t in range(T):
                    part = slice(0, P) if t == 0 else slice(P, 3 * P)
                    last = v.tensor_tensor_reduce(out=e[:, part], in0=PD[:, h % 2, part], in1=bias[:, part], scale=1.0,
                                                  scalar=3.0e38, op0=ALU.add, op1=ALU.min,
                                                  accum_out=MINMAX[:, at + t * AH:at + t * AH + 1])
                last.then_inc(S_["logits"], 1)

            def attended(l, at, pair, to):
                then(l, v.reciprocal(RSUM[:, at:at + T * AH], SUM[:, at:at + T * AH]))
                for t in range(T):
                    last = v.tensor_tensor(XN[:, t, to:to + AW].rearrange("p (h d) -> p h d", d=HD),
                                           pair[:, t, :].rearrange("p (h d) -> p h d", d=HD),
                                           times(RSUM[:, at + t * AH:at + (t + 1) * AH], 2, HD), ALU.mult)
                return last

            def difference(l, n):
                b = 2 << n
                view = GB.rearrange("p a s -> p (a s)").rearrange("p (m b) -> p m b", b=b)
                if n:
                    dve.wait_ge(*upto("gla_decay", l, n))
                v.tensor_tensor(DIFF.rearrange("p a s -> p (a s)").rearrange("p (m b) -> p m b", b=b), view,
                                view[:, :, b // 2 - 1:b // 2].broadcast_to(tuple(view.shape)), ALU.subtract) \
                    .then_inc(S_["gla_diff"], 1)

            def scaled_q(l, n):
                dve.wait_ge(*upto("gla_decay", l, n + 1))
                if n == 0:
                    dve.wait_ge(*upto("gqk_ready", l, 1))
                if n >= 2:
                    dve.wait_ge(*upto("gla_scores", l, n))
                v.tensor_tensor(QE[:, n % 2], GQ, EDEC, ALU.mult).then_inc(S_["gla_qe"], 1)

            def merge(l, n):
                dve.wait_ge(*upto("gla_scores", l, n + 2))
                v.memset(wait_col[:, 2:3], 0.0)
                if n == LEVELS - 1:
                    last = v.tensor_copy(ACROSS, PB[:, 0, :].rearrange("p (h n) -> p h n", h=GH))
                else:
                    m = k_("level")[:, (n % LEVELS) * P:(n % LEVELS + 1) * P].bitcast(U32)
                    for t in range(T):
                        last = v.copy_predicated(MERGED[:, t], times(m, 1, GH),
                                                 PB[:, t, :].rearrange("p (h n) -> p h n", h=GH))
                last.then_inc(S_["gla_merged"], 1)

            v.memset(REL[BUCKETS:BUCKETS + 1, :], 1.0).then_inc(rel_ready, 1)
            v.memset(soft[:, :, :], 0.0)
            dve.wait_ge(gains_t, 1)
            v.tensor_copy(gain_all[:, :], PD[:, 0, 0:L * 3 * KD]).then_inc(gains_kept, 1)
            dve.wait_ge(x_loaded, 16)
            for t in range(T):
                normed(0, 0, PRE_MIX, t)
            dve.wait_ge(filled, 2)
            with dve.Fori(0, L) as l:
                steps[0] = 0
                fill_ht(l, 0)
                rows_fine(l, 0, INF, INC)
                fine(l, 0)
                rope(l, QRAW, PB, "cos_q", "sin_q", QT, add_q, "q_ready")
                fine(l, 1)
                dve.wait_ge(*upto("low_proj", l, 1))
                v.tensor_copy(LOW[:, :], PA[0:GR, 0, 0:S]).then_inc(S_["low_ready"], 1)
                dve.wait_ge(*upto("q_ready", l, 1))
                dve.wait_ge(*upto("zeros_set", l, 1))
                rope(l, KRAW, PD, "cos_k", "sin_k", QRAW, add_k, "k_ready")
                dve.wait_ge(*upto("z_step", l, 1))
                dve.wait_ge(*upto("gate_weights", l, 48))
                for a in range(2):
                    last = v.tensor_scalar(LA[:, a, :], PA[:, 1, a * S:(a + 1) * S], BGATE[:, a:a + 1], 0.0,
                                           ALU.add, ALU.min)
                then(l, last)
                dve.wait_ge(*upto("z_step", l, 3))
                then(l, v.tensor_tensor(LA, LA, DIFF, ALU.subtract))
                for a in range(2):
                    last = v.tensor_tensor_scan(GB[:, a, :], ones[:, 0:1].broadcast_to((P, S)),
                                                LA[:, a, :], 0.0, ALU.mult, ALU.add)
                last.then_inc(S_["decay_sum"], 1)
                dve.wait_ge(*upto("decay_sum", l, 1))
                difference(l, 0)
                fine(l, 2)
                scaled_q(l, 0)
                merge(l, -1)
                for h in range(AH):
                    logits(l, h, k_("dilated"), h)
                    n = h
                    if n:
                        scaled_q(l, n)
                    if n + 1 < LEVELS:
                        difference(l, n + 1)
                    if n:
                        merge(l, n - 1)
                merge(l, LEVELS - 1)
                dve.wait_ge(*upto("attended", l, AH))
                attended(l, 0, PC, 0).then_inc(S_["attn_out"], 1)
                dve.wait_ge(*upto("rstd_attn", l, 1))
                dve.wait_ge(*upto("attn_out", l, 1))
                for t in range(T):
                    last = v.tensor_scalar(XN[:, t, 0:AW], XN[:, t, 0:AW], st(2, ATTN, t, t + 1), None, ALU.mult)
                last.then_inc(S_["mixed_ready"], 1)
                dve.wait_ge(*upto("gla_square", l, 1))
                v.tensor_reduce(st(0, GLA, 0, T * GH), ar(1024, 1024).rearrange("p (g n) -> p g n", n=GDV), X_AXIS,
                                ALU.add).then_inc(S_["sq_gla"], 1)
                dve.wait_ge(*upto("gr_ready", l, 1))
                for t in range(T):
                    last = v.tensor_tensor(XN[:, t, AW:D], PD[:, t, :], GRS[:, t, :], ALU.mult)
                then(l, last)
                fill_ht(l, 1, (0,))
                dve.wait_ge(*upto("rstd_gla", l, 1))
                for t in range(T):
                    w = XN[:, t, AW:D].rearrange("p (h n) -> p h n", n=GDV)
                    last = v.tensor_tensor(w, w, times(st(2, GLA, t * GH, (t + 1) * GH), 2, GDV), ALU.mult)
                last.then_inc(S_["mixed_ready"], 1)
                fine(l, OUT)
                fill_ht(l, 1, (1,))
                rows_fine(l, 1, OUTF, OUTC)
                fine(l, GU)
                residual(l, 0, POST_MIX, PRE_FFN)
                fill_rows(l, T - 1)
                fill_fine(l, T - 1)
                fine(l, GU + 1)
                dve.wait_ge(*upto("c_silu", l, 1))
                for i in range(GU_CHUNKS):
                    dve.wait_ge(*upto("silu_done", l, i + 1))
                    if i >= 2:
                        dve.wait_ge(*upto("hidden_t", l, i - 1))
                    v.tensor_tensor(HID[:, i % 2], SG, gate_up_bank(i)[:, :, S:2 * S], ALU.mult).then_inc(S_["act_done"], 1)
                    if i:
                        hidden_fine(l, i - 1)
                    fine(l, GU + i + 2)
                    modulation(l, range(ADA_STEPS)[ADA_BUFFERS * i:ADA_BUFFERS * (i + 1)])
                hidden_fine(l, GU_CHUNKS - 1)
                for i in range(GU_CHUNKS, GU_CHUNKS + DN_CHUNKS - 2):
                    fine(l, GU + i + 2)
                    modulation(l, range(ADA_STEPS)[ADA_BUFFERS * i:ADA_BUFFERS * (i + 1)])
                dve.wait_ge(*upto("ada_mod", l, 1))
                v.tensor_copy(ring[:, 5, bass.ds(3 * D - l * D, D)], banks(PA)).then_inc(S_["ada_rows"], 1)
                residual(l, 1, POST_FFN, PRE_MIX)
                assert steps[0] == PER["dve_step"], steps
            steps[0] = 0
            dve.wait_ge(small_loaded, 16 * 5)
            dve.wait_ge(*upto("ada_cols", L, 1))
            dve.wait_ge(*upto("ada_rows", L, 0))
            for n in range(2):
                for m in range(2):
                    last = v.tensor_tensor(modc[:, n, m * KD:(m + 1) * KD], modc[:, n, m * KD:(m + 1) * KD],
                                           badac[:, (3 * n + m) * KD:(3 * n + m + 1) * KD], ALU.add)
            then(L, last)
            for n in range(2):
                v.scalar_tensor_tensor(cols[:, 2 * n, :], modc[:, n, KD:2 * KD], 1.0, gpre[:, n, :], ALU.add, ALU.mult)
                last = v.tensor_copy(cols[:, 2 * n + 1, :], modc[:, n, 0:KD])
            last.then_inc(cols_ready, 1)
            dve.wait_ge(cols_ready, 1)
            fill_ht(L, 0)
            rows_fine(L, 0, INF, INC)
            dve.wait_ge(ada_rows_loaded, 32)
            for n in range(2):
                last = v.tensor_tensor(GATES[n], GATES[n], ADAROWS[:, n * D:(n + 1) * D], ALU.add)
            last.then_inc(gates_biased, 1)
            dve.wait_ge(gates_biased, 1)
            dve.wait_ge(gates_loaded, 32)
            for n in range(2):
                last = v.tensor_tensor(POSTG[:, n, :], POSTG[:, n, :], GATES[n], ALU.mult)
            last.then_inc(gates_ready, 1)
            fine(L, 0)
            dve.wait_ge(forget_logits, 1)
            v.tensor_tensor(LF[:, 0], PB[:, 0, 0:T * AH].rearrange("p (t h) -> p t h", t=T),
                            times(brow[:, NE:NE + AH], 1, T), ALU.add).then_inc(forget_in, 1)
            dve.wait_ge(forget_step, 3)
            then(L, v.tensor_scalar(LF[:, 0], LF[:, 0], 0.0, None, ALU.min))
            v.tensor_tensor(LF[:, 0], LF[:, 0], LF[:, 1], ALU.subtract).then_inc(log_forget, 1)
            dve.wait_ge(forget_sums, 1)
            v.tensor_copy(LF[:, 2], PB[:, 0, 0:T * AH].rearrange("p (t h) -> p t h", t=T)).then_inc(forget_cum, 1)
            dve.wait_ge(forget_cum, 1)
            fine(L, 1)
            for h in range(AH):
                if h == 0:
                    dve.wait_ge(flipped_done, 3)
                dve.wait_ge(forget_rows, h // 4 + 1)
                row = (PD, PB)[h // 4][:, h % 4 // 2, (h % 2) * S:(h % 2 + 1) * S]
                for t in range(T):
                    part = slice(0, P) if t == 0 else slice(P, 3 * P)
                    last = v.scalar_tensor_tensor(BIAS_F[:, h, part], row[:, 0:(t + 1) * P], LF[:, 2, t, h:h + 1],
                                                  k_("causal")[:, part], ALU.subtract, ALU.add)
                if h % 4 == 3:
                    last.then_inc(bias_f, 1)
            dve.wait_ge(bias_f, 2)
            for h in range(2 * AH):
                logits(L, h, attention(h)[3], (h // AH) * T * AH + h % AH)
                if h == AH + 1:
                    dve.wait_ge(*upto("attended", L, AH))
                    attended(L, 0, PC, 0).then_inc(S_["mixed_ready"], 1)
            dve.wait_ge(*upto("attended", L, 2 * AH))
            attended(L, T * AH, PB, AW).then_inc(S_["mixed_ready"], 1)
            fill_ht(L, 1)
            residual(L, 0, POST_MIX, PRE_FFN)
            fill_rows(L, T - 1)
            def select(G, slot_of, gate_of):
                for t in range(T):
                    last = v.tensor_tensor(SELG[:, t], times(k_("iota")[:, 1:1 + SLOTS], 1, 2),
                                           times(slot_of(t), 2, SLOTS), ALU.is_equal)
                last.then_inc(S_["selected"], 1)
                dve.wait_ge(*pair_("selected", G, 1))
                for t in range(T):
                    last = v.tensor_tensor(WG[:, t], SELG[:, t], times(gate_of(t), 2, SLOTS), ALU.mult)
                last.then_inc(S_["sel_ready"], 1)

            dve.wait_ge(router_done, 1)
            for t in range(T):
                last = v.tensor_tensor(LOG(t), PA[:, 0, t * NE:(t + 1) * NE], brow[:, 0:NE], ALU.add)
            then(L, last)
            for t in range(T):
                last = v.max(TOP(t), LOG(t))
            then(L, last)
            for t in range(T):
                v.tensor_scalar(TSUM(t, 0), TOP(t)[:, 0:1], -1.0, None, ALU.mult)
                last = v.max_index(topi[:, t, :], TOP(t), LOG(t))
            last.then_inc(top_ready, 1)
            dve.wait_ge(top_ready, 1)
            for t in range(T):
                last = v.tensor_copy(TOPF(t), topi[:, t, 0:TOPK])
            then(L, last)
            for t in range(T):
                last = v.tensor_tensor(HOT(t), times(k_("iota")[:, 0:NE], 1, TOPK), times(TOPF(t), 2, NE), ALU.is_equal)
            then(L, last)
            for t in range(T):
                last = v.tensor_reduce(MASK(t).rearrange("p (r e) -> p r e", e=NE),
                                       times(HOT(t).rearrange("p j e -> p e j"), 1, PARTS), X_AXIS, ALU.add)
            last.then_inc(mask_ready, 1)
            dve.wait_ge(mask_ready, 1)
            dve.wait_ge(top_exp, 1)
            for t in range(T):
                last = v.reciprocal(TSUM(t, 2), TSUM(t, 1))
            then(L, last)
            for t in range(T):
                last = v.tensor_scalar(PROBS(t), PROBS(t), TSUM(t, 2), None, ALU.mult)
            then(L, last)
            for t in range(T):
                last = v.tensor_tensor(HOT(t), HOT(t), times(PROBS(t), 2, NE), ALU.mult)
            then(L, last)
            for t in range(T):
                last = v.tensor_reduce(GATE[:, t, :].rearrange("p (r e) -> p r e", e=NE),
                                       times(HOT(t).rearrange("p j e -> p e j"), 1, PARTS), X_AXIS, ALU.add)
            then(L, last)
            dve.wait_ge(ranks_done, 1)
            count = PA[:, 0, 2 * NE:2 * NE + 1]
            then(L, v.tensor_tensor(OTHER[:, 0:1], count, k_("upto_full"), ALU.is_le))
            v.scalar_tensor_tensor(FLAGS[:, 0:1], count, k_("over"), OTHER[:, 0:1], ALU.is_gt, ALU.mult)
            v.tensor_tensor(FLAGS[:, 1:2], count, k_("over_full"), ALU.is_gt).then_inc(flags_ready, 1)
            for t in range(T):
                last = v.scalar_tensor_tensor(RK[:, t, 0:NE], PA[:, 0, t * NE:(t + 1) * NE], 1.0, MASK(t)[:, 0:NE], ALU.add, ALU.mult)
            then(L, last)
            for t in range(T):
                for r in range(1, PARTS):
                    last = v.tensor_scalar(RK[:, t, r * NE:(r + 1) * NE], RK[:, t, 0:NE], float(-r * SLOTS), None, ALU.add)
            last.then_inc(routed, 1)
            dve.wait_ge(routed, 1)
            select(0, lambda t: RK[:, t, 0:2], lambda t: GATE[:, t, 0:2])
            dve.wait_ge(places_done, 1)
            then(L, v.tensor_copy(PLACES, PB[:, 0, 0:4]))
            v.tensor_tensor(PLACES[:, 1:2], PLACES[:, 1:2], k_("odd"), ALU.add)
            then(L, v.tensor_scalar(OTHER[:, 0:1], PLACES[:, 0:1], 2.0 * LEAD, PLACES[:, 3:4], ALU.is_ge, ALU.mult))
            then(L, v.tensor_tensor(PLACES[:, 0:1], PLACES[:, 0:1], OTHER[:, 0:1], ALU.add))
            v.tensor_scalar(PERM, k_("iota"), PLACES[:, 0:1], FLAGS[:, 0:1], ALU.is_equal, ALU.mult)
            then(L, v.tensor_scalar(OTHER, k_("iota"), PLACES[:, 1:2], FLAGS[:, 1:2], ALU.is_equal, ALU.mult))
            v.tensor_tensor(PERM, PERM, OTHER, ALU.add).then_inc(perm_ready, 1)
            then(L, v.tensor_scalar(PAIRF, k_("pairs"), PLACES[:, 2:3], None, ALU.is_lt))
            v.tensor_scalar(NPAIRS[:, 1:2], PLACES[:, 3:4], 0.5, None, ALU.mult)
            then(L, v.tensor_reduce(NPAIRS[:, 0:1], PAIRF, X_AXIS, ALU.add))
            v.tensor_copy(items[:, LISTED:LISTED + 2], NPAIRS)
            dve.wait_ge(items_done, 1)
            v.tensor_copy(SLOT_OF, PB[:, 0, LISTS:LISTS + T * LISTED].rearrange("p (t n) -> p t n", t=T))
            v.tensor_copy(GATE_OF, PB[:, 0, LISTS + T * LISTED:LISTS + 2 * T * LISTED].rearrange("p (t n) -> p t n", t=T))
            v.tensor_copy(items[0:1, 0:LISTED], PB[0:1, 0, 4:4 + LISTED]).then_inc(items_ready, 1)

            def take_rows(G):
                dve.wait_ge(*pair_("gathered", G, 2))
                for c in range(KD // 2):
                    b = c + KD // 2
                    last = v.tensor_scalar(XT[:, b, :], PA[:, 1, c * P:(c + 1) * P], cols[:, 2, b:b + 1],
                                           cols[:, 3, b:b + 1], ALU.mult, ALU.add)
                last.then_inc(S_["xt_dve"], 1)

            mixed, same = pair_counts(dve)
            take_rows(0)
            with dve.Fori(0, mixed + same) as G:
                for x in range(2):
                    dve.wait_ge(*pair_("gu_ready", G, x + 1))
                    v.tensor_scalar(XG, PA[:, 0, :], LIMIT, None, ALU.min).then_inc(S_["clipped"], 1)
                    v.tensor_scalar(XL, PA[:, 1, :], -LIMIT, LIMIT, ALU.max, ALU.min).then_inc(S_["gu_drained"], 1)
                    dve.wait_ge(*pair_("gu_drained", G, x + 1))
                    v.scalar_tensor_tensor(XL, XL, 1.0, XG, ALU.add, ALU.mult).then_inc(S_["gated"], 1)
                    dve.wait_ge(*pair_("sig_ready", G, x + 1))
                    dve.wait_ge(*pair_("gated", G, x + 1))
                    if x:
                        dve.wait_ge(*pair_("act_t", G, 1))
                    v.tensor_tensor(ACTV, XL, SIG, ALU.mult).then_inc(S_["actv_ready"], 1)
                    dve.wait_ge(*pair_("actv_ready", G, x + 1))
                    if x == 0:
                        dve.wait_ge(*pair_("wt_t", G, 1))
                        select(G + 1, lambda t: SLOT_OF[:, t, bass.ds(2 * G + 2, 2)], lambda t: GATE_OF[:, t, bass.ds(2 * G + 2, 2)])
                take_rows(G + 1)
                dve.wait_ge(*pair_("dn_chunk", G, 2 + DN_CREDIT))
                v.tensor_copy(YP[:, BANK:D], PB[:, 1, :]).then_inc(S_["yp_dve"], 1)
            residual(L, 1, POST_FFN, None)

        @block.tensor
        def _(pe):
            mm = nc.tensor.matmul

            def weights(l, i):
                pe.wait_ge(*chunk_loaded(l, i))
                return ring[:, i % DENSE_SLOTS, :]

            def transposes(l, n):
                for t in range(T):
                    pe.wait_ge(*upto("pre_ready", l, T * (n // 2) + t + 1))
                    for c in range(KD):
                        last = transpose(t, c)
                        if t == T - 1 and c == KD // 2 - 1:
                            last.then_inc(S_["transposed_a"], 1)
                last.then_inc(S_["transposed_b"], 1)

            def transpose(t, c):
                pair, b = (PA, c) if c < KD // 2 else (PB, c - KD // 2)
                return nc.tensor.transpose(pair[:, b // 2, (b % 2) * S + t * P:(b % 2) * S + (t + 1) * P],
                                           XN[:, t, c * P:(c + 1) * P], ident)

            def transpose_mixed(l, half):
                pe.wait_ge(*upto("mixed_ready", l, half + 1))
                for t in range(T):
                    for c in range(half * KD // 2, (half + 1) * KD // 2):
                        last = transpose(t, c)
                last.then_inc(S_[("transposed_a", "transposed_b")[half]], 1)

            def transpose_rows(l, t):
                pe.wait_ge(*upto("pre_ready", l, T + t + 1))
                for c in range(KD):
                    last = nc.tensor.transpose((PA, PB)[t][:, c // 4, (c % 4) * P:(c % 4 + 1) * P],
                                               XN[:, t, c * P:(c + 1) * P], ident)
                last.then_inc(S_[("transposed_a", "transposed_b")[t]], 1)

            def ht_ready(l, n, c):
                if c % 4 == 0:
                    pe.wait_ge(*upto("ht_act", l, 2 * n + c // 4 + 1))
                    pe.wait_ge(*upto("ht_dve", l, 2 * n + c // 4 + 1))

            def project_t(l, i, pair, done):
                w = weights(l, i)
                w = w.rearrange("p (c n) -> p c n", n=BANK)
                for b in range(4):
                    for c in range(KD):
                        if i == 0 and b == 0:
                            ht_ready(l, 0, c)
                        last = mm(pair[:, b // 2, (b % 2) * S:(b % 2 + 1) * S], w[:, c, b * P:(b + 1) * P],
                                  HT[:, c, :], start=c == 0, stop=c == KD - 1)
                last.then_inc(S_[done], 1)

            def project_split(l, k, pair, done):
                pe.wait_ge(*upto("w_fine", l, k + 1))
                if k == 0:
                    pe.wait_ge(*upto("ht_fine", l, 1))
                wf, wc = (w.rearrange("p (c n) -> p c n", n=BANK) for w in split(l, k)[2:])
                for t in range(T):
                    rows = slice(t * P, (t + 1) * P)
                    for c in range(KD):
                        mm(pair[:, t, :], INC[:, c, rows], wc[:, c, :], start=c == 0, stop=False)
                        mm(pair[:, t, :], INC[:, c, rows], wf[:, c, :], start=False, stop=False)
                        last = mm(pair[:, t, :], INF[:, c, rows], wc[:, c, :], start=False, stop=c == KD - 1)
                last.then_inc(S_[done], 1)

            def project_out(l):
                w = weights(l, IN_CHUNKS).rearrange("p (c n) -> p c n", n=BANK)
                transpose_mixed(l, 0)
                for half in range(2):
                    for t in range(T):
                        for c in range(half * KD // 2, (half + 1) * KD // 2):
                            if t == 0:
                                ht_ready(l, 1, c)
                            last = mm((PC, PD)[t][:, 0, :], HT[:, c, t * P:(t + 1) * P], w[:, c, :], start=c == 0,
                                      stop=c == KD - 1)
                        if half == 0 and t == 0:
                            transpose_mixed(l, 1)
                last.then_inc(S_["mix_done"], 1)
                if l is L:
                    w = weights(l, IN_CHUNKS + 1).rearrange("p (c n) -> p c n", n=BANK)
                else:
                    pe.wait_ge(*upto("ht_fine", l, 2))
                    pe.wait_ge(*upto("w_fine", l, OUT + 1))
                    wf, wc = (w.rearrange("p (c n) -> p c n", n=BANK) for w in split(l, OUT)[2:])
                for t in range(T):
                    acc, rows = (PC, PD)[t][:, 1, :], slice(t * P, (t + 1) * P)
                    for c in range(KD):
                        if l is L:
                            last = mm(acc, HT[:, c, rows], w[:, c, :], start=c == 0, stop=c == KD - 1)
                        else:
                            mm(acc, OUTC[:, c, rows], wc[:, c, :], start=c == 0, stop=False)
                            mm(acc, OUTC[:, c, rows], wf[:, c, :], start=False, stop=False)
                            last = mm(acc, OUTF[:, c, rows], wc[:, c, :], start=False, stop=c == KD - 1)
                    last.then_inc(S_["mix_done"], 1)

            def transpose_hidden(l, i):
                pe.wait_ge(*upto("act_done", l, i + 1))
                if i >= 2:
                    pe.wait_ge(*upto("hidden_fine", l, i - 1))
                for b in range(2):
                    for t in range(T):
                        last = nc.tensor.transpose(PB[:, i % 2, b * S + t * P:b * S + (t + 1) * P],
                                                   HID[:, i % 2, t, b * P:(b + 1) * P], ident)
                last.then_inc(S_["hidden_t"], 1)

            def rotate(l, raw, pair, done):
                for b in range(2):
                    last = mm(pair[:, b, :], k_("rotate"), raw[:, 2 * b:2 * b + 2, :].rearrange("p b s -> p (b s)"),
                              start=True, stop=True)
                last.then_inc(S_[done], 1)

            def score(l, h, q=None, k=None):
                if h >= 2:
                    pe.wait_ge(*upto("logits", l, h - 1))
                q, k = (QT[:, h // 2, :], KT[:, h, :]) if q is None else (q, k)
                for t in range(T):
                    part = slice(0, P) if t == 0 else slice(P, 3 * P)
                    last = mm(PD[:, h % 2, part], q[:, t * P:(t + 1) * P], k[:, 0:(t + 1) * P],
                              start=True, stop=True)
                last.then_inc(S_["scores"], 1)

            def transpose_probs(l, h):
                pe.wait_ge(*upto("probs", l, h + 1))
                if h >= 2:
                    pe.wait_ge(*upto("probs_ready", l, h - 1))
                for b in range(3):
                    last = nc.tensor.transpose(PA[:, h % 2, b * P:(b + 1) * P], prob[:, h % 2, b * P:(b + 1) * P], ident)
                last.then_inc(S_["probs_t"], 1)

            def attend(l, h, val=None, pair=PC):
                pe.wait_ge(*upto("probs_ready", l, h + 1))
                pt = prob[:, 2 + h % 2, :]
                to = slice(h % AH * HD, (h % AH + 1) * HD)
                val = [V[0][:, to], V[1][:, to]] if val is None else val
                mm(pair[:, 0, to], pt[:, 0:P], val[0], start=True, stop=True)
                mm(pair[:, 1, to], pt[:, P:2 * P], val[0], start=True, stop=False)
                mm(pair[:, 1, to], pt[:, 2 * P:3 * P], val[1], start=False, stop=True).then_inc(S_["attended"], 1)

            def level(l, n):
                if n >= 0:
                    pe.wait_ge(*upto("gla_qe", l, n + 1))
                    pe.wait_ge(*upto("gla_ke", l, n + 1))
                    pe.wait_ge(*upto("gla_merged", l, n + 1))
                q, k = (GQ, GKT) if n < 0 else (QE[:, n % 2], KE[:, n % 2])
                for h in range(GH):
                    if n == LEVELS - 1:
                        last = mm(PB[:, 0, h * P:(h + 1) * P], k[:, h, 0:P], q[:, h // 2, P:S], start=True, stop=True)
                        continue
                    for t in range(T):
                        cols = slice(t * P, (t + 1) * P)
                        last = mm(PB[:, t, h * P:(h + 1) * P], k[:, h, cols], q[:, h // 2, cols], start=True, stop=True)
                last.then_inc(S_["gla_scores"], 1)

            pe.sem_inc(S_["dn_done"], PER["dn_done"])
            pe.sem_inc(S_["dn_chunk"], DN_CREDIT)
            pe.sem_inc(S_["combined"], T)
            pe.sem_inc(S_["ada_cols"], 1)
            pe.wait_ge(ident_loaded, 16)
            pe.wait_ge(gains_loaded, 64)
            nc.tensor.transpose(PD[:, 0, 0:L * 3 * KD], GROWS, ident[0:L * 3 * KD, 0:L * 3 * KD]).then_inc(gains_t, 1)
            pe.wait_ge(filled, 2)
            with pe.Fori(0, L) as l:
                transposes(l, 0)
                pe.wait_ge(*upto("ada_cols", l, 1))
                project_t(l, 0, PC, "q_proj")
                project_split(l, 0, PD, "v_proj")
                pe.wait_ge(const_loaded, 16)
                pe.wait_ge(*upto("q_raw", l, 1))
                rotate(l, QRAW, PB, "q_rot")
                project_t(l, 2, PA, "k_proj")
                project_split(l, 1, PC, "gv_proj")
                pe.wait_ge(*upto("gate_weights", l, 48))
                pe.wait_ge(*upto("k_raw", l, 1))
                for c in range(KD):
                    last = mm(PA[0:GR, 0, 0:S], WLOW[:, c, :], HT[:, c, :], start=c == 0, stop=c == KD - 1)
                last.then_inc(S_["low_proj"], 1)
                pe.wait_ge(*upto("v_ready", l, 1))
                rotate(l, KRAW, PD, "k_rot")
                pe.wait_ge(*upto("low_ready", l, 1))
                for a in range(2):
                    last = mm(PA[:, 1, a * S:(a + 1) * S], WGU[:, a * P:(a + 1) * P], LOW[:, :], start=True, stop=True)
                last.then_inc(S_["z_proj"], 1)
                pe.wait_ge(*upto("q_ready", l, 1))
                project_t(l, 4, PB, "gqk_proj")
                pe.wait_ge(*upto("gv_ready", l, 1))
                project_split(l, 2, PC, "gr_proj")
                pe.wait_ge(*upto("k_ready", l, 1))
                score(l, 0)
                pe.wait_ge(*upto("gqk_ready", l, 1))
                level(l, -1)
                pe.wait_ge(*upto("decay_sum", l, 1))
                pe.wait_ge(*upto("gr_ready", l, 1))
                for h in range(AH):
                    if h + 1 < AH:
                        score(l, h + 1)
                    level(l, h)
                    transpose_probs(l, h)
                    if h:
                        attend(l, h - 1)
                attend(l, AH - 1)
                pe.wait_ge(*upto("gla_merged", l, LEVELS + 1))
                for h in range(GH):
                    cols = slice(h * P, (h + 1) * P)
                    mm(PD[:, 0, cols], MERGED[:, 0, h, :], GV[:, 0, cols], start=True, stop=True)
                    mm(PD[:, 1, cols], ACROSS[:, h, :], GV[:, 0, cols], start=True, stop=False)
                    last = mm(PD[:, 1, cols], MERGED[:, 1, h, :], GV[:, 1, cols], start=False, stop=True)
                last.then_inc(S_["gla_done"], 1)
                project_out(l)
                transpose_rows(l, 0)
                for i in range(GU_CHUNKS):
                    pe.wait_ge(*upto("w_fine", l, GU + i + 1))
                    wf, wc = (w.rearrange("p (u c n) -> p c u n", u=2, c=KD) for w in split(l, GU + i)[2:])
                    if i >= 2:
                        pe.wait_ge(*upto("act_done", l, i - 1))
                    for t in range(T):
                        acc = gate_up_bank(i)[:, t, :].rearrange("p (u n) -> p u n", u=2)
                        rows = slice(t * P, (t + 1) * P)
                        if i == 0:
                            pe.wait_ge(*upto("ht_act", l, 4 + t + 1))
                            pe.wait_ge(*upto("ht_dve", l, 4 + t + 1))
                        for c in range(KD):
                            mm(acc, HTC[:, c, rows], wc[:, c], start=c == 0, stop=False)
                            mm(acc, HTC[:, c, rows], wf[:, c], start=False, stop=False)
                        if i == 0:
                            if t + 1 < T:
                                transpose_rows(l, t + 1)
                            pe.wait_ge(*upto("ht_fine", l, 2 + t + 1))
                        for c in range(KD):
                            last = mm(acc, HTF[:, t, c, :], wc[:, c], start=False, stop=c == KD - 1)
                    last.then_inc(S_["gu_done"], 1)
                    if i:
                        transpose_hidden(l, i - 1)
                tail, one, both = DN_BLOCKS * DN_TAIL, ((0,), (1,)), range(T)
                for tiles, blocks in (*((t, range(DN_BLOCKS)) for t in one), (both, range(DN_BLOCKS, tail)),
                                      *((t, range(tail, FB)) for t in one)):
                    if tiles == (1,) and blocks[0] == 0:
                        transpose_hidden(l, GU_CHUNKS - 1)
                    for f in blocks:
                        if f % 2 == 0 and tiles != (1,):
                            pe.wait_ge(*upto("hidden_fine", l, f // 2 + 1))
                        if f == FB - 2 and tiles == (0,):
                            pe.wait_ge(*upto("ada_used", l, ADA_STEPS))
                            for n in range(2):
                                last = mm(PA[:, n, :], ones[:, :], ASUM[:, 2 * D + n * BANK:2 * D + (n + 1) * BANK],
                                          start=True, stop=True)
                            last.then_inc(S_["ada_mod"], 1)
                        if f % DN_BLOCKS == 0 and tiles != (1,):
                            pe.wait_ge(*upto("w_fine", l, DN + f // DN_BLOCKS + 1))
                        wf, wc = (w.rearrange("p (f n) -> p f n", n=D)[:, f % DN_BLOCKS]
                                  for w in split(l, DN + f // DN_BLOCKS)[2:])
                        for t in tiles:
                            rows = slice(t * P, (t + 1) * P)
                            for n in range(2):
                                acc, at = (PC, PD)[t][:, n, :], slice(n * BANK, (n + 1) * BANK)
                                mm(acc, ACTC[:, f, rows], wc[:, at], start=f == 0, stop=False)
                                mm(acc, ACTC[:, f, rows], wf[:, at], start=False, stop=False)
                                last = mm(acc, ACTF[:, f, rows], wc[:, at], start=False, stop=f == FB - 1)
                        if f == FB - 1 or f % DN_BLOCKS == DN_BLOCKS - 1 and tiles != (0,):
                            last.then_inc(S_["dn_done"], 1)
                pe.wait_ge(*upto("x_ready", l, T + 1))
                for n in range(2 * KD):
                    last = mm(PC[:, 0, n:n + 1], ASUM[:, n * P:(n + 1) * P], ones[:, 0:1], start=True, stop=True)
                last.then_inc(S_["ada_mod"], 1)
                pe.wait_ge(*upto("ada_rows", l, 1))

            transposes(L, 0)
            pe.wait_ge(*upto("ada_cols", L, 1))
            def flip(n):
                if n == 0:
                    pe.wait_ge(dist_copied, 1)
                    pe.wait_ge(flipped_loaded, 32)
                else:
                    pe.wait_ge(bias_b_ready, n)
                for b in range(2):
                    at = (2 * n + b) * BANK
                    last = mm(PD[:, b, :], k_("flip"), FLIPPED.rearrange("p h n -> p (h n)")[:, at:at + BANK], start=True,
                              stop=True)
                last.then_inc(flipped_done, 1)

            project_t(L, 0, PC, "q_proj")
            pe.wait_ge(narrow_loaded, 48)
            for t in range(T):
                for c in range(KD):
                    last = mm(PB[:, 0, t * AH:(t + 1) * AH], HT[:, c, t * P:(t + 1) * P], WF[:, c, :], start=c == 0,
                              stop=c == KD - 1)
            last.then_inc(forget_logits, 1)
            pe.wait_ge(rel_ready, 16 + 1)
            mm(PD[0:AH, 0, :], REL[:, :], k_("bucket", BUCKETS + 1), start=True, stop=True).then_inc(dist_done, 1)
            project_t(L, 1, PA, "k_proj")
            flip(0)
            pe.wait_ge(log_forget, 1)
            upto_, lf = k_("upto"), LF[:, 0]
            mm(PB[:, 0, 0:AH], upto_, lf[:, 0, :], start=True, stop=True)
            mm(PB[:, 0, AH:2 * AH], ones[:, :], lf[:, 0, :], start=True, stop=False)
            mm(PB[:, 0, AH:2 * AH], upto_, lf[:, 1, :], start=False, stop=True).then_inc(forget_sums, 1)
            pe.wait_ge(*upto("q_ready", L, 1))
            project_split(L, 0, PC, "v_proj")
            flip(1)
            pe.wait_ge(*upto("k_ready", L, 1))
            project_t(L, 3, PA, "q_proj")
            flip(2)
            pe.wait_ge(*upto("v_ready", L, 1))
            project_split(L, 1, PC, "v_proj")
            pe.wait_ge(bias_b_ready, 3)
            pe.wait_ge(forget_cum, 1)
            for h in range(AH):
                row = (PD, PB)[h // 4][:, h % 4 // 2, (h % 2) * S:(h % 2 + 1) * S]
                w = [lf[:, t, h:h + 1].broadcast_to((P, P)) for t in range(T)]
                mm(row[:, 0:P], w[0], upto_, start=True, stop=True)
                mm(row[:, P:S], w[0], ones[:, :], start=True, stop=False)
                last = mm(row[:, P:S], w[1], upto_, start=False, stop=True)
                if h % 4 == 3:
                    last.then_inc(forget_rows, 1)
            pe.wait_ge(*upto("q_ready", L, 2))
            project_t(L, 5, PA, "k_proj")
            pe.wait_ge(bias_f, 2)
            for h in range(2 * AH):
                if h == 0:
                    score(L, 0, *attention(0)[0:2])
                    pe.wait_ge(*upto("v_ready", L, 2))
                    pe.wait_ge(*upto("k_ready", L, 2))
                if h + 1 < 2 * AH:
                    score(L, h + 1, *attention(h + 1)[0:2])
                transpose_probs(L, h)
                if h:
                    attend(L, h - 1, attention(h - 1)[2], attention(h - 1)[4])
            attend(L, 2 * AH - 1, attention(2 * AH - 1)[2], PB)
            project_out(L)
            for t in range(T):
                transpose_rows(L, t)
                pe.wait_ge(*upto("ht_act", L, 4 + t + 1))
                pe.wait_ge(*upto("ht_dve", L, 4 + t + 1))
                for c in range(KD):
                    last = mm(PA[:, 0, t * NE:(t + 1) * NE], HT[:, c, t * P:(t + 1) * P], WR[:, c, :], start=c == 0,
                              stop=c == KD - 1)
            last.then_inc(router_done, 1)
            pe.wait_ge(mask_ready, 1)
            mm(PA[:, 0, 0:NE], k_("before"), MASK(0)[:, 0:NE], start=True, stop=True)
            mm(PA[:, 0, NE:2 * NE], ones[:, :], MASK(0)[:, 0:NE], start=True, stop=False)
            mm(PA[:, 0, NE:2 * NE], k_("before"), MASK(1)[:, 0:NE], start=False, stop=True)
            for t in range(T):
                last = mm(PA[:, 0, 2 * NE:2 * NE + 1], MASK(t), ones[:, 0:1], start=t == 0, stop=t == T - 1)
            last.then_inc(ranks_done, 1)
            pe.wait_ge(flags_ready, 1)
            mm(PB[:, 0, 0:1], k_("before"), FLAGS[:, 0:1], start=True, stop=True)
            mm(PB[:, 0, 1:2], k_("before_pair"), FLAGS[:, 1:2], start=True, stop=True)
            mm(PB[:, 0, 2:4], ones[:, :], FLAGS, start=True, stop=True).then_inc(places_done, 1)
            pe.wait_ge(routed, 1)
            for t in range(T):
                nc.tensor.transpose(PB[:, 1, t * P:(t + 1) * P], RK[:, t, :], ident)
                last = nc.tensor.transpose(PB[:, 1, S + t * P:S + (t + 1) * P], GATE[:, t, :], ident)
            last.then_inc(parted_t, 1)
            def gather(G, halves):
                pe.wait_ge(*pair_("sel_ready", G, 1))
                for q in halves:
                    for c in range(KD // 2):
                        d = KD // 2 * q + c
                        for t in range(T):
                            last = mm(PA[:, q, c * P:(c + 1) * P], XN[:, t, d * P:(d + 1) * P],
                                      SELG[:, t].rearrange("p e n -> p (e n)"), start=t == 0, stop=t == T - 1)
                    last.then_inc(S_["gathered"], 1)

            gather(0, (0,))
            pe.wait_ge(parted, 1)
            pe.wait_ge(perm_ready, 1)
            for u in range(2):
                for t in range(T):
                    mm(PB[:, 0, LISTS + (T * u + t) * LISTED:LISTS + (T * u + t + 1) * LISTED], PARTED[:, u, t * P:(t + 1) * P], PERM,
                       start=True, stop=True)
            mm(PB[0:1, 0, 4:4 + LISTED], k_("expert"), PERM, start=True, stop=True).then_inc(items_done, 1)
            def gate_up(x, slots, loaded, bias, biased, release):
                for c in range(KD):
                    s = slots[c // 2]
                    if c % 2 == 0:
                        pe.wait_ge(efull[s], loaded[c // 2])
                    for u in range(2):
                        for h in range(2):
                            at = (c % 2) * 2 * D + (2 * u + h) * BANK
                            last = mm(PA[h * SLOTS:(h + 1) * SLOTS, u, :], XT[:, c, x * SLOTS:(x + 1) * SLOTS],
                                      ring[:, s, at:at + BANK], start=c == 0, stop=False)
                    if c % 2 and release:
                        last.then_inc(S_["gu_chunk"], 1)
                pe.wait_ge(*biased)
                for u in range(2):
                    for h in range(2):
                        at = (2 * u + h) * BANK
                        last = mm(PA[h * SLOTS:(h + 1) * SLOTS, u, :], ones[:, 0:SLOTS], bias[:, at:at + BANK],
                                  start=False, stop=True)
                last.then_inc(S_["gu_ready"], 1)

            def down(slots, loaded):
                for q in range(2):
                    for x in range(2):
                        pe.wait_ge(efull[slots[q][x]], loaded)
                    for j in range(4):
                        for n in range(2):
                            for x in range(2):
                                last = mm(PB[x * SLOTS:(x + 1) * SLOTS, n, :], ATT[x][:, j, q, :],
                                          ring[:, slots[q][x], j * D + n * BANK:j * D + (n + 1) * BANK],
                                          start=q + j == 0, stop=q + j == 4)
                    last.then_inc(S_["dn_chunk"], 1)

            def items_pair(G, gate_ups, downs):
                pe.wait_ge(*pair_("xt_act", G, 1))
                pe.wait_ge(*pair_("xt_dve", G, 1))
                for t in range(T):
                    last = nc.tensor.transpose(PA[:, 0, t * P:(t + 1) * P], WG[:, t].rearrange("p e n -> p (e n)"), ident)
                last.then_inc(S_["wt_t"], 1)
                pe.wait_ge(*pair_("wt_ready", G, 1))
                gate_up(0, *gate_ups[0])
                pe.wait_ge(*pair_("gu_drained", G, 1))
                gate_up(1, *gate_ups[1])
                for x in range(2):
                    pe.wait_ge(*pair_("actv_ready", G, x + 1))
                    for j in range(4):
                        last = nc.tensor.transpose(PB[:, x, j * P:(j + 1) * P], ACTV[:, j * P:(j + 1) * P], ident)
                    last.then_inc(S_["act_t"], 1)
                pe.wait_ge(*pair_("gu_drained", G, 2))
                gather(G + 1, range(2))
                pe.wait_ge(*pair_("att_ready", G, 2))
                down(*downs)
                pe.wait_ge(*pair_("yp_act", G, 1))
                pe.wait_ge(*pair_("yp_dve", G, 1))
                for t in range(T):
                    for n in range(2):
                        last = mm((PC, PD)[t][:, n, :], WT[:, t * P:(t + 1) * P], YP[:, n * BANK:(n + 1) * BANK], start=False,
                                  stop=True, skip_group_check=True)
                    last.then_inc(S_["combined"], 1)

            gather(0, (1,))
            pe.wait_ge(bd_loaded, 16)
            pe.wait_ge(*upto("x_ready", L, T))
            for t in range(T):
                for n in range(2):
                    mm((PC, PD)[t][:, n, :], PARTED[0:NE, 1, t * P:(t + 1) * P], BD[:, n * BANK:(n + 1) * BANK], start=True,
                       stop=True, skip_group_check=True)
            def mixed_pair(m, others):
                ups = [(EXPERT_SLOT[n % RING], m * 64 + others * 32 + 32 * (n // RING + 1)) for n in range(8)]
                biased = [(bfull[0], m * 16 + others * 16 + 16), (bfull[1], m * 16 + 16)]
                items_pair(m + others, [([s for s, _ in ups[4 * x:4 * x + 4]], [w for _, w in ups[4 * x:4 * x + 4]], BZ[x],
                                         biased[x], True) for x in range(2)],
                           ([[EXPERT_SLOT[2 + 2 * q + x] for x in range(2)] for q in range(2)], m * 64 + others * 32 + 64))

            mixed, same = pair_counts(pe)
            with pe.Fori(0, LEAD) as m:
                mixed_pair(m, 0)
            with pe.Fori(0, same) as h:
                loaded = LEAD * 64 + h * 32 + 32
                items_pair(h + LEAD, [(EXPERT_SLOT[0:4], [loaded] * 4, BZ[0], (bfull[0], LEAD * 16 + h * 16 + 16), x == 1)
                                   for x in range(2)],
                           ([[EXPERT_SLOT[4 + q]] * 2 for q in range(2)], loaded))
            with pe.Fori(LEAD, mixed) as m:
                mixed_pair(m, same)


_INS = ["x", "mix_pre_norm", "mix_post_norm", "ffn_pre_norm", "ffn_post_norm", "w_in", "gla_w_gate_up",
        "gla_b_gate", "gla_out_norm", "attn_out_norm", "w_out", "w_gate", "w_up", "w_down", "c_2", "w_ada_2",
        "b_ada_2", "g_pre_mix_2", "g_post_mix_2", "w_in_2", "b_forget_2", "rel_bias_2", "w_out_2", "g_pre_ffn_2",
        "g_post_ffn_2", "w_router_2", "b_router_2", "w_gate_up_2", "b_gate_up_2", "w_down_2", "b_down_2"]


def kernel(**inputs):
    import concourse.bacc as bacc
    from concourse.bass_utils import run_bass_kernel_spmd

    nc = bacc.Bacc("TRN2", target_bir_lowering=False, num_devices=1)
    arrays, A = {}, {}
    for name in _INS:
        a = np.ascontiguousarray(inputs[name])
        arrays[name] = a
        A[name] = nc.dram_tensor(name, a.shape, mybir.dt.from_np(a.dtype), kind="ExternalInput").ap()
    arrays["constants"] = constants()
    const = nc.dram_tensor("constants", arrays["constants"].shape, F32, kind="ExternalInput").ap()
    out = nc.dram_tensor("out", (1, S, D), F32, kind="ExternalOutput").ap()
    program(nc, A, const, out)
    return run_bass_kernel_spmd(nc, [arrays], core_ids=[0]).results[0]["out"]
```
